# Optimizing a Trainium2 kernel written in Bass

```python
import math
import jax
import jax.numpy as jnp
from jax import lax
import numpy as np

D_MODEL = 1024
BATCH = 1
SEQ = 128
DEPTH = 2
DEC_BATCH = 1
DEC_SEQ = 256
PAST_LEN = 128

GRID_W = 64
HEAD_DIM = 64
A_HEADS = 6
A_WIDTH = A_HEADS * HEAD_DIM
LORA_W = 64
LORA_A = 64
LORA_G = 128
N_DIR = 2
DECAY_SCALE = 0.606531
B_Q_HEADS = 6
B_KV_HEADS = 2
B_WIDTH = B_Q_HEADS * HEAD_DIM
KV_WIDTH = B_KV_HEADS * HEAD_DIM
ROPE_THETA = 10000.0
Q_BLOCK = 128
POOL_WINDOWS = (2, 4, 8, 16)
C_GROUPS = 4
C_GROUP_W = 64
C_WIDTH = C_GROUPS * C_GROUP_W
MIX_WIDTH = A_WIDTH + B_WIDTH + C_WIDTH
IN_SPLITS = (A_WIDTH, A_WIDTH, A_WIDTH, N_DIR * LORA_W, N_DIR * LORA_A, LORA_G,
             B_WIDTH, KV_WIDTH, KV_WIDTH, C_WIDTH)
IN_COLS = sum(IN_SPLITS)
N_GROUPS = 4
EXP_PER_GROUP = 4
N_EXPERTS = N_GROUPS * EXP_PER_GROUP
TOP_K_INNER = 2
D_EXPERT = 256
ALPHA = (2 * DEPTH) ** 0.25
BETA = (8 * DEPTH) ** -0.25
LN_EPS = 1e-5
GN_EPS = 64e-5
QK_EPS = 1e-6

kernel_name = "hybrid_rwkv7_gqa_pool_hmoe_diffusion_step"

F32 = jnp.float32

def layer_norm(x, g, b):
    xf = x.astype(F32)
    mu = jnp.mean(xf, -1, keepdims=True)
    var = jnp.mean(jnp.square(xf - mu), -1, keepdims=True)
    return ((xf - mu) * lax.rsqrt(var + LN_EPS) * g + b).astype(x.dtype)

def rms_norm_heads(x, g):
    xf = x.astype(F32)
    return (xf * lax.rsqrt(jnp.mean(xf * xf, -1, keepdims=True) + QK_EPS) * g).astype(x.dtype)

def rope_tables(length):
    rows = length // GRID_W
    t = jnp.arange(rows * GRID_W)
    row = (t // GRID_W).astype(F32)
    col = (t % GRID_W).astype(F32)
    n = HEAD_DIM // 4
    inv = 1.0 / (ROPE_THETA ** (jnp.arange(n, dtype=F32) / n))
    ang = jnp.concatenate([row[:, None] * inv, col[:, None] * inv], -1)
    return jnp.cos(ang), jnp.sin(ang)

def apply_rope(x, cos, sin):
    bsz, length, nh, _ = x.shape
    n = HEAD_DIM // 4
    xs = x.astype(F32).reshape(bsz, length, nh, 2, 2, n)
    x1, x2 = xs[..., 0, :], xs[..., 1, :]
    c = cos.reshape(length, 2, n)[None, :, None]
    s = sin.reshape(length, 2, n)[None, :, None]
    out = jnp.stack([x1 * c - x2 * s, x2 * c + x1 * s], axis=-2)
    return out.reshape(x.shape).astype(x.dtype)

def block_attention(q, k, v):
    bsz, lq, hq, hd = q.shape
    hkv = k.shape[2]
    grp = hq // hkv
    nb = lq // Q_BLOCK
    qb = jnp.moveaxis(q.reshape(bsz, nb, Q_BLOCK, hkv, grp, hd), 1, 0)
    kf = k.astype(F32)
    vf = v.astype(F32)
    scale = 1.0 / math.sqrt(hd)

    def one_block(qblk):
        s = jnp.einsum('bqhgd,bkhd->bhgqk', qblk.astype(F32), kf) * scale
        p = jax.nn.softmax(s, axis=-1)
        return jnp.einsum('bhgqk,bkhd->bqhgd', p, vf).astype(q.dtype)

    o = lax.map(one_block, qb)
    return jnp.moveaxis(o, 0, 1).reshape(bsz, lq, hq * hd)

def _both_dirs(t):
    return jnp.stack([t, jnp.flip(t, axis=1)], axis=2)

def _per_dir(t):
    return jnp.stack([t[:, :, 0], jnp.flip(t[:, :, 1], axis=1)], axis=2)

def _time_major(t):
    return jnp.moveaxis(t, 1, 0)

def _rwkv7_step(S, inp):
    r_t, w_t, k_t, v_t, kk_t, a_t = inp
    sa = jnp.einsum('bshvk,bshk->bshv', S, -kk_t)
    S = S * w_t[..., None, :] + sa[..., None] * (kk_t * a_t)[..., None, :] + v_t[..., None] * k_t[..., None, :]
    y = jnp.einsum('bshvk,bshk->bshv', S, r_t)
    return S, y

def rwkv7_mixer(r, k, v, lo_w, lo_a, lo_g, s0, lp):
    bsz, seqlen, _ = r.shape
    hshape = (bsz, seqlen, A_HEADS, HEAD_DIM)
    dshape = (bsz, seqlen, N_DIR, A_HEADS, HEAD_DIM)
    lo_w = lo_w.reshape(bsz, seqlen, N_DIR, LORA_W)
    lo_a = lo_a.reshape(bsz, seqlen, N_DIR, LORA_A)
    w_pre = lp['rw_w0'] + jnp.einsum('blsr,src->blsc', jnp.tanh(lo_w), lp['rw_w2'])
    decay = jnp.exp(-DECAY_SCALE * jax.nn.sigmoid(w_pre.astype(F32)))
    a = jax.nn.sigmoid((lp['rw_a0'] + jnp.einsum('blsr,src->blsc', lo_a, lp['rw_a2'])).astype(F32))
    g = jnp.einsum('blr,rc->blc', jax.nn.sigmoid(lo_g), lp['rw_g2']).astype(F32)
    kf = k.astype(F32)
    kk = (kf * lp['rw_kk']).reshape(hshape)
    kk = kk * lax.rsqrt(jnp.maximum(jnp.sum(kk * kk, -1, keepdims=True), 1e-24))
    kd = kf[:, :, None, :] * (1.0 + (a - 1.0) * lp['rw_ka'])
    rh = r.astype(F32).reshape(hshape)
    vh = v.astype(F32).reshape(hshape)
    kd_h = kd.reshape(dshape)
    xs = (_time_major(_both_dirs(rh)),
          _time_major(_per_dir(decay.reshape(dshape))),
          _time_major(_per_dir(kd_h)),
          _time_major(_both_dirs(vh)),
          _time_major(_both_dirs(kk)),
          _time_major(_per_dir(a.reshape(dshape))))
    s_final, ys = lax.scan(_rwkv7_step, s0.astype(F32), xs)
    ys = jnp.moveaxis(ys, 0, 1)
    y = ys[:, :, 0] + jnp.flip(ys[:, :, 1], axis=1)
    mu = jnp.mean(y, -1, keepdims=True)
    var = jnp.mean(jnp.square(y - mu), -1, keepdims=True)
    yn = ((y - mu) * lax.rsqrt(var + GN_EPS) * lp['rw_gn_g'].reshape(A_HEADS, HEAD_DIM)
          + lp['rw_gn_b'].reshape(A_HEADS, HEAD_DIM))
    bonus = jnp.sum(rh * (kd_h[:, :, 0] + kd_h[:, :, 1]) * lp['rw_rk'], -1, keepdims=True) * vh
    out = (yn + bonus).reshape(bsz, seqlen, A_WIDTH) * g
    return out.astype(r.dtype), s_final

def pool_mixer(p, pool_w, pool_scale):
    bsz, seqlen, _ = p.shape
    pf = p.astype(F32)
    cs = jnp.concatenate([jnp.zeros((bsz, 1, C_WIDTH), F32), jnp.cumsum(pf, axis=1)], axis=1)
    t = jnp.arange(seqlen)
    outs = []
    for gi, win in enumerate(POOL_WINDOWS):
        lo = jnp.clip(t - win // 2, 0, seqlen)
        hi = jnp.clip(t + win // 2, 0, seqlen)
        csg = cs[..., gi * C_GROUP_W:(gi + 1) * C_GROUP_W]
        s = jnp.take(csg, hi, axis=1) - jnp.take(csg, lo, axis=1)
        mean = s / (hi - lo).astype(F32)[None, :, None]
        outs.append(mean - pf[..., gi * C_GROUP_W:(gi + 1) * C_GROUP_W])
    d = jnp.stack(outs, axis=2)
    y = jnp.einsum('blgc,gcd->blgd', d, pool_w.astype(F32)).reshape(bsz, seqlen, C_WIDTH)
    return (y * pool_scale).astype(p.dtype)

def mixing_sublayer(u, lp, rope, ctx_k, ctx_v, s0):
    bsz, seqlen, _ = u.shape
    proj = u @ lp['w_in']
    cuts = [int(i) for i in np.cumsum(IN_SPLITS)[:-1]]
    r, k, v, lo_w, lo_a, lo_g, q, kb, vb, p = jnp.split(proj, cuts, axis=-1)
    a_out, s_final = rwkv7_mixer(r, k, v, lo_w, lo_a, lo_g, s0, lp)
    qh = rms_norm_heads(q.reshape(bsz, seqlen, B_Q_HEADS, HEAD_DIM), lp['q_norm'])
    kh = rms_norm_heads(kb.reshape(bsz, seqlen, B_KV_HEADS, HEAD_DIM), lp['k_norm'])
    vh = vb.reshape(bsz, seqlen, B_KV_HEADS, HEAD_DIM)
    if rope is None:
        q_use, k_all, v_all = qh, kh, vh
    else:
        cos, sin = rope
        q_use = apply_rope(qh, cos, sin)
        k_all = jnp.concatenate([apply_rope(kh, cos, sin), ctx_k.astype(kh.dtype)], axis=1)
        v_all = jnp.concatenate([vh, ctx_v.astype(vh.dtype)], axis=1)
    b_out = block_attention(q_use, k_all, v_all)
    c_out = pool_mixer(p, lp['pool_w'], lp['pool_scale'])
    mixed = jnp.concatenate([a_out, b_out.astype(u.dtype), c_out], axis=-1) @ lp['w_out']
    return mixed, kh, vh, s_final

def hier_moe(u, lp):
    bsz, seqlen, dm = u.shape
    x = u.reshape(-1, dm)
    lg = (x @ lp['rt_grp_w'] + lp['rt_grp_b']).astype(F32)
    pg = jax.nn.softmax(lg, axis=-1)
    sel = jnp.argmax(lg, axis=-1)
    gsel = jnp.take_along_axis(pg, sel[:, None], axis=1)
    le = (x @ lp['rt_exp_w'] + lp['rt_exp_b']).astype(F32).reshape(-1, N_GROUPS, EXP_PER_GROUP)
    le_sel = jnp.take_along_axis(le, sel[:, None, None], axis=1)[:, 0]
    tv, ti = lax.top_k(le_sel, TOP_K_INNER)
    tw = jax.nn.softmax(tv, axis=-1) * gsel
    inner = jnp.einsum('nk,nke->ne', tw, jax.nn.one_hot(ti, EXP_PER_GROUP, dtype=F32))
    gate = (jax.nn.one_hot(sel, N_GROUPS, dtype=F32)[:, :, None] * inner[:, None, :]).reshape(-1, N_EXPERTS)
    hid = jax.nn.silu(jnp.einsum('nd,edf->nef', x, lp['moe_w1'])) * jnp.einsum('nd,edf->nef', x, lp['moe_w3'])
    y = jnp.einsum('nef,efd->nd', hid * gate[:, :, None].astype(hid.dtype), lp['moe_w2'])
    return y.reshape(bsz, seqlen, dm)

def trunk_layer(h, cond, lp, rope, ctx_k, ctx_v, s0):
    mod = (jax.nn.silu(cond) @ lp['w_mod'] + lp['b_mod'])[:, None, :]
    sh1, sc1, g1, sh2, sc2, g2 = jnp.split(mod, 6, axis=-1)
    u = h * (1.0 + sc1) + sh1
    m, k, v, s_final = mixing_sublayer(u, lp, rope, ctx_k, ctx_v, s0)
    h = layer_norm(ALPHA * h + g1 * m, lp['ln1_g'], lp['ln1_b'])
    u = h * (1.0 + sc2) + sh2
    f = hier_moe(u, lp)
    h = layer_norm(ALPHA * h + g2 * f, lp['ln2_g'], lp['ln2_b'])
    return h, k, v, s_final

def setup_inputs(seed: int = 0) -> dict:
    key = jax.random.key(seed)
    ks = iter(jax.random.split(key, 48))

    def nrm(shape, scale):
        return jax.random.normal(next(ks), shape, F32) * scale

    d = D_MODEL
    return {
        'x_prompt': nrm((BATCH, SEQ, d), 1.0),
        'x_sample': nrm((DEC_BATCH, DEC_SEQ, d), 1.0),
        'state_rwkv': nrm((DEC_BATCH, DEPTH, N_DIR, A_HEADS, HEAD_DIM, HEAD_DIM), 0.5),
        'cache_k': nrm((DEC_BATCH, DEPTH, PAST_LEN, B_KV_HEADS, HEAD_DIM), 1.0),
        'cache_v': nrm((DEC_BATCH, DEPTH, PAST_LEN, B_KV_HEADS, HEAD_DIM), 1.0),
        'c': nrm((DEC_BATCH, d), 1.0),
        'c_ctx': nrm((d,), 1.0),
        'w_in': nrm((DEPTH, d, IN_COLS), d ** -0.5),
        'w_out': nrm((DEPTH, MIX_WIDTH, d), MIX_WIDTH ** -0.5 * BETA),
        'w_mod': nrm((DEPTH, d, 6 * d), 0.5 * d ** -0.5),
        'b_mod': nrm((DEPTH, 6 * d), 0.02),
        'ln1_g': 1.0 + nrm((DEPTH, d), 0.05),
        'ln1_b': nrm((DEPTH, d), 0.02),
        'ln2_g': 1.0 + nrm((DEPTH, d), 0.05),
        'ln2_b': nrm((DEPTH, d), 0.02),
        'rw_w0': nrm((DEPTH, N_DIR, A_WIDTH), 0.5),
        'rw_w2': nrm((DEPTH, N_DIR, LORA_W, A_WIDTH), 0.1 * LORA_W ** -0.5),
        'rw_a0': nrm((DEPTH, N_DIR, A_WIDTH), 0.5),
        'rw_a2': nrm((DEPTH, N_DIR, LORA_A, A_WIDTH), LORA_A ** -0.5),
        'rw_g2': nrm((DEPTH, LORA_G, A_WIDTH), LORA_G ** -0.5),
        'rw_kk': 0.85 + nrm((DEPTH, A_WIDTH), 0.05),
        'rw_ka': 1.0 + nrm((DEPTH, A_WIDTH), 0.05),
        'rw_rk': nrm((DEPTH, A_HEADS, HEAD_DIM), 0.1),
        'rw_gn_g': 1.0 + nrm((DEPTH, A_WIDTH), 0.05),
        'rw_gn_b': nrm((DEPTH, A_WIDTH), 0.02),
        'q_norm': 1.0 + nrm((DEPTH, HEAD_DIM), 0.05),
        'k_norm': 1.0 + nrm((DEPTH, HEAD_DIM), 0.05),
        'pool_w': nrm((DEPTH, C_GROUPS, C_GROUP_W, C_GROUP_W), C_GROUP_W ** -0.5),
        'pool_scale': 1.0 + nrm((DEPTH, C_WIDTH), 0.05),
        'rt_grp_w': nrm((DEPTH, d, N_GROUPS), d ** -0.5),
        'rt_grp_b': nrm((DEPTH, N_GROUPS), 0.01),
        'rt_exp_w': nrm((DEPTH, d, N_EXPERTS), d ** -0.5),
        'rt_exp_b': nrm((DEPTH, N_EXPERTS), 0.01),
        'moe_w1': nrm((DEPTH, N_EXPERTS, d, D_EXPERT), d ** -0.5),
        'moe_w3': nrm((DEPTH, N_EXPERTS, d, D_EXPERT), d ** -0.5),
        'moe_w2': nrm((DEPTH, N_EXPERTS, D_EXPERT, d), D_EXPERT ** -0.5 * BETA),
    }

def reference(x_prompt, x_sample, state_rwkv, cache_k, cache_v, c, c_ctx,
              w_in, w_out, w_mod, b_mod, ln1_g, ln1_b, ln2_g, ln2_b,
              rw_w0, rw_w2, rw_a0, rw_a2, rw_g2, rw_kk, rw_ka, rw_rk, rw_gn_g, rw_gn_b,
              q_norm, k_norm, pool_w, pool_scale,
              rt_grp_w, rt_grp_b, rt_exp_w, rt_exp_b, moe_w1, moe_w3, moe_w2):
    rope = rope_tables(x_sample.shape[1])
    s0_ctx = jnp.zeros((x_prompt.shape[0], N_DIR, A_HEADS, HEAD_DIM, HEAD_DIM), F32)
    cond_ctx = c_ctx[None, :]
    hp = x_prompt
    hs = x_sample
    new_s, new_k, new_v = [], [], []
    for l in range(DEPTH):
        lp = {
            'w_in': w_in[l], 'w_out': w_out[l], 'w_mod': w_mod[l], 'b_mod': b_mod[l],
            'ln1_g': ln1_g[l], 'ln1_b': ln1_b[l], 'ln2_g': ln2_g[l], 'ln2_b': ln2_b[l],
            'rw_w0': rw_w0[l], 'rw_w2': rw_w2[l], 'rw_a0': rw_a0[l], 'rw_a2': rw_a2[l],
            'rw_g2': rw_g2[l], 'rw_kk': rw_kk[l], 'rw_ka': rw_ka[l], 'rw_rk': rw_rk[l],
            'rw_gn_g': rw_gn_g[l], 'rw_gn_b': rw_gn_b[l],
            'q_norm': q_norm[l], 'k_norm': k_norm[l],
            'pool_w': pool_w[l], 'pool_scale': pool_scale[l],
            'rt_grp_w': rt_grp_w[l], 'rt_grp_b': rt_grp_b[l],
            'rt_exp_w': rt_exp_w[l], 'rt_exp_b': rt_exp_b[l],
            'moe_w1': moe_w1[l], 'moe_w3': moe_w3[l], 'moe_w2': moe_w2[l],
        }
        hp, k_l, v_l, s_l = trunk_layer(hp, cond_ctx, lp, None, None, None, s0_ctx)
        new_s.append(s_l)
        new_k.append(k_l)
        new_v.append(v_l)
        hs, _, _, _ = trunk_layer(hs, c, lp, rope, cache_k[:, l], cache_v[:, l], state_rwkv[:, l])
    return (hp, hs, jnp.stack(new_s, axis=1), jnp.stack(new_k, axis=1), jnp.stack(new_v, axis=1))


_drawn_inputs = setup_inputs


def setup_inputs(seed=0):
    import zlib

    import numpy as np

    out = dict(_drawn_inputs(seed))
    spreads = {}
    factors = {'state_rwkv': 8.0,
     'cache_k': 8.0,
     'cache_v': 8.0,
     'rw_w2': 4.66,
     'rw_kk': 31.868,
     'rw_gn_g': 8.0,
     'rw_gn_b': 28.599,
     'q_norm': 8.0,
     'pool_scale': 8.0,
     'rt_grp_b': 45.663,
     'rt_exp_b': 40.981}
    for name, (base, spread) in spreads.items():
        noise = np.random.default_rng([zlib.crc32(name.encode()), seed]).standard_normal(out[name].shape)
        drawn = base * np.exp(spread * noise) if base else spread * noise
        out[name] = jnp.asarray(drawn.astype(out[name].dtype))
    for name, factor in factors.items():
        out[name] = (out[name] * factor).astype(out[name].dtype)
    return out
```

```python
from contextlib import ExitStack

import numpy as np

import concourse.bass as bass
from concourse import mybir

ALU = mybir.AluOpType
ACT = mybir.ActivationFunctionType
AX = mybir.AxisListType
F32 = mybir.dt.float32
U8 = mybir.dt.uint8

P = 128
DEPTH = 2
D = 1024
KT = D // P
SEQ, DEC = 128, 256
T = SEQ + DEC
NT = T // P
GRID_W = 64
HD = 64
AH = 6
NJ = AH // 2
KVH = 2
GRP = 3
POOL_WINDOWS = (2, 4, 8, 16)
NG, EPG = 4, 4
NE = NG * EPG
DE = 256
ALPHA = (2 * DEPTH) ** 0.25
DECAY = 0.606531
LN_EPS, GN_EPS, QK_EPS = 1e-5, 64e-5, 1e-6
LEVELS = 7
STREAMS = ((0, SEQ), (SEQ, T))

BMOD, LN1G, LN1B, LN2G, LN2B = 0, 48, 56, 64, 72
W0, A0, KKP, KAP, RKP, GNG, GNB, PSC, QN, KN, COND, NPAR = 80, 86, 92, 95, 98, 101, 104, 107, 109, 110, 111, 127

RING = 3
SLOT = 4096
N_MOD, N_IN, N_OUT, N_EXP, N_DOWN = 12, 6, 3, NE, KT
I_MOD, I_IN = 0, N_MOD
I_OUT = I_IN + N_IN
I_EXP = I_OUT + N_OUT
I_DOWN = I_EXP + N_EXP
ITEMS = I_DOWN + N_DOWN
IN_COLS = ((1536, 512), (2048, 384), (768, 384), (1152, 384), (0, 384), (384, 384))
OUT_TILES = (3, 3, 2)


N_PAR_DMAS = 19
FRONT = 19 + 12 + 4 + NJ + NJ
SMALL = 14


def item_dmas(i):
    return 4 if I_OUT <= i < I_EXP else 7 if i == I_IN else 2


def landed_value(n):
    return sum(16 * item_dmas(m % ITEMS) for m in range(n % RING, n + 1, RING))


def constants():
    f = np.float32
    ident = np.eye(P, dtype=f)
    ones_d = np.full((P, P), 1.0 / D, f)
    head_ones = np.kron(np.eye(2), np.ones((HD, HD))).astype(f)
    rot = np.zeros((P, P), f)
    for c in range(P):
        i = c % 32
        if i < 16:
            rot[c + 16, c] = -1.0
        else:
            rot[c - 16, c] = 1.0
    n = HD // 4
    inv = (1.0 / (10000.0 ** (np.arange(n, dtype=f) / n))).astype(f)
    t = np.arange(DEC)
    pos = np.stack([(t // GRID_W).astype(f), (t % GRID_W).astype(f)])
    rope = np.zeros((P, 2, DEC), f)
    for c in range(P):
        ang = pos[(c % HD) // 32] * inv[c % 16]
        rope[c, 0], rope[c, 1] = np.cos(ang), np.sin(ang)

    def band(length):
        out = np.zeros((4, length, length), f)
        tt = np.arange(length)
        for g, w in enumerate(POOL_WINDOWS):
            lo, hi = np.clip(tt - w // 2, 0, length), np.clip(tt + w // 2, 0, length)
            s = np.arange(length)[:, None]
            out[g] = ((s >= lo) & (s < hi)) / (hi - lo).astype(f)
            out[g] -= np.eye(length, dtype=f)
        return out

    band_p = band(SEQ).transpose(1, 0, 2)
    band_s = band(DEC).reshape(4, 2, P, DEC).transpose(2, 0, 1, 3).reshape(P, 8, DEC)
    s, tt = np.arange(P)[:, None], np.arange(P)[None, :]
    strict = np.stack([s < tt, s > tt], 1).astype(f)
    incl = np.stack([s <= tt, s >= tt], 1).astype(f)
    level = np.zeros((P, LEVELS, 3, P), f)
    for k in range(LEVELS):
        b = 1 << k
        low = (s // (2 * b) == tt // (2 * b)) & ((s // b) % 2 == 1) & ((tt // b) % 2 == 0)
        level[:, k, 0], level[:, k, 1], level[:, k, 2] = low, low.T, low
    first = np.tile(np.arange(4, 0, -1, dtype=f), (P, NT, 1))
    mats = np.concatenate([ident, ones_d, head_ones, rot, rope.reshape(P, -1), strict.reshape(P, -1),
                           incl.reshape(P, -1), first.reshape(P, -1)], 1)
    bands = np.concatenate([band_p.reshape(P, -1), band_s.reshape(P, -1)], 1)
    return {"mats": np.ascontiguousarray(mats), "bands": np.ascontiguousarray(bands),
            "level": np.ascontiguousarray(level.reshape(P, -1))}


def build(nc, a, out):
    y_prompt, y_sample, new_state, new_k, new_v = out
    with ExitStack() as ctx:
        def sb(name, shape, dt=F32):
            return ctx.enter_context(nc.sbuf_tensor(name, shape, dt))

        def sem(name):
            return ctx.enter_context(nc.semaphore(name))

        bank = [ctx.enter_context(nc.psum_tensor(f"bank{i}", [P, 512], F32)) for i in range(8)]

        n_mats = a["mats"].shape[1]
        cst = sb("cst", [P, n_mats])
        at = [0]

        def const(n):
            at[0] += n
            return cst[:, at[0] - n:at[0]]

        ident, ones_d, head_ones, rot = const(P), const(P), const(P), const(P)
        rope_cos, rope_sin = const(DEC), const(DEC)
        strict = const(2 * P).rearrange("p (d n) -> p d n", d=2)
        incl = const(2 * P).rearrange("p (d n) -> p d n", d=2)
        first = const(NT * 4).rearrange("p (t n) -> p t n", t=NT)
        lev = sb("lev", [P, LEVELS, 3, P], U8)
        ones_row = sb("ones_row", [1, P])
        eps = sb("eps", [P, 3])

        h = sb("h", [P, KT, T])
        u = sb("u", [P, KT, T])
        mixed = u
        ring = sb("ring", [P, RING, SLOT])
        par = sb("par", [P, DEPTH, NPAR])
        cond = sb("cond", [P, KT, 2])
        mod = sb("mod", [P, 48, 2])
        one_less_ka = sb("one_less_ka", [P, NJ])
        lora_w2 = sb("lora_w2", [P, NJ * P])
        lora_a2 = sb("lora_a2", [P, NJ * P])
        lora_g2 = sb("lora_g2", [P, NJ * P])
        pool_w = sb("pool_w", [P, 2, HD])
        route_w = sb("route_w", [P, KT, 20])
        route_b = sb("route_b", [1, 20])
        ctx_k = sb("ctx_k", [P, P])
        ctx_v = sb("ctx_v", [P, P])
        state_nat = sb("state_nat", [P, NJ, 2, P])

        REGION = 28300
        region = sb("region", [P, REGION])
        off = [0]

        def view(*shape):
            n = int(np.prod(shape))
            v = region[:, off[0]:off[0] + n]
            off[0] += n
            assert off[0] <= REGION, off[0]
            if len(shape) == 2:
                v = v.rearrange("p (a b) -> p a b", a=shape[0])
            if len(shape) == 3:
                v = v.rearrange("p (a b c) -> p a b c", a=shape[0], b=shape[1])
            return v

        r_t = view(NJ, T)
        kk_t = view(NJ, T)
        v_t = view(NJ, T)
        kd_t = view(2, NJ, T)
        b_t = view(2, NJ, T)
        run = view(2 * NJ * NT, P + 1)
        lo_g = view(T)
        v_tok = view(NT, NJ * P)
        y_t = view(NJ, T)
        centre = view(2 * NJ * NT)
        edge = view(2 * NJ * NT)
        shared = off[0]
        x_m = view(NJ, 4, P)
        xt_m = view(NJ, 4, P)
        at_m = view(NJ, 4, P)
        t_m = view(NJ, 4, P)
        scaled = view(4, NJ, 2 * P)
        tok_m = view(2, NJ, 2 * P)
        lak = view(4, P)
        mrb = view(4, P)
        mrk = view(4, P)
        r_s = view(2, 2 * P)
        sa_s = view(2, 2 * P)
        s_t = view(NJ, 2, P)
        s_hat = view(NJ, 2, P)
        s_new = view(2, P)
        off[0] = shared
        k_t = view(NJ, T)
        lo_w = view(T)
        lo_a = view(T)
        qk = view(4, T)
        qk_s = view(4, T)
        rs = view(4, T)
        kr = view(NJ, T)
        vp = view(NT, T)
        ckt = view(P)
        kh_out = view(P)
        stat = view(3, 18)
        pool_d = view(2, T)
        bands = view(4 * SEQ + 8 * DEC)
        band_p = bands[:, 0:4 * SEQ].rearrange("p (g n) -> p g n", g=4)
        band_s = bands[:, 4 * SEQ:].rearrange("p (g n) -> p g n", g=8)
        rate = view(2, NJ, T)
        prob = qk_s[:, 0:2, :]
        prob_t = qk_s[:, 2:4, :]
        off[0] = shared
        gn_s = view(NJ, T)
        gn_r = view(NJ, T)
        off[0] = 0
        hid = view(2 * NE, T)
        sq = view(KT, T)
        rstd = view(T)
        gate_b = view(2, T)
        silu = view(2, T)
        gate_t = view(T)
        rl = view(NT, 20)
        gt = view(NT, 16)
        g4 = [view(NT, 4) for _ in range(8)]
        g1 = [view(NT) for _ in range(10)]
        les_in = view(NT, 4, 4)
        off[0] = 0
        x_in = view(NT, D)
        rows = view(DEPTH, P)
        level = view(LEVELS * 3 * P)
        off[0] = 0
        y_out = view(NT, D)
        state_out = sb("state_out", [P, NJ, 2, P])

        cst_in, x_in_s, par_in, small_in = sem("cst_in"), sem("x_in"), sem("par_in"), sem("small_in")
        slot_in = [sem(f"slot_in{i}") for i in range(RING)]
        k_out, v_out, s_out, y_out_s = sem("k_out"), sem("v_out"), sem("s_out"), sem("y_out_s")
        bands_in = sem("bands_in")
        head_mm = sem("head_mm")
        mod_mm = sem("mod_mm")
        front_mm = sem("front_mm")
        khead_mm, rot_mm, ckt_mm = sem("khead_mm"), sem("rot_mm"), sem("ckt_mm")
        score_mm, pt_mm, o_mm = sem("score_mm"), sem("pt_mm"), sem("o_mm")
        pool_mm, poolw_mm, bonus_mm = sem("pool_mm"), sem("poolw_mm"), sem("bonus_mm")
        st_mm, tok_mm, inv_mm, t_mm, x_mm = sem("st_mm"), sem("tok_mm"), sem("inv_mm"), sem("t_mm"), sem("x_mm")
        msc_mm, rhs_mm, sa_mm, ys_mm = sem("msc_mm"), sem("rhs_mm"), sem("sa_mm"), sem("ys_mm")
        so_mm, gn_mm, g_mm = sem("so_mm"), sem("gn_mm"), sem("g_mm")
        proj_mm, ln_mm = sem("proj_mm"), sem("ln_mm")
        route_mm, gatet_mm, gateb_mm, hid_mm, down_mm = (sem("route_mm"), sem("gatet_mm"), sem("gateb_mm"),
                                                         sem("hid_mm"), sem("down_mm"))
        tail_mm = sem("tail_mm")
        head_cp, cond_up, front_cp = sem("head_cp"), sem("cond_up"), sem("front_cp")
        kh_cp, ckt_cp, prob_up, pt_cp, o_cp = sem("kh_cp"), sem("ckt_cp"), sem("prob_up"), sem("pt_cp"), sem("o_cp")
        pool_cp, poolw_cp = sem("pool_cp"), sem("poolw_cp")
        edge_up, exp_up, st_cp, tok_cp, t_cp = sem("edge_up"), sem("exp_up"), sem("st_cp"), sem("tok_cp"), sem("t_cp")
        rhs_cp, sa_cp, so_cp = sem("rhs_cp"), sem("sa_cp"), sem("so_cp")
        gn_rt, gn_sq, ln_sq, ln_rt = sem("gn_rt"), sem("gn_sq"), sem("ln_sq"), sem("ln_rt")
        gexp_up, e2_up, gateb_cp, silu_up = sem("gexp_up"), sem("e2_up"), sem("gateb_cp"), sem("silu_up")
        tail_cp = sem("tail_cp")
        vec_step = sem("vec_step")
        set_up, mod_up, u_up = sem("set_up"), sem("mod_up"), sem("u_up")
        qk_sq, kk_sq, qk_up, qkr_up, max_up, pn_up = (sem("qk_sq"), sem("kk_sq"), sem("qk_up"), sem("qkr_up"),
                                                      sem("max_up"), sem("pn_up"))
        rates_up, bonus_in, bonus_up = sem("rates_up"), sem("bonus_in"), sem("bonus_up")
        scaled_up, at_up, x_up, shat_up = sem("scaled_up"), sem("at_up"), sem("x_up"), sem("shat_up")
        msc_up, ys_up, state_up = sem("msc_up"), sem("ys_up"), sem("state_up")
        gn_c, mixa_up, z_up, xc_up = sem("gn_c"), sem("mixa_up"), sem("z_up"), sem("xc_up")
        rl_up, d_up, gate_up, gatet_cp, h3_used, hid_up, z2_up, h_up = (
            sem("rl_up"), sem("d_up"), sem("gate_up"), sem("gatet_cp"), sem("h3_used"), sem("hid_up"),
            sem("z2_up"), sem("h_up"))
        x_init = sem("x_init")

        def tiles(s):
            return ((0, 0), (1, 2), (2, 1))[s]

        def tc(t):
            return slice(t * P, (t + 1) * P)

        def both(m):
            return m.unsqueeze(2).broadcast_to([P, 2, 2, P])

        def quad(ap):
            return ap.rearrange("p (d e) n -> p d e n", d=2)

        def bank4(b):
            return bank[b][:, :].rearrange("p (q n) -> p q n", q=4)

        XL = 2 * NJ * (LEVELS - 2) + NJ

        def xi(l, s, k, j, which):
            base = (l * 3 + s) * XL
            if k < LEVELS - 1:
                return base + (k - 1) * 2 * NJ + 2 * j + which + 1
            return base + (LEVELS - 2) * 2 * NJ + j + 1

        def used(n):
            l, i = divmod(n, ITEMS)
            if i < I_IN:
                return mod_mm, N_MOD * l + i + 1
            if i < I_OUT:
                return front_mm, FRONT * l + 3 * (i - I_IN + 1) + 1
            if i < I_EXP:
                return proj_mm, KT * l + sum(OUT_TILES[:i - I_OUT + 1])
            if i < I_DOWN:
                return hid_mm, 2 * NE * l + 2 * (i - I_EXP + 1)
            return down_mm, KT * l + i - I_DOWN + 1

        block = ctx.enter_context(nc.Block())

        @block.sync
        def _(sp):
            def item(l, i):
                n = l * ITEMS + i
                slot = n % RING
                if n >= RING:
                    sp.wait_ge(*used(n - RING))
                w = ring[:, slot, :]
                landed = slot_in[slot]

                def halves(dst, src):
                    k = dst.shape[1] // 2
                    sp.dma_start(dst[:, 0:k], src[:, 0:k]).then_inc(landed, 16)
                    sp.dma_start(dst[:, k:2 * k], src[:, k:2 * k]).then_inc(landed, 16)

                if i < I_IN:
                    halves(w.rearrange("p (c n) -> p c n", c=KT),
                           a["w_mod"][l].rearrange("(c p) n -> p c n", p=P)[:, :, i * 512:(i + 1) * 512])
                elif i == I_IN:
                    lo, n_cols = IN_COLS[0]
                    dst = w.rearrange("p (c n) -> p c n", c=KT)
                    src = a["w_in"][l].rearrange("(c p) n -> p c n", p=P)[:, :, lo:lo + n_cols]
                    for hq in range(GRP * KVH):
                        to = P * (hq % GRP) + HD * (hq // GRP)
                        sp.dma_start(dst[:, :, to:to + HD], src[:, :, hq * HD:(hq + 1) * HD]).then_inc(landed, 16)
                    sp.dma_start(dst[:, :, T:n_cols], src[:, :, T:n_cols]).then_inc(landed, 16)
                elif i < I_OUT:
                    lo, n_cols = IN_COLS[i - I_IN]
                    halves(w[:, 0:KT * n_cols].rearrange("p (c n) -> p c n", c=KT),
                           a["w_in"][l].rearrange("(c p) n -> p c n", p=P)[:, :, lo:lo + n_cols])
                elif i < I_EXP:
                    m = i - I_OUT
                    lo = P * sum(OUT_TILES[:m])
                    n_cols = P * OUT_TILES[m]
                    dst = w[:, 0:KT * n_cols].rearrange("p (c n) -> p c n", c=KT)
                    src = a["w_out"][l][:, lo:lo + n_cols]
                    sp.dma_start(dst[:, 0:NJ], src[0:NJ * P].rearrange("(c p) n -> p c n", p=P)).then_inc(landed, 16)
                    for g in range(KVH):
                        lo_r = NJ * P + g * GRP * HD
                        sp.dma_start(dst[g * HD:(g + 1) * HD, NJ:2 * NJ],
                                     src[lo_r:lo_r + GRP * HD].rearrange("(c p) n -> p c n", p=HD)).then_inc(landed, 16)
                    sp.dma_start(dst[:, 2 * NJ:KT],
                                 src[2 * NJ * P:D].rearrange("(c p) n -> p c n", p=P)).then_inc(landed, 16)
                elif i < I_DOWN:
                    e = i - I_EXP
                    for half, name in enumerate(("moe_w1", "moe_w3")):
                        sp.dma_start(w[:, half * 2048:(half + 1) * 2048].rearrange("p (c n) -> p c n", c=KT),
                                     a[name][l, e].rearrange("(c p) n -> p c n", p=P)).then_inc(landed, 16)
                else:
                    d = i - I_DOWN
                    halves(w.rearrange("p (f n) -> p f n", f=2 * NE),
                           a["moe_w2"][l].rearrange("e (f p) n -> p (e f) n", p=P)[:, :, tc(d)])

            for l in range(DEPTH):
                for i in range(ITEMS):
                    item(l, i)

        @block.gpsimd
        def _(pool):
            pool.dma_start(cst[:, :], a["mats"]).then_inc(cst_in, 16)
            pool.dma_start(level, a["level"]).then_inc(cst_in, 16)
            for l in range(DEPTH):
                def row(at_row, n, src, name=None):
                    pool.dma_start(rows[at_row:at_row + n, l, :], src.rearrange("(a b) -> a b", b=P)).then_inc(par_in, 16)
                row(BMOD, 48, a["b_mod"][l])
                for at_row, name in ((LN1G, "ln1_g"), (LN1B, "ln1_b"), (LN2G, "ln2_g"), (LN2B, "ln2_b")):
                    row(at_row, KT, a[name][l])
                row(W0, 6, a["rw_w0"][l].rearrange("d c -> (d c)"))
                row(A0, 6, a["rw_a0"][l].rearrange("d c -> (d c)"))
                row(KKP, NJ, a["rw_kk"][l])
                row(KAP, NJ, a["rw_ka"][l])
                row(RKP, NJ, a["rw_rk"][l].rearrange("h c -> (h c)"))
                row(GNG, NJ, a["rw_gn_g"][l])
                row(GNB, NJ, a["rw_gn_b"][l])
                row(PSC, 2, a["pool_scale"][l])
                row(COND, KT, a["c_ctx"])
                row(COND + KT, KT, a["c"][0])
                for at_row, name in ((QN, "q_norm"), (KN, "k_norm")):
                    for e in range(2):
                        pool.dma_start(rows[at_row:at_row + 1, l, e * HD:(e + 1) * HD],
                                       a[name][l].rearrange("(a b) -> a b", b=HD)).then_inc(par_in, 16)
            for l in range(DEPTH):
                if l > 0:
                    pool.wait_ge(route_mm, l)
                    pool.wait_ge(st_mm, 2 * l)
                for dst, name in ((lora_w2, "rw_w2"), (lora_a2, "rw_a2")):
                    pool.dma_start(dst[:, :], a[name][l].rearrange("d r c -> (d r) c")).then_inc(small_in, 16)
                pool.dma_start(lora_g2[:, :], a["rw_g2"][l]).then_inc(small_in, 16)
                pool.dma_start(pool_w[:, :, :],
                               a["pool_w"][l].rearrange("(t g) c d -> t (g c) d", t=2).rearrange("t p d -> p t d")
                               ).then_inc(small_in, 16)
                pool.dma_start(route_w[:, :, 0:NG], a["rt_grp_w"][l].rearrange("(c p) n -> p c n", p=P)).then_inc(small_in, 16)
                pool.dma_start(route_w[:, :, NG:20], a["rt_exp_w"][l].rearrange("(c p) n -> p c n", p=P)).then_inc(small_in, 16)
                pool.dma_start(route_b[:, 0:NG], a["rt_grp_b"][l:l + 1, :]).then_inc(small_in, 16)
                pool.dma_start(route_b[:, NG:20], a["rt_exp_b"][l:l + 1, :]).then_inc(small_in, 16)
                pool.dma_start(ctx_k[:, :], a["cache_k"][0, l].rearrange("t h c -> t (h c)")).then_inc(small_in, 16)
                pool.dma_start(ctx_v[:, :], a["cache_v"][0, l].rearrange("t h c -> t (h c)")).then_inc(small_in, 16)
                if l == 0:
                    pool.wait_ge(set_up, 1)
                for d in range(2):
                    for e in range(2):
                        src = a["state_rwkv"][0, l, d].rearrange("(j e) v k -> e v j k", e=2)[e]
                        pool.dma_start(state_nat[e * HD:(e + 1) * HD, :, d, e * HD:(e + 1) * HD], src).then_inc(small_in, 16)
                pool.wait_ge(mod_mm, N_MOD * (l + 1))
                pool.dma_start(bands, a["bands"]).then_inc(bands_in, 16)
                pool.wait_ge(front_cp, FRONT * l + 5)
                pool.dma_start(new_v[0, l].rearrange("t h c -> t (h c)"), vp[:, 0, 0:P]).then_inc(v_out, 16)
                pool.wait_ge(kh_cp, l + 1)
                pool.dma_start(new_k[0, l].rearrange("t h c -> t (h c)"), kh_out).then_inc(k_out, 16)
                for s in range(3):
                    n = l * 3 + s
                    if s == 0:
                        pool.wait_ge(poolw_cp, 2 * (l + 1))
                        pool.wait_ge(bonus_up, NJ * (l + 1))
                        pool.wait_ge(v_out, 16 * (l + 1))
                        pool.wait_ge(k_out, 16 * (l + 1))
                    else:
                        pool.wait_ge(sa_mm, NJ * n)
                    for m in (x_m, xt_m):
                        for j in range(NJ):
                            pool.tensor_copy(m[:, j], ident.unsqueeze(1).broadcast_to([P, 4, P])).then_inc(x_init, 1)
                pool.wait_ge(so_cp, 2 * (l + 1))
                for d in range(2):
                    for e in range(2):
                        dst = new_state[0, l, d].rearrange("(j e) v k -> e v j k", e=2)[e]
                        pool.dma_start(dst, state_out[e * HD:(e + 1) * HD, :, d, e * HD:(e + 1) * HD]).then_inc(s_out, 16)
            for t in range(NT):
                pool.wait_ge(tail_cp, 2 * (t + 1))
                dst = y_prompt[0] if t == 0 else y_sample[0, (t - 1) * P:t * P]
                pool.dma_start(dst, y_out[:, t, :]).then_inc(y_out_s, 16)
            pool.wait_ge(v_out, 16 * DEPTH)
            pool.wait_ge(k_out, 16 * DEPTH)
            pool.wait_ge(s_out, 64 * DEPTH)
            pool.wait_ge(y_out_s, 16 * NT)

        @block.tensor
        def _(pe):
            def item_in(l, i):
                n = l * ITEMS + i
                pe.wait_ge(slot_in[n % RING], landed_value(n))
                return ring[:, n % RING, :]

            def attention(l):
                def unit(i):
                    return i // AH, i % AH

                def scores(i):
                    t, hq = unit(i)
                    j, g = hq % GRP, hq // GRP
                    n = 18 * l + i
                    if i >= 2:
                        pe.wait_ge(prob_up, n - 1)
                        pe.wait_ge(max_up, n - 1)
                    q = qk[g * HD:(g + 1) * HD, j, tc(t)]
                    if t == 0:
                        last = pe.matmul(bank[i % 2][:, 0:P], q, qk[g * HD:(g + 1) * HD, 3, 0:P], start=True, stop=True)
                    else:
                        pe.matmul(bank[i % 2][:, 0:DEC], q, qk[g * HD:(g + 1) * HD, 3, P:T], start=True, stop=True)
                        last = pe.matmul(bank[i % 2][:, DEC:T], q, ckt[g * HD:(g + 1) * HD, :], start=True, stop=True)
                    last.then_inc(score_mm, 1)

                def turn(i):
                    t, _ = unit(i)
                    n = 18 * l + i
                    pe.wait_ge(pn_up, n + 1)
                    if i >= 2:
                        pe.wait_ge(pt_cp, n - 1)
                    for c in range(1 if t == 0 else 3):
                        last = pe.transpose(bank[2 + i % 2][:, tc(c)], prob[:, i % 2, tc(c)], ident)
                    last.then_inc(pt_mm, 1)

                def outs(i):
                    t, hq = unit(i)
                    j, g = hq % GRP, hq // GRP
                    n = 18 * l + i
                    pe.wait_ge(pt_cp, n + 1)
                    dst = bank[4 + t][g * HD:(g + 1) * HD, tc(j)]
                    if t == 0:
                        values = [vp[:, 0, g * HD:(g + 1) * HD]]
                    else:
                        values = [vp[:, 1, g * HD:(g + 1) * HD], vp[:, 2, g * HD:(g + 1) * HD],
                                  ctx_v[:, g * HD:(g + 1) * HD]]
                    for c, vals in enumerate(values):
                        last = pe.matmul(dst, vals, prob_t[:, i % 2, tc(c)], start=(c == 0), stop=(c == len(values) - 1))
                    last.then_inc(o_mm, 1)

                pe.wait_ge(qkr_up, l + 1)
                pe.wait_ge(ckt_cp, l + 1)
                for i in range(18 + 2):
                    if i < 18:
                        scores(i)
                    if 1 <= i <= 18:
                        turn(i - 1)
                    if i >= 2:
                        outs(i - 2)

            def pooling(l):
                pe.wait_ge(o_cp, 3 * l + 3)
                pe.wait_ge(bands_in, 16 * (l + 1))
                for c in range(2):
                    for g in range(2):
                        dst = bank[6 + c][g * HD:(g + 1) * HD, :]
                        src = slice(P + (2 * c + g) * HD, P + (2 * c + g + 1) * HD)
                        pe.matmul(dst[:, 0:P], vp[:, 0, src], band_p[:, 2 * c + g, :], start=True, stop=True)
                        for k in range(2):
                            last = pe.matmul(dst[:, P:T], vp[:, 1 + k, src], band_s[:, 2 * (2 * c + g) + k, :],
                                             start=(k == 0), stop=(k == 1))
                    last.then_inc(pool_mm, 1)
                for c in range(2):
                    pe.wait_ge(pool_cp, 2 * l + c + 1)
                    for g in range(2):
                        rows_g = slice(g * HD, (g + 1) * HD)
                        last = pe.matmul(bank[6 + c][rows_g, 0:T], pool_w[rows_g, c, :], pool_d[rows_g, c, :],
                                         start=True, stop=True)
                    last.then_inc(poolw_mm, 1)

            def rwkv_step(l, s):
                n = l * 3 + s
                if s == 1:
                    pe.wait_ge(so_cp, 2 * (l + 1))
                    for d2 in range(2):
                        for q in range(3):
                            jd = 3 * d2 + q
                            last = pe.transpose(bank[6 + d2][:, tc(q)], state_nat[:, jd // 2, jd % 2, :], ident)
                        last.then_inc(st_mm, 1)
                pe.wait_ge(scaled_up, n + 1)
                for kind in range(2):
                    for half in range(2):
                        b = 2 * kind + half
                        for q in range(4 if half == 0 else 2):
                            jd = 4 * half + q
                            last = pe.transpose(bank[b][:, tc(q)], scaled[:, 2 + kind, jd // 2, tc(jd % 2)], ident)
                        last.then_inc(tok_mm, 1)
                pe.wait_ge(tok_cp, 4 * (n + 1))
                for j in range(NJ):
                    for q in range(4):
                        d = q % 2
                        for e in range(2):
                            rows_e = slice(e * HD, (e + 1) * HD)
                            al, be = scaled[rows_e, 1, j, tc(d)], scaled[rows_e, 2, j, tc(d)]
                            lhs, rhs = (al, be) if q < 2 else (be, al)
                            last = pe.matmul(bank[2 * j + e][:, tc(q)], lhs, rhs, start=True, stop=True)
                            if q == 3:
                                last.then_inc(inv_mm, 1)
                for k in range(1, LEVELS):
                    for j in range(NJ):
                        if k == 1:
                            pe.wait_ge(at_up, NJ * (n + 1))
                        else:
                            pe.wait_ge(x_up, xi(l, s, k - 1, j, 1))
                        for q in range(4):
                            last = pe.matmul(bank[j][:, tc(q)], at_m[:, j, q, :], x_m[:, j, q, :], start=True, stop=True)
                        last.then_inc(t_mm, 1)
                    for j in range(NJ):
                        pe.wait_ge(t_cp, ((l * 3 + s) * (LEVELS - 1) + k - 1) * NJ + j + 1)
                        if k < LEVELS - 1:
                            for q in range(4):
                                last = pe.matmul(bank[j][:, tc(q)], xt_m[:, j, q, :], t_m[:, j, q, :], start=True, stop=True)
                            last.then_inc(x_mm, 1)
                        for q in range(4):
                            last = pe.matmul(bank[3 + j][:, tc(q)], t_m[:, j, q, :], xt_m[:, j, q, :], start=True, stop=True)
                        last.then_inc(x_mm, 1)

                def masked(j):
                    if j == 0:
                        pe.wait_ge(x_up, xi(l, s, LEVELS - 1, NJ - 1, 1))
                    else:
                        pe.wait_ge(msc_up, 3 * (NJ * n + j))
                    for m, (kl, kr_) in enumerate(((3, 1), (2, 0), (3, 0))):
                        for d in range(2):
                            for e in range(2):
                                rows_e = slice(e * HD, (e + 1) * HD)
                                last = pe.matmul(bank[2 * (m // 2) + e][:, tc(2 * (m % 2) + d)],
                                                 scaled[rows_e, kl, j, tc(d)], scaled[rows_e, kr_, j, tc(d)],
                                                 start=True, stop=True)
                                if d == 1:
                                    last.then_inc(msc_mm, 1)

                def rhs_of(j):
                    pe.wait_ge(msc_up, 3 * (NJ * n + j) + 1)
                    pe.wait_ge(shat_up, n + 1)
                    if n * NJ + j > 0:
                        pe.wait_ge(rhs_cp, NJ * n + j)
                    for d in range(2):
                        t = tiles(s)[d]
                        pe.matmul(bank[6][:, tc(d)], scaled[:, 1, j, tc(d)], s_hat[:, j, d, :], start=True, stop=False,
                                  skip_group_check=True)
                        for e in range(2):
                            col = slice(d * P + e * HD, d * P + (e + 1) * HD)
                            last = pe.matmul(bank[6][:, col], lak[:, 2 * d + e, :],
                                             v_tok[:, t, j * P + e * HD:j * P + (e + 1) * HD], start=False, stop=True,
                                             skip_group_check=True)
                    last.then_inc(rhs_mm, 1)

                def solve(j):
                    pe.wait_ge(rhs_cp, NJ * n + j + 1)
                    if n * NJ + j > 0:
                        pe.wait_ge(sa_cp, NJ * n + j)
                    for q in range(4):
                        col = slice(q * HD, (q + 1) * HD)
                        last = pe.matmul(bank[7][:, col], xt_m[:, j, q, :], r_s[:, j % 2, col], start=True, stop=True)
                    last.then_inc(sa_mm, 1)

                def outputs(j):
                    b = 4 + j % 2
                    pe.wait_ge(sa_cp, NJ * n + j + 1)
                    pe.wait_ge(msc_up, 3 * (NJ * n + j) + 3)
                    if j == 2:
                        pe.wait_ge(ys_up, NJ * n + 1)
                    for d in range(2):
                        t = tiles(s)[d]
                        pe.matmul(bank[b][:, tc(d)], s_hat[:, j, d, :], scaled[:, 0, j, tc(d)], start=True, stop=False,
                                  skip_group_check=True)
                        for e in range(2):
                            rows_e = slice(e * HD, (e + 1) * HD)
                            pe.matmul(bank[b][rows_e, tc(d)], sa_s[:, j % 2, d * P + e * HD:d * P + (e + 1) * HD],
                                      mrb[:, 2 * d + e, :], start=False, stop=False, skip_group_check=True)
                            pe.matmul(bank[b][rows_e, tc(d)], v_tok[:, t, j * P + e * HD:j * P + (e + 1) * HD],
                                      mrk[:, 2 * d + e, :], start=False, stop=True, skip_group_check=True)
                        dst = bank[b][:, tc(2 + d)]
                        pe.matmul(dst, tok_m[:, 1, j, tc(d)], v_tok[:, t, tc(j)], start=True, stop=False,
                                  skip_group_check=True)
                        last = pe.matmul(dst, tok_m[:, 0, j, tc(d)], sa_s[:, j % 2, tc(d)], start=False, stop=True,
                                         skip_group_check=True)
                    last.then_inc(ys_mm, 1)

                masked(0)
                rhs_of(0)
                for j in range(NJ):
                    if j + 1 < NJ:
                        masked(j + 1)
                    solve(j)
                    outputs(j)
                    if j + 1 < NJ:
                        rhs_of(j + 1)
                if s == 0:
                    pe.wait_ge(state_up, NJ * n + NJ)
                    for d2 in range(2):
                        for q in range(3):
                            jd = 3 * d2 + q
                            last = pe.transpose(bank[6 + d2][:, tc(q)], s_t[:, jd // 2, jd % 2, :], ident)
                        last.then_inc(so_mm, 1)

            def norm_sums(l, which, ready, per):
                src = h if which == 0 else sq
                for c in range(KT):
                    pe.wait_ge(ready, per(c))
                    last = pe.matmul(bank[4 + which][:, 0:T], ones_d, src[:, c, :], start=(c == 0), stop=(c == KT - 1))
                last.then_inc(ln_mm, 1)

            pe.wait_ge(cst_in, 32)
            pe.wait_ge(par_in, 16 * N_PAR_DMAS * DEPTH)
            for l in range(DEPTH):
                pe.transpose(bank[l][:, 0:NPAR], rows[0:NPAR, l, :], ident[0:NPAR, 0:NPAR]).then_inc(head_mm, 1)
            pe.wait_ge(x_in_s, 16 * NT)
            for t in range(NT):
                for half in range(2):
                    for q in range(4):
                        last = pe.transpose(bank[2 + 2 * t + half][:, tc(q)], x_in[:, t, tc(4 * half + q)], ident)
                    last.then_inc(head_mm, 1)

            for l in range(DEPTH):
                if l == 0:
                    pe.wait_ge(cond_up, 1)
                    pe.wait_ge(head_cp, 8)
                else:
                    pe.wait_ge(z2_up, KT * l)
                for i in range(N_MOD):
                    w = item_in(l, I_MOD + i).rearrange("p (c n) -> p c n", c=KT)
                    for m in range(4):
                        for c in range(KT):
                            last = pe.matmul(bank[7][:, 2 * (4 * i + m):2 * (4 * i + m) + 2], w[:, c, tc(m)],
                                             cond[:, c, :], start=(c == 0), stop=(c == KT - 1))
                    last.then_inc(mod_mm, 1)
                n_front = [0]

                def front_bank():
                    n = FRONT * l + n_front[0]
                    b = n_front[0] % 7
                    if n_front[0] >= 7:
                        pe.wait_ge(front_cp, n - 6)
                    n_front[0] += 1
                    return bank[b]

                for c in range(KT):
                    pe.wait_ge(u_up, 2 * KT * l + c + 1)
                for i in range(N_IN):
                    n_cols = IN_COLS[i][1]
                    w = item_in(l, I_IN + i)[:, 0:KT * n_cols].rearrange("p (c n) -> p c n", c=KT)
                    for m in range(4 if i == 0 else 3):
                        dst = front_bank()
                        for c in range(KT):
                            if i in (1, 2):
                                last_c = pe.matmul(dst[:, 0:n_cols], u[:, c, tc(m)], w[:, c, :],
                                                   start=(c == 0), stop=(c == KT - 1))
                            else:
                                last_c = pe.matmul(dst[:, 0:T], w[:, c, tc(m)], u[:, c, :],
                                                   start=(c == 0), stop=(c == KT - 1))
                        last_c.then_inc(front_mm, 1)
                pe.wait_ge(small_in, 16 * SMALL * (l + 1))
                for d in range(2):
                    for j in range(NJ):
                        for w2, lo in ((lora_w2, lo_w), (lora_a2, lo_a)):
                            dst = front_bank()
                            pe.wait_ge(front_cp, FRONT * l + 12)
                            pe.matmul(dst[:, 0:T], w2[d * HD:(d + 1) * HD, tc(j)], lo[d * HD:(d + 1) * HD, :],
                                      start=True, stop=True).then_inc(front_mm, 1)
                pe.wait_ge(qk_sq, l + 1)
                for m in range(4):
                    dst = front_bank()
                    pe.matmul(dst[:, 0:T], head_ones, qk_s[:, m, :], start=True, stop=True).then_inc(front_mm, 1)
                pe.wait_ge(kk_sq, l + 1)
                for j in range(NJ):
                    dst = front_bank()
                    pe.matmul(dst[:, 0:T], head_ones, kr[:, j, :], start=True, stop=True).then_inc(front_mm, 1)
                for j in range(NJ):
                    dst = front_bank()
                    for t in range(NT):
                        last = pe.transpose(dst[:, tc(t)], v_tok[:, t, tc(j)], ident)
                    last.then_inc(front_mm, 1)
                pe.wait_ge(front_cp, FRONT * (l + 1))
                pe.transpose(bank[0][:, 0:P], ctx_k[:, :], ident).then_inc(ckt_mm, 1)
                pe.wait_ge(qk_up, l + 1)
                pe.transpose(bank[1][:, 0:P], qk[:, 3, 0:P], ident).then_inc(khead_mm, 1)
                for m in range(4):
                    last = pe.matmul(bank[2 + m // 2][:, (m % 2) * DEC:(m % 2 + 1) * DEC], rot, qk[:, m, P:T],
                                     start=True, stop=True)
                    if m % 2:
                        last.then_inc(rot_mm, 1)
                pe.wait_ge(kh_cp, l + 1)
                attention(l)
                pooling(l)
                pe.wait_ge(bonus_in, l + 1)
                for j in range(NJ):
                    pe.matmul(bank[j][:, 0:T], head_ones, kr[:, j, :], start=True, stop=True).then_inc(bonus_mm, 1)
                pe.wait_ge(bonus_up, NJ * (l + 1))
                for s in range(3):
                    rwkv_step(l, s)
                pe.wait_ge(state_up, NJ * 3 * (l + 1))
                for j in range(NJ):
                    pe.matmul(bank[j][:, 0:T], head_ones, y_t[:, j, :], start=True, stop=True).then_inc(gn_mm, 1)
                for j in range(NJ):
                    pe.matmul(bank[3 + j][:, 0:T], lora_g2[:, tc(j)], lo_g, start=True, stop=True).then_inc(g_mm, 1)
                for j in range(NJ):
                    pe.wait_ge(gn_sq, NJ * l + j + 1)
                    pe.matmul(bank[j][:, 0:T], head_ones, gn_s[:, j, :], start=True, stop=True).then_inc(gn_mm, 1)
                pe.wait_ge(mixa_up, NJ * (l + 1))
                pe.wait_ge(poolw_cp, 2 * (l + 1))
                dt = 0
                for i in range(N_OUT):
                    w = item_in(l, I_OUT + i)[:, 0:KT * P * OUT_TILES[i]].rearrange("p (c n) -> p c n", c=KT)
                    for m in range(OUT_TILES[i]):
                        if dt >= 4:
                            pe.wait_ge(z_up, KT * l + dt - 3)
                        for c in range(KT):
                            last = pe.matmul(bank[dt % 4][:, 0:T], w[:, c, tc(m)], mixed[:, c, :],
                                             start=(c == 0), stop=(c == KT - 1))
                        last.then_inc(proj_mm, 1)
                        dt += 1
                norm_sums(l, 0, z_up, lambda c: KT * l + c + 1)
                norm_sums(l, 1, ln_sq, lambda c: KT * (2 * l) + c + 1)
                for c in range(KT):
                    pe.wait_ge(u_up, 2 * KT * l + KT + c + 1)
                for t in range(NT):
                    dst = bank[7][:, t * 20:(t + 1) * 20]
                    for c in range(KT):
                        pe.matmul(dst, u[:, c, tc(t)], route_w[:, c, :], start=(c == 0), stop=False)
                    last = pe.matmul(dst, ones_row[:, :], route_b[:, :], start=False, stop=True)
                last.then_inc(route_mm, 1)

                def hidden(e):
                    w = item_in(l, I_EXP + e).rearrange("p (w c n) -> p w c n", w=2, c=KT)
                    for f in range(2):
                        n = 32 * l + 2 * e + f
                        un = 2 * e + f
                        b = 2 * (un % 3)
                        if un >= 3:
                            pe.wait_ge(silu_up, n - 2)
                            pe.wait_ge(h3_used, n - 2)
                        else:
                            pe.wait_ge(h_up, KT * (2 * l + 1))
                        for which in range(2):
                            for c in range(KT):
                                last = pe.matmul(bank[b + which][:, 0:T], w[:, which, c, tc(f)], u[:, c, :],
                                                 start=(c == 0), stop=(c == KT - 1))
                        last.then_inc(hid_mm, 1)

                def gate_row(e):
                    n = NE * l + e
                    if e >= 1:
                        pe.wait_ge(gateb_cp, n)
                    pe.matmul(bank[6][:, 0:T], ident[0:NE, e:e + 1].broadcast_to([NE, P]), gate_t[0:NE, :],
                              start=True, stop=True).then_inc(gateb_mm, 1)

                hidden(0)
                pe.wait_ge(gate_up, l + 1)
                for t in range(NT):
                    last = pe.transpose(bank[7][0:NE, tc(t)], gt[:, t, :], ident)
                last.then_inc(gatet_mm, 1)
                pe.wait_ge(gatet_cp, l + 1)
                gate_row(0)
                for e in range(1, NE):
                    gate_row(e)
                    hidden(e)
                pe.wait_ge(hid_up, 32 * (l + 1))
                for d in range(N_DOWN):
                    w = item_in(l, I_DOWN + d).rearrange("p (f n) -> p f n", f=2 * NE)
                    if d >= 4:
                        pe.wait_ge(z2_up, KT * l + d - 3)
                    for f in range(2 * NE):
                        last = pe.matmul(bank[d % 4][:, 0:T], w[:, f, :], hid[:, f, :], start=(f == 0), stop=(f == 2 * NE - 1))
                    last.then_inc(down_mm, 1)
                norm_sums(l, 0, z2_up, lambda c: KT * l + c + 1)
                norm_sums(l, 1, ln_sq, lambda c: KT * (2 * l + 1) + c + 1)
            pe.wait_ge(h_up, KT * 2 * DEPTH)
            for t in range(NT):
                for half in range(2):
                    for q in range(4):
                        last = pe.transpose(bank[2 * t + half][:, tc(q)], h[:, 4 * half + q, tc(t)], ident)
                    last.then_inc(tail_mm, 1)

        @block.scalar
        def _(act):
            def copy(dst, src):
                return act.activation(dst, src, ACT.Copy)

            for t in range(NT):
                src = a["x_prompt"][0] if t == 0 else a["x_sample"][0, (t - 1) * P:t * P]
                act.dma_start(x_in[:, t, :], src).then_inc(x_in_s, 16)
            for l in range(DEPTH):
                act.wait_ge(head_mm, l + 1)
                copy(par[:, l, :], bank[l][:, 0:NPAR]).then_inc(head_cp, 1)
            act.wait_ge(head_cp, 1)
            act.activation(cond[:, :, :], par[:, 0, COND:COND + 2 * KT].rearrange("p (s k) -> p k s", s=2),
                           ACT.Silu).then_inc(cond_up, 1)
            for g in range(2 * NT):
                t, half = g // 2, g % 2
                act.wait_ge(head_mm, DEPTH + g + 1)
                copy(h[:, 4 * half:4 * half + 4, tc(t)], bank4(2 + g)).then_inc(head_cp, 1)
            act.wait_ge(set_up, 1)

            def front(l):
                def arrived(n):
                    act.wait_ge(front_mm, FRONT * l + n + 1)
                    return bank[n % 7][:, 0:T]

                jobs = [(qk[:, m, :], ACT.Copy) for m in range(4)]
                jobs += [(vp[:, t, :], ACT.Copy) for t in range(NT)]
                jobs += [(v_tok[:, t, :], ACT.Copy) for t in range(NT)]
                jobs += [(lo_w, ACT.Tanh), (lo_a, ACT.Copy), (lo_g, ACT.Sigmoid)]
                jobs += [(r_t[:, j, :], ACT.Copy) for j in range(NJ)]
                jobs += [(k_t[:, j, :], ACT.Copy) for j in range(NJ)]
                n = 0
                for dst, func in jobs:
                    act.activation(dst, arrived(n), func).then_inc(front_cp, 1)
                    n += 1
                for d in range(2):
                    for j in range(NJ):
                        for dst, col in ((rate, W0), (b_t, A0)):
                            act.activation(dst[:, d, j, :], arrived(n), ACT.Sigmoid,
                                           bias=par[:, l, col + 3 * d + j:col + 3 * d + j + 1]).then_inc(front_cp, 1)
                            n += 1
                for m in range(4):
                    act.activation(rs[:, m, :], arrived(n), ACT.Sqrt, bias=eps[:, 0:1], scale=1.0 / HD).then_inc(front_cp, 1)
                    n += 1
                for j in range(NJ):
                    act.activation(y_t[:, j, :], arrived(n), ACT.Sqrt).then_inc(front_cp, 1)
                    n += 1
                for j in range(NJ):
                    copy(v_t[:, j, :], arrived(n)).then_inc(front_cp, 1)
                    n += 1

            def attention(l):
                def width(i):
                    return P if i < AH else T

                def exps(i):
                    n = 18 * l + i
                    act.wait_ge(max_up, n + 1)
                    if i >= 2:
                        act.wait_ge(pt_mm, n - 1)
                    act.activation(prob[:, i % 2, 0:width(i)], bank[i % 2][:, 0:width(i)], ACT.Exp,
                                   bias=stat[:, 0, i:i + 1], scale=HD ** -0.5,
                                   accum_out=stat[:, 1, i:i + 1]).then_inc(prob_up, 1)

                def turned(i):
                    n = 18 * l + i
                    act.wait_ge(pt_mm, n + 1)
                    if i >= 2:
                        act.wait_ge(o_mm, n - 1)
                    copy(prob_t[:, i % 2, 0:width(i)], bank[2 + i % 2][:, 0:width(i)]).then_inc(pt_cp, 1)

                def heads(t):
                    act.wait_ge(o_mm, 18 * l + AH * (t + 1))
                    copy(mixed[:, NJ:2 * NJ, tc(t)],
                         bank[4 + t][:, 0:T].rearrange("p (j n) -> p j n", j=NJ)).then_inc(o_cp, 1)

                for i in range(19):
                    if i < 18:
                        exps(i)
                    if i >= 1:
                        turned(i - 1)
                    if i >= 7 and (i - 7) % AH == 0:
                        heads((i - 7) // AH)
                heads(2)

            def rwkv_step(l, s):
                n = l * 3 + s
                if s > 0:
                    act.wait_ge(ys_mm, NJ * n)
                for d, kinds in enumerate((((0, 1, -1), (1, 0, -1), (2, 1, 1)), ((0, 0, 1), (1, 1, 1), (2, 0, -1)))):
                    t = tiles(s)[d]
                    runs = run[:, 9 * d:9 * d + 9, :].rearrange("p (j t) n -> p j t n", j=NJ)[:, :, t, :]
                    for kind, with_t, sign in kinds:
                        act.activation(scaled[:, kind, :, tc(d)], runs[:, :, with_t:with_t + P], ACT.Exp,
                                       scale=sign * DECAY).then_inc(exp_up, 1)
                if s == 1:
                    for d2 in range(2):
                        act.wait_ge(st_mm, 2 * l + d2 + 1)
                        copy(s_t.rearrange("p j d n -> p (j d) n")[:, 3 * d2:3 * d2 + 3, :],
                             bank4(6 + d2)[:, 0:3, :]).then_inc(st_cp, 1)
                for kind in range(2):
                    for half in range(2):
                        w = 4 if half == 0 else 2
                        act.wait_ge(tok_mm, 4 * n + 2 * kind + half + 1)
                        copy(tok_m[:, kind].rearrange("p j n -> p (j n)")[:, 512 * half:512 * half + w * P],
                             bank[2 * kind + half][:, 0:w * P]).then_inc(tok_cp, 1)
                for k in range(1, LEVELS):
                    for j in range(NJ):
                        act.wait_ge(t_mm, (n * (LEVELS - 1) + k - 1) * NJ + j + 1)
                        copy(t_m[:, j], bank4(j)).then_inc(t_cp, 1)
                for j in range(NJ):
                    act.wait_ge(rhs_mm, NJ * n + j + 1)
                    copy(r_s[:, j % 2, :], bank[6][:, 0:2 * P]).then_inc(rhs_cp, 1)
                    act.wait_ge(sa_mm, NJ * n + j + 1)
                    copy(sa_s[:, j % 2, :], bank[7][:, 0:2 * P]).then_inc(sa_cp, 1)
                if s == 0:
                    if l > 0:
                        act.wait_ge(s_out, 64 * l)
                    for d2 in range(2):
                        act.wait_ge(so_mm, 2 * l + d2 + 1)
                        copy(state_out[:, :, :, :].rearrange("p j d n -> p (j d) n")[:, 3 * d2:3 * d2 + 3, :],
                             bank4(6 + d2)[:, 0:3, :]).then_inc(so_cp, 1)

            def norm(l, which):
                n = 2 * l + which
                for c in range(KT):
                    act.wait_ge(xc_up, KT * n + c + 1)
                    act.activation(sq[:, c, :], h[:, c, :], ACT.Square).then_inc(ln_sq, 1)
                act.wait_ge(ln_mm, 2 * n + 2)
                act.activation(rstd, bank[5][:, 0:T], ACT.Sqrt, bias=eps[:, 2:3]).then_inc(ln_rt, 1)

            for l in range(DEPTH):
                front(l)
                act.wait_ge(ckt_mm, l + 1)
                copy(ckt, bank[0][:, 0:P]).then_inc(ckt_cp, 1)
                act.wait_ge(khead_mm, l + 1)
                copy(kh_out, bank[1][:, 0:P]).then_inc(kh_cp, 1)
                attention(l)
                for c in range(2):
                    act.wait_ge(pool_mm, 2 * l + c + 1)
                    copy(pool_d[:, c, :], bank[6 + c][:, 0:T]).then_inc(pool_cp, 1)
                for c in range(2):
                    act.wait_ge(poolw_mm, 2 * l + c + 1)
                    act.activation(mixed[:, 2 * NJ + c, :], bank[6 + c][:, 0:T], ACT.Copy,
                                   scale=par[:, l, PSC + c:PSC + c + 1]).then_inc(poolw_cp, 1)
                act.wait_ge(rates_up, l + 1)
                act.activation(edge, centre, ACT.Exp, scale=-DECAY).then_inc(edge_up, 1)
                act.wait_ge(bonus_up, NJ * (l + 1))
                act.wait_ge(v_out, 16 * (l + 1))
                act.wait_ge(k_out, 16 * (l + 1))
                for s in range(3):
                    rwkv_step(l, s)
                for j in range(NJ):
                    act.wait_ge(gn_c, NJ * l + j + 1)
                    act.activation(gn_s[:, j, :], y_t[:, j, :], ACT.Square).then_inc(gn_sq, 1)
                for j in range(NJ):
                    act.wait_ge(gn_mm, 2 * NJ * l + NJ + j + 1)
                    act.activation(gn_r[:, j, :], bank[j][:, 0:T], ACT.Sqrt, bias=eps[:, 1:2],
                                   scale=1.0 / HD).then_inc(gn_rt, 1)
                norm(l, 0)
                act.wait_ge(d_up, 2 * l + 1)
                act.activation(g4[1], g4[0], ACT.Exp).then_inc(gexp_up, 1)
                act.wait_ge(d_up, 2 * l + 2)
                act.activation(g1[1], g1[0], ACT.Exp).then_inc(e2_up, 1)

                def hidden(e):
                    for f in range(2):
                        n = 2 * NE * l + 2 * e + f
                        un = 2 * e + f
                        act.wait_ge(hid_mm, n + 1)
                        if un >= 2:
                            act.wait_ge(hid_up, n - 1)
                        act.activation(silu[:, un % 2, :], bank[2 * (un % 3)][:, 0:T], ACT.Silu).then_inc(silu_up, 1)

                def gate_row(e):
                    act.wait_ge(gateb_mm, NE * l + e + 1)
                    if e >= 2:
                        act.wait_ge(hid_up, 2 * NE * l + 2 * e - 2)
                    copy(gate_b[:, e % 2, :], bank[6][:, 0:T]).then_inc(gateb_cp, 1)

                hidden(0)
                gate_row(0)
                for e in range(1, NE):
                    gate_row(e)
                    hidden(e)
                norm(l, 1)
            for g in range(2 * NT):
                t, half = g // 2, g % 2
                act.wait_ge(tail_mm, g + 1)
                copy(y_out[:, t, 512 * half:512 * half + 512], bank[g][:, :]).then_inc(tail_cp, 1)

        @block.vector
        def _(dve):
            steps = [0]

            def mark(ins):
                steps[0] += 1
                ins.then_inc(vec_step, 1)
                return steps[0]

            def after(n=None):
                dve.wait_ge(vec_step, steps[0] if n is None else n)

            def link(ins):
                mark(ins)
                after()

            tt, ts, stt = dve.tensor_tensor, dve.tensor_scalar, dve.scalar_tensor_tensor
            dve.memset(eps[:, 0:1], QK_EPS)
            dve.memset(eps[:, 1:2], GN_EPS)
            dve.memset(eps[:, 2:3], LN_EPS / ALPHA ** 2)
            dve.memset(ones_row[:, :], 1.0)
            dve.memset(state_nat[:, :, :, :], 0.0).then_inc(set_up, 1)
            dve.wait_ge(cst_in, 32)
            link(dve.tensor_copy(lev[:, :, :, :].rearrange("p a b n -> p (a b n)"), level))

            def modulate(l, which):
                base = 24 * which
                for c in range(KT):
                    for g, (lo, hi) in enumerate(STREAMS):
                        last = ts(u[:, c, lo:hi], h[:, c, lo:hi], mod[:, base + 8 + c, g:g + 1],
                                  mod[:, base + c, g:g + 1], ALU.mult, ALU.add)
                    last.then_inc(u_up, 1)

            def residual(l, c, base, psum, done):
                for g, (lo, hi) in enumerate(STREAMS):
                    last = stt(h[:, c, lo:hi], psum[:, lo:hi], mod[:, base + c, g:g + 1], h[:, c, lo:hi],
                               ALU.mult, ALU.add)
                last.then_inc(done, 1)

            def norm(l, which):
                n = 2 * l + which
                g0, b0 = ((LN1G, LN1B), (LN2G, LN2B))[which]
                dve.wait_ge(ln_mm, 2 * n + 1)
                for c in range(KT):
                    tt(h[:, c, :], h[:, c, :], bank[4][:, 0:T], ALU.subtract).then_inc(xc_up, 1)
                dve.wait_ge(ln_rt, n + 1)
                link(dve.reciprocal(rstd, rstd))
                first_step = steps[0]
                dve.wait_ge(ln_sq, KT * (n + 1))
                for c in range(KT):
                    mark(stt(h[:, c, :], h[:, c, :], par[:, l, g0 + c:g0 + c + 1], rstd, ALU.mult, ALU.mult))
                for c in range(KT):
                    after(first_step + c + 1)
                    ts(h[:, c, :], h[:, c, :], par[:, l, b0 + c:b0 + c + 1], None, ALU.add).then_inc(h_up, 1)
                dve.wait_ge(h_up, KT * (n + 1))

            def front(l):
                base = FRONT * l
                dve.wait_ge(front_cp, base + 4)
                tt(qk_s, qk, qk, ALU.mult).then_inc(qk_sq, 1)
                dve.memset(run[:, :, 0:1], 0.0)
                dve.wait_ge(front_cp, base + 19)
                for j in range(NJ):
                    last = ts(kk_t[:, j, :], k_t[:, j, :], par[:, l, KKP + j:KKP + j + 1], None, ALU.mult)
                link(last)
                tt(kr, kk_t, kk_t, ALU.mult).then_inc(kk_sq, 1)
                dve.wait_ge(front_cp, base + 31)
                for d in range(2):
                    for j in range(NJ):
                        for t in range(NT):
                            src = rate[:, d, j, tc(t)]
                            last = dve.tensor_tensor_scan(run[:, 9 * d + 3 * j + t, 1:P + 1], src, src, 0.0,
                                                          ALU.add, ALU.max)
                link(last)
                link(ts(centre, run[:, :, P], 0.5, None, ALU.mult))
                tt(run, run, centre.unsqueeze(2).broadcast_to([P, 2 * NJ * NT, P + 1]), ALU.subtract).then_inc(rates_up, 1)
                for d in range(2):
                    for j in range(NJ):
                        last = ts(kd_t[:, d, j, :], b_t[:, d, j, :], par[:, l, KAP + j:KAP + j + 1],
                                  one_less_ka[:, j:j + 1], ALU.mult, ALU.add)
                link(last)
                for d in range(2):
                    last = tt(kd_t[:, d], kd_t[:, d], k_t, ALU.mult)
                link(last)
                dve.wait_ge(front_cp, base + 35)
                link(dve.reciprocal(rs, rs))
                for m in range(4):
                    col = QN if m < 3 else KN
                    last = stt(qk[:, m, :], qk[:, m, :], par[:, l, col:col + 1], rs[:, m, :], ALU.mult, ALU.mult)
                last.then_inc(qk_up, 1)
                dve.wait_ge(front_cp, base + 38)
                link(ts(y_t, y_t, 1e-12, None, ALU.max))
                link(dve.reciprocal(y_t, y_t))
                link(tt(kk_t, kk_t, y_t, ALU.mult))
                for d in range(2):
                    mark(tt(b_t[:, d], b_t[:, d], kk_t, ALU.mult))
                link(tt(kr, kd_t[:, 0], kd_t[:, 1], ALU.add))
                for j in range(NJ):
                    last = stt(kr[:, j, :], r_t[:, j, :], par[:, l, RKP + j:RKP + j + 1], kr[:, j, :], ALU.mult, ALU.mult)
                last.then_inc(bonus_in, 1)
                dve.wait_ge(qk_up, l + 1)
                mark(tt(rs[:, :, P:T], qk[:, :, P:T], rope_cos.unsqueeze(1).broadcast_to([P, 4, DEC]), ALU.mult))
                for m in range(2):
                    dve.wait_ge(rot_mm, 2 * l + m + 1)
                    last = tt(qk_s[:, 2 * m:2 * m + 2, P:T], bank[2 + m][:, :].rearrange("p (m n) -> p m n", m=2),
                              rope_sin.unsqueeze(1).broadcast_to([P, 2, DEC]), ALU.mult)
                link(last)
                tt(qk[:, :, P:T], rs[:, :, P:T], qk_s[:, :, P:T], ALU.add).then_inc(qkr_up, 1)

            def attention(l):
                def maxima(i):
                    w = P if i < AH else T
                    dve.wait_ge(score_mm, 18 * l + i + 1)
                    link(dve.tensor_reduce(stat[:, 2, i:i + 1], bank[i % 2][:, 0:w], AX.X, ALU.max, negate=True))
                    ts(stat[:, 0, i:i + 1], stat[:, 2, i:i + 1], HD ** -0.5, None, ALU.mult).then_inc(max_up, 1)

                def normal(i):
                    w = P if i < AH else T
                    dve.wait_ge(prob_up, 18 * l + i + 1)
                    link(dve.reciprocal(stat[:, 2, i:i + 1], stat[:, 1, i:i + 1]))
                    ts(prob[:, i % 2, 0:w], prob[:, i % 2, 0:w], stat[:, 2, i:i + 1], None, ALU.mult).then_inc(pn_up, 1)

                for i in range(19):
                    if i < 18:
                        maxima(i)
                    if i >= 1:
                        normal(i - 1)

            def rwkv_step(l, s):
                n = l * 3 + s
                if s == 0:
                    link(dve.memset(s_t, 0.0))
                if s == 1:
                    dve.wait_ge(st_cp, 2 * (l + 1))
                dve.wait_ge(edge_up, l + 1)
                for d in range(2):
                    t = tiles(s)[d]
                    for j in range(NJ):
                        i = 9 * d + 3 * j + t
                        last = ts(s_hat[:, j, d, :], s_t[:, j, d, :], edge[:, i:i + 1], None, ALU.mult)
                last.then_inc(shat_up, 1)
                dve.wait_ge(exp_up, 6 * (n + 1))
                for d in range(2):
                    t = tiles(s)[d]

                    def part(kind):
                        return scaled[:, kind, :, tc(d)]

                    tt(part(0), part(0), r_t[:, :, tc(t)], ALU.mult)
                    stt(part(1), kk_t[:, :, tc(t)], -1.0, part(1), ALU.mult, ALU.mult)
                    mark(tt(part(3), part(2), kd_t[:, d, :, tc(t)], ALU.mult))
                    last = tt(part(2), part(2), b_t[:, d, :, tc(t)], ALU.mult)
                last.then_inc(scaled_up, 1)
                dve.wait_ge(x_init, 2 * NJ * (n + 1))
                for j in range(NJ):
                    for e in range(2):
                        b = bank4(2 * j + e)
                        dve.wait_ge(inv_mm, 2 * (NJ * n + j) + e + 1)
                        dve.copy_predicated(quad(x_m[:, j])[:, :, e, :], lev[:, 0, 0:2, :], b[:, 0:2, :])
                        tt(quad(at_m[:, j])[:, :, e, :], b[:, 2:4, :], strict, ALU.mult)
                        last = dve.copy_predicated(quad(xt_m[:, j])[:, :, e, :], lev[:, 0, 1:3, :], b[:, 2:4, :])
                    last.then_inc(at_up, 1)
                for k in range(1, LEVELS):
                    for j in range(NJ):
                        if k < LEVELS - 1:
                            dve.wait_ge(x_mm, xi(l, s, k, j, 0))
                            dve.copy_predicated(quad(x_m[:, j]), both(lev[:, k, 0:2, :]), quad(bank4(j))).then_inc(x_up, 1)
                        dve.wait_ge(x_mm, xi(l, s, k, j, 1))
                        dve.copy_predicated(quad(xt_m[:, j]), both(lev[:, k, 1:3, :]), quad(bank4(3 + j))).then_inc(x_up, 1)

                def masks(j):
                    for m, (dst, mask) in enumerate(((lak, strict), (mrb, incl), (mrk, incl))):
                        for e in range(2):
                            dve.wait_ge(msc_mm, 6 * (NJ * n + j) + 2 * max(m, 1) + e + 1)
                            last = tt(quad(dst)[:, :, e, :], bank4(2 * (m // 2) + e)[:, 2 * (m % 2):2 * (m % 2) + 2, :],
                                      mask, ALU.mult)
                        last.then_inc(msc_up, 1)

                def outputs(j):
                    b = 4 + j % 2
                    dve.wait_ge(ys_mm, NJ * n + j + 1)
                    for d in range(2):
                        t = tiles(s)[d]
                        dst = y_t[:, j, tc(t)]
                        if s == 1 or (s == 0 and d == 0):
                            link(dve.tensor_copy(dst, bank[b][:, tc(d)]))
                        else:
                            link(tt(dst, dst, bank[b][:, tc(d)], ALU.add))
                    for d in range(2):
                        i = 9 * d + 3 * j + tiles(s)[d]
                        last = stt(s_new[:, d, :], bank[b][:, tc(2 + d)], edge[:, i:i + 1], head_ones, ALU.mult, ALU.mult)
                    last.then_inc(ys_up, 1)
                    dve.wait_ge(ys_up, NJ * n + j + 1)
                    for d in range(2):
                        i = 9 * d + 3 * j + tiles(s)[d]
                        last = stt(s_t[:, j, d, :], s_hat[:, j, d, :], edge[:, i:i + 1], s_new[:, d, :], ALU.mult, ALU.add)
                    last.then_inc(state_up, 1)

                masks(0)
                for j in range(NJ):
                    outputs(j)
                    if j + 1 < NJ:
                        masks(j + 1)
                dve.wait_ge(state_up, NJ * (n + 1))

            def heads_norm(l):
                for j in range(NJ):
                    dve.wait_ge(gn_mm, 2 * NJ * l + j + 1)
                    stt(y_t[:, j, :], bank[j][:, 0:T], -1.0 / HD, y_t[:, j, :], ALU.mult, ALU.add).then_inc(gn_c, 1)
                dve.wait_ge(gn_rt, NJ * (l + 1))
                link(dve.reciprocal(gn_r, gn_r))
                link(tt(y_t, y_t, gn_r, ALU.mult))
                for j in range(NJ):
                    last = ts(y_t[:, j, :], y_t[:, j, :], par[:, l, GNG + j:GNG + j + 1], par[:, l, GNB + j:GNB + j + 1],
                              ALU.mult, ALU.add)
                link(last)
                link(tt(y_t, y_t, v_t, ALU.add))
                for j in range(NJ):
                    dve.wait_ge(g_mm, NJ * l + j + 1)
                    tt(mixed[:, j, :], y_t[:, j, :], bank[3 + j][:, 0:T], ALU.mult).then_inc(mixa_up, 1)

            def route(l):
                gd, ge, gm, gsel, ls, oh1, oh2, gtmp = g4
                mx, e2, s_g, m1, m2, mw, den, p1, p2, p1e = (g1[2], g1[1], g1[3], g1[4], g1[5], g1[6], g1[7], g1[8],
                                                            g1[9], g1[0])

                def wide(v):
                    return v.unsqueeze(2).broadcast_to([P, NT, 4])

                def first_of(dst, src, top):
                    link(tt(gtmp, src, wide(top), ALU.is_equal))
                    link(tt(gtmp, gtmp, first, ALU.mult))
                    link(dve.tensor_reduce(mw, gtmp, AX.X, ALU.max))
                    link(tt(dst, gtmp, wide(mw), ALU.is_equal))

                dve.wait_ge(route_mm, l + 1)
                link(dve.tensor_copy(rl, bank[7][:, 0:20 * NT].rearrange("p (t n) -> p t n", t=NT)))
                lg = rl[:, :, 0:NG]
                link(dve.tensor_reduce(mx, lg, AX.X, ALU.max))
                tt(gd, lg, wide(mx), ALU.subtract).then_inc(d_up, 1)
                first_of(gsel, lg, mx)
                experts = rl[:, :, NG:20].rearrange("p t (g j) -> p t g j", g=NG)
                link(tt(les_in, experts, gsel.unsqueeze(3).broadcast_to([P, NT, NG, EPG]), ALU.mult))
                link(dve.tensor_reduce(ls, les_in.rearrange("p t g j -> p t j g"), AX.X, ALU.add))
                link(dve.tensor_reduce(m1, ls, AX.X, ALU.max))
                first_of(oh1, ls, m1)
                link(stt(gm, oh1, -1e30, ls, ALU.mult, ALU.add))
                link(dve.tensor_reduce(m2, gm, AX.X, ALU.max))
                first_of(oh2, gm, m2)
                tt(p1e, m2, m1, ALU.subtract).then_inc(d_up, 1)
                dve.wait_ge(gexp_up, l + 1)
                link(dve.tensor_reduce(s_g, ge, AX.X, ALU.add))
                dve.wait_ge(e2_up, l + 1)
                link(ts(den, e2, 1.0, None, ALU.add))
                link(tt(den, den, s_g, ALU.mult))
                link(dve.reciprocal(p1, den))
                link(tt(p2, p1, e2, ALU.mult))
                mark(tt(oh1, oh1, wide(p1), ALU.mult))
                link(tt(oh2, oh2, wide(p2), ALU.mult))
                link(tt(oh1, oh1, oh2, ALU.add))
                tt(gt.rearrange("p t (g j) -> p t g j", g=NG), gsel.unsqueeze(3).broadcast_to([P, NT, NG, EPG]),
                   oh1.unsqueeze(2).broadcast_to([P, NT, NG, EPG]), ALU.mult).then_inc(gate_up, 1)
                dve.wait_ge(gatet_mm, l + 1)
                dve.tensor_copy(gate_t[0:NE, :], bank[7][0:NE, 0:T]).then_inc(gatet_cp, 1)

            def experts(l):
                for e in range(NE):
                    for f in range(2):
                        un = 2 * e + f
                        n = 2 * NE * l + un
                        dve.wait_ge(silu_up, n + 1)
                        tt(silu[:, un % 2, :], silu[:, un % 2, :], bank[2 * (un % 3) + 1][:, 0:T], ALU.mult).then_inc(h3_used, 1)
                        dve.wait_ge(h3_used, n + 1)
                        dve.wait_ge(gateb_cp, NE * l + e + 1)
                        tt(hid[:, un, :], silu[:, un % 2, :], gate_b[:, e % 2, :], ALU.mult).then_inc(hid_up, 1)

            for l in range(DEPTH):
                dve.wait_ge(mod_mm, N_MOD * (l + 1))
                dve.wait_ge(head_cp, 8)
                link(tt(mod[:, :, :], bank[7][:, 0:96].rearrange("p (m s) -> p m s", s=2),
                        par[:, l, 0:48].unsqueeze(2).broadcast_to([P, 48, 2]), ALU.add))
                for which in range(2):
                    lo = 24 * which
                    mark(ts(mod[:, lo + 8:lo + 16, :], mod[:, lo + 8:lo + 16, :], 1.0, None, ALU.add))
                    mark(ts(mod[:, lo + 16:lo + 24, :], mod[:, lo + 16:lo + 24, :], 1.0 / ALPHA, None, ALU.mult))
                link(ts(one_less_ka[:, :], par[:, l, KAP:KAP + NJ], -1.0, 1.0, ALU.mult, ALU.add))
                modulate(l, 0)
                front(l)
                attention(l)
                for j in range(NJ):
                    dve.wait_ge(bonus_mm, NJ * l + j + 1)
                    dve.wait_ge(front_cp, FRONT * (l + 1))
                    tt(v_t[:, j, :], v_t[:, j, :], bank[j][:, 0:T], ALU.mult).then_inc(bonus_up, 1)
                dve.wait_ge(poolw_cp, 2 * (l + 1))
                dve.wait_ge(v_out, 16 * (l + 1))
                dve.wait_ge(k_out, 16 * (l + 1))
                for s in range(3):
                    rwkv_step(l, s)
                heads_norm(l)
                for c in range(KT):
                    dve.wait_ge(proj_mm, KT * l + c + 1)
                    residual(l, c, 16, bank[c % 4], z_up)
                norm(l, 0)
                modulate(l, 1)
                route(l)
                experts(l)
                for c in range(KT):
                    dve.wait_ge(down_mm, KT * l + c + 1)
                    residual(l, c, 40, bank[c % 4], z2_up)
                norm(l, 1)


INPUTS = ("x_prompt", "x_sample", "state_rwkv", "cache_k", "cache_v", "c", "c_ctx", "w_in", "w_out", "w_mod", "b_mod",
          "ln1_g", "ln1_b", "ln2_g", "ln2_b", "rw_w0", "rw_w2", "rw_a0", "rw_a2", "rw_g2", "rw_kk", "rw_ka", "rw_rk",
          "rw_gn_g", "rw_gn_b", "q_norm", "k_norm", "pool_w", "pool_scale", "rt_grp_w", "rt_grp_b", "rt_exp_w",
          "rt_exp_b", "moe_w1", "moe_w3", "moe_w2")
OUTPUTS = ((1, SEQ, D), (1, DEC, D), (1, DEPTH, 2, AH, HD, HD), (1, DEPTH, SEQ, KVH, HD), (1, DEPTH, SEQ, KVH, HD))


def kernel(**inputs):
    import concourse.bacc as bacc
    from concourse.bass_utils import run_bass_kernel_spmd

    nc = bacc.Bacc("TRN2", target_bir_lowering=False, num_devices=1)
    arrays = {name: np.ascontiguousarray(inputs[name]) for name in INPUTS}
    arrays.update(constants())
    aps = {name: nc.dram_tensor(f"in_{name}", v.shape, mybir.dt.from_np(v.dtype), kind="ExternalInput").ap()
           for name, v in arrays.items()}
    outs = [nc.dram_tensor(f"out_{i}", shape, F32, kind="ExternalOutput").ap() for i, shape in enumerate(OUTPUTS)]
    build(nc, aps, outs)
    r = run_bass_kernel_spmd(nc, [{f"in_{name}": v for name, v in arrays.items()}], core_ids=[0])
    return tuple(r.results[0][f"out_{i}"] for i in range(len(OUTPUTS)))
```

```python
from contextlib import ExitStack

import numpy as np

import concourse.bass as bass
from concourse import mybir

ALU = mybir.AluOpType
ACT = mybir.ActivationFunctionType
AX = mybir.AxisListType
F32 = mybir.dt.float32
U8 = mybir.dt.uint8

P = 128
DEPTH = 2
D = 1024
KT = D // P
SEQ, DEC = 128, 256
T = SEQ + DEC
NT = T // P
GRID_W = 64
HD = 64
AH = 6
NJ = AH // 2
KVH = 2
GRP = 3
POOL_WINDOWS = (2, 4, 8, 16)
NG, EPG = 4, 4
NE = NG * EPG
DE = 256
ALPHA = (2 * DEPTH) ** 0.25
DECAY = 0.606531
LN_EPS, GN_EPS, QK_EPS = 1e-5, 64e-5, 1e-6
LEVELS = 7
STREAMS = ((0, SEQ), (SEQ, T))

BMOD, LN1G, LN1B, LN2G, LN2B = 0, 48, 56, 64, 72
W0, A0, KKP, KAP, RKP, GNG, GNB, PSC, QN, KN, COND, NPAR = 80, 86, 92, 95, 98, 101, 104, 107, 109, 110, 111, 127

RING = 3
SLOT = 4096
IN_COLS = ((1536, 512), (2048, 384), (768, 384), (1152, 384), (0, 384), (384, 384))
OUT_TILES = (3, 3, 2)
N_MOD = 12
JOBS = NG + 2
OVER = NG
JOB_ITEMS = EPG + 2
ORDER = [("mod", 0, i) for i in range(N_MOD)]
for _l in range(DEPTH):
    ORDER += [("in", _l, i) for i in range(len(IN_COLS))]
    ORDER += [("mod", _l + 1, i) for i in range(N_MOD)] if _l + 1 < DEPTH else []
    ORDER += [("out", _l, i) for i in range(len(OUT_TILES))]
    ORDER += [("job", _l, i) for i in range(JOBS * JOB_ITEMS)]
PLACE = {item: n for n, item in enumerate(ORDER)}

N_PAR_DMAS = 19
CTILE = 32
FRONT = 19 + 12 + 4 + NJ + NJ
SMALL = 14


def item_dmas(item):
    kind, _, i = item
    return 4 if kind == "out" else 7 if kind == "in" and i == 0 else 2


def landed_value(n):
    return sum(16 * item_dmas(ORDER[m]) for m in range(n % RING, n + 1, RING))


def constants():
    f = np.float32
    ident = np.eye(P, dtype=f)
    ones_d = np.full((P, P), 1.0 / D, f)
    head_ones = np.kron(np.eye(2), np.ones((HD, HD))).astype(f)
    rot = np.zeros((P, P), f)
    for c in range(P):
        i = c % 32
        if i < 16:
            rot[c + 16, c] = -1.0
        else:
            rot[c - 16, c] = 1.0
    n = HD // 4
    inv = (1.0 / (10000.0 ** (np.arange(n, dtype=f) / n))).astype(f)
    t = np.arange(DEC)
    pos = np.stack([(t // GRID_W).astype(f), (t % GRID_W).astype(f)])
    rope = np.zeros((P, 2, DEC), f)
    for c in range(P):
        ang = pos[(c % HD) // 32] * inv[c % 16]
        rope[c, 0], rope[c, 1] = np.cos(ang), np.sin(ang)

    def band(length):
        out = np.zeros((4, length, length), f)
        tt = np.arange(length)
        for g, w in enumerate(POOL_WINDOWS):
            lo, hi = np.clip(tt - w // 2, 0, length), np.clip(tt + w // 2, 0, length)
            s = np.arange(length)[:, None]
            out[g] = ((s >= lo) & (s < hi)) / (hi - lo).astype(f)
            out[g] -= np.eye(length, dtype=f)
        return out

    band_p = band(SEQ).transpose(1, 0, 2)
    band_s = band(DEC).reshape(4, 2, P, DEC).transpose(2, 0, 1, 3).reshape(P, 8, DEC)
    s, tt = np.arange(P)[:, None], np.arange(P)[None, :]
    strict = np.stack([s < tt, s > tt], 1).astype(f)
    incl = np.stack([s <= tt, s >= tt], 1).astype(f)
    level = np.zeros((P, LEVELS, 3, P), f)
    for k in range(LEVELS):
        b = 1 << k
        low = (s // (2 * b) == tt // (2 * b)) & ((s // b) % 2 == 1) & ((tt // b) % 2 == 0)
        level[:, k, 0], level[:, k, 1], level[:, k, 2] = low, low.T, low
    slots = np.tile(np.arange(P, dtype=f), (P, 1))
    first = np.tile(np.arange(4, 0, -1, dtype=f), (P, NT, 1))
    mats = np.concatenate([ident, ones_d, head_ones, rot, rope.reshape(P, -1), strict.reshape(P, -1),
                           incl.reshape(P, -1), first.reshape(P, -1), slots], 1)
    bands = np.concatenate([band_p.reshape(P, -1), band_s.reshape(P, -1)], 1)
    return {"mats": np.ascontiguousarray(mats), "bands": np.ascontiguousarray(bands),
            "level": np.ascontiguousarray(level.reshape(P, -1))}


def build(nc, a, out):
    y_prompt, y_sample, new_state, new_k, new_v = out
    with ExitStack() as ctx:
        def sb(name, shape, dt=F32):
            return ctx.enter_context(nc.sbuf_tensor(name, shape, dt))

        def sem(name):
            return ctx.enter_context(nc.semaphore(name))

        bank = [ctx.enter_context(nc.psum_tensor(f"bank{i}", [P, 512], F32)) for i in range(8)]

        n_mats = a["mats"].shape[1]
        cst = sb("cst", [P, n_mats])
        at = [0]

        def const(n):
            at[0] += n
            return cst[:, at[0] - n:at[0]]

        ident, ones_d, head_ones, rot = const(P), const(P), const(P), const(P)
        rope_cos, rope_sin = const(DEC), const(DEC)
        strict = const(2 * P).rearrange("p (d n) -> p d n", d=2)
        incl = const(2 * P).rearrange("p (d n) -> p d n", d=2)
        first = const(NT * 4).rearrange("p (t n) -> p t n", t=NT)
        slots = const(P)
        lev = sb("lev", [P, LEVELS, 3, P], U8)
        ones_row = sb("ones_row", [1, P])
        eps = sb("eps", [P, 3])

        h = sb("h", [P, KT, T])
        u = sb("u", [P, KT, T])
        mixed = u
        ring = sb("ring", [P, RING, SLOT])
        par = sb("par", [P, DEPTH, NPAR])
        cond = sb("cond", [P, KT, CTILE])
        mod = sb("mod", [P, 48, 2])
        mod_raw = sb("mod_raw", [P, 48, 2])
        plan = sb("plan", [1, 4], mybir.dt.int32)
        one_less_ka = sb("one_less_ka", [P, NJ])
        lora_w2 = sb("lora_w2", [P, NJ * P])
        lora_a2 = sb("lora_a2", [P, NJ * P])
        lora_g2 = sb("lora_g2", [P, NJ * P])
        pool_w = sb("pool_w", [P, 2, HD])
        route_w = sb("route_w", [P, KT, 20])
        route_b = sb("route_b", [1, 20])
        ctx_k = sb("ctx_k", [P, P])
        ctx_v = sb("ctx_v", [P, P])
        state_nat = sb("state_nat", [P, NJ, 2, P])

        REGION = 28300
        region = sb("region", [P, REGION])
        off = [0]

        def view(*shape):
            n = int(np.prod(shape))
            v = region[:, off[0]:off[0] + n]
            off[0] += n
            assert off[0] <= REGION, off[0]
            if len(shape) == 2:
                v = v.rearrange("p (a b) -> p a b", a=shape[0])
            if len(shape) == 3:
                v = v.rearrange("p (a b c) -> p a b c", a=shape[0], b=shape[1])
            return v

        r_t = view(NJ, T)
        kk_t = view(NJ, T)
        v_t = view(NJ, T)
        kd_t = view(2, NJ, T)
        b_t = view(2, NJ, T)
        run = view(2 * NJ * NT, P + 1)
        lo_g = view(T)
        v_tok = view(NT, NJ * P)
        y_t = view(NJ, T)
        centre = view(2 * NJ * NT)
        edge = view(2 * NJ * NT)
        shared = off[0]
        x_m = view(NJ, 4, P)
        xt_m = view(NJ, 4, P)
        at_m = view(NJ, 4, P)
        t_m = view(NJ, 4, P)
        scaled = view(4, NJ, 2 * P)
        tok_m = view(2, NJ, 2 * P)
        lmasks = view(3, 4, P)
        masks_of = (lmasks, at_m, t_m)
        r_s = view(2 * P)
        sa_s = view(2 * P)
        mod_row = view(P)
        s_t = view(NJ, 2, P)
        s_hat = view(NJ, 2, P)
        s_new = view(2, P)
        off[0] = shared
        k_t = view(NJ, T)
        lo_w = view(T)
        lo_a = view(T)
        qk = view(4, T)
        qk_s = view(4, T)
        rs = view(4, T)
        kr = view(NJ, T)
        vp = view(NT, T)
        ckt = view(P)
        kh_out = view(P)
        stat = view(3, 18)
        pool_d = view(2, T)
        bands = view(4 * SEQ + 8 * DEC)
        band_p = bands[:, 0:4 * SEQ].rearrange("p (g n) -> p g n", g=4)
        band_s = bands[:, 4 * SEQ:].rearrange("p (g n) -> p g n", g=8)
        rate = view(2, NJ, T)
        prob = qk_s[:, 0:2, :]
        prob_t = qk_s[:, 2:4, :]
        off[0] = shared
        gn_s = view(NJ, T)
        gn_r = view(NJ, T)
        off[0] = 0
        sq = view(KT, T)
        rstd = view(T)
        u_tok = view(NT, D)
        sel = view(2, NT, P)
        sel_t = view(2, T)
        xs = view(2, KT, P)
        silu = view(2, DE)
        hs = view(2, DE)
        hid = view(2, 2 * EPG, P)
        ys = view(D)
        gates = view(2, EPG)
        rl = view(NT, 20)
        g4 = [view(NT, 4) for _ in range(9)]
        g1 = [view(NT) for _ in range(17)]
        les_in = view(NT, 4, 4)
        group_1h, codes, inner, over_codes = view(NT, 4), view(NT, 4), view(NT, 4), view(NT, 2)
        rank_s = view(16)
        row4 = [view(4) for _ in range(6)]
        off[0] = 0
        x_in = view(NT, D)
        rows = view(DEPTH, P)
        level = view(LEVELS * 3 * P)
        off[0] = 0
        y_out = view(NT, D)
        state_out = sb("state_out", [P, NJ, 2, P])

        cst_in, x_in_s, par_in, small_in = sem("cst_in"), sem("x_in"), sem("par_in"), sem("small_in")
        level_in = sem("level_in")
        slot_in = [sem(f"slot_in{i}") for i in range(RING)]
        k_out, v_out, s_out, y_out_s = sem("k_out"), sem("v_out"), sem("s_out"), sem("y_out_s")
        bands_in = sem("bands_in")
        head_mm = sem("head_mm")
        mod_mm = sem("mod_mm")
        front_mm = sem("front_mm")
        khead_mm, rot_mm, ckt_mm = sem("khead_mm"), sem("rot_mm"), sem("ckt_mm")
        score_mm, pt_mm, o_mm = sem("score_mm"), sem("pt_mm"), sem("o_mm")
        pool_mm, poolw_mm, bonus_mm = sem("pool_mm"), sem("poolw_mm"), sem("bonus_mm")
        st_mm, tok_mm, inv_mm, t_mm, x_mm = sem("st_mm"), sem("tok_mm"), sem("inv_mm"), sem("t_mm"), sem("x_mm")
        msc_mm, rhs_mm, sa_mm, ys_mm = sem("msc_mm"), sem("rhs_mm"), sem("sa_mm"), sem("ys_mm")
        so_mm, gn_mm, g_mm = sem("so_mm"), sem("gn_mm"), sem("g_mm")
        proj_mm, ln_mm = sem("proj_mm"), sem("ln_mm")
        modt_mm = sem("modt_mm")
        route_mm, utok_mm, rank_mm, hid_mm, down_mm = (sem("route_mm"), sem("utok_mm"), sem("rank_mm"),
                                                       sem("hid_mm"), sem("down_mm"))
        xg_mm, misc_mm, ht_mm, un_mm = sem("xg_mm"), sem("misc_mm"), sem("ht_mm"), sem("un_mm")
        tail_mm = sem("tail_mm")
        head_cp, cond_up, front_cp = sem("head_cp"), sem("cond_up"), sem("front_cp")
        kh_cp, ckt_cp, prob_up, pt_cp, o_cp = sem("kh_cp"), sem("ckt_cp"), sem("prob_up"), sem("pt_cp"), sem("o_cp")
        pool_cp, poolw_cp = sem("pool_cp"), sem("poolw_cp")
        edge_up, exp_up, st_cp, tok_cp, t_cp = sem("edge_up"), sem("exp_up"), sem("st_cp"), sem("tok_cp"), sem("t_cp")
        rhs_cp, sa_cp, so_cp = sem("rhs_cp"), sem("sa_cp"), sem("so_cp")
        gn_rt, gn_sq, ln_sq, ln_rt = sem("gn_rt"), sem("gn_sq"), sem("ln_sq"), sem("ln_rt")
        modr_cp, modt_cp = sem("modr_cp"), sem("modt_cp")
        gexp_up, e2_up, utok_cp, silu_up = sem("gexp_up"), sem("e2_up"), sem("utok_cp"), sem("silu_up")
        xg_cp, misc_cp, ht_cp, ys_cp = sem("xg_cp"), sem("misc_cp"), sem("ht_cp"), sem("ys_cp")
        tail_cp = sem("tail_cp")
        vec_step = sem("vec_step")
        set_up, mod_up, u_up = sem("set_up"), sem("mod_up"), sem("u_up")
        qk_sq, kk_sq, qk_up, qkr_up, max_up, pn_up = (sem("qk_sq"), sem("kk_sq"), sem("qk_up"), sem("qkr_up"),
                                                      sem("max_up"), sem("pn_up"))
        rates_up, bonus_in, bonus_up = sem("rates_up"), sem("bonus_in"), sem("bonus_up")
        scaled_up, at_up, x_up, shat_up = sem("scaled_up"), sem("at_up"), sem("x_up"), sem("shat_up")
        msc_up, ys_up, state_up = sem("msc_up"), sem("ys_up"), sem("state_up")
        gn_c, mixa_up, z_up, xc_up = sem("gn_c"), sem("mixa_up"), sem("z_up"), sem("xc_up")
        d_up, onehot_up, sel_up, plan_up, hid_up, z2_up, h_up = (
            sem("d_up"), sem("onehot_up"), sem("sel_up"), sem("plan_up"), sem("hid_up"), sem("z2_up"), sem("h_up"))
        x_init = sem("x_init")

        def tiles(s):
            return ((0, 0), (1, 2), (2, 1))[s]

        def tc(t):
            return slice(t * P, (t + 1) * P)

        def both(m):
            return m.unsqueeze(2).broadcast_to([P, 2, 2, P])

        def n_par(l):
            return NPAR if l == 0 else COND

        def quad(ap):
            return ap.rearrange("p (d e) n -> p d e n", d=2)

        def bank4(b):
            return bank[b][:, :].rearrange("p (q n) -> p q n", q=4)

        XL = 2 * NJ * (LEVELS - 2) + NJ

        def xi(l, s, k, j, which):
            base = (l * 3 + s) * XL
            if k < LEVELS - 1:
                return base + (k - 1) * 2 * NJ + 2 * j + which + 1
            return base + (LEVELS - 2) * 2 * NJ + j + 1

        def used(n):
            kind, l, i = ORDER[n]
            if kind == "mod":
                return mod_mm, N_MOD * l + i + 1
            if kind == "in":
                return front_mm, FRONT * l + 3 * (i + 1) + 1
            if kind == "out":
                return proj_mm, KT * l + sum(OUT_TILES[:i + 1])
            job, i = divmod(i, JOB_ITEMS)
            jn = JOBS * l + job
            return (hid_mm, EPG * jn + i + 1) if i < EPG else (down_mm, 2 * jn + i - EPG + 1)

        def skip(eng, jn, per_job):
            for s, per in per_job:
                eng.wait_ge(s, per * jn)
                eng.sem_inc(s, per)

        block = ctx.enter_context(nc.Block())

        @block.sync
        def _(sp):
            def item(n, first_expert=None):
                kind, l, i = ORDER[n]
                slot = n % RING
                if n >= RING:
                    sp.wait_ge(*used(n - RING))
                w = ring[:, slot, :]
                landed = slot_in[slot]

                def halves(dst, src):
                    k = dst.shape[1] // 2
                    sp.dma_start(dst[:, 0:k], src[:, 0:k]).then_inc(landed, 16)
                    sp.dma_start(dst[:, k:2 * k], src[:, k:2 * k]).then_inc(landed, 16)

                if kind == "mod":
                    halves(w.rearrange("p (c n) -> p c n", c=KT),
                           a["w_mod"][l].rearrange("(c p) n -> p c n", p=P)[:, :, i * 512:(i + 1) * 512])
                elif kind == "in" and i == 0:
                    lo, n_cols = IN_COLS[0]
                    dst = w.rearrange("p (c n) -> p c n", c=KT)
                    src = a["w_in"][l].rearrange("(c p) n -> p c n", p=P)[:, :, lo:lo + n_cols]
                    for hq in range(GRP * KVH):
                        to = P * (hq % GRP) + HD * (hq // GRP)
                        sp.dma_start(dst[:, :, to:to + HD], src[:, :, hq * HD:(hq + 1) * HD]).then_inc(landed, 16)
                    sp.dma_start(dst[:, :, T:n_cols], src[:, :, T:n_cols]).then_inc(landed, 16)
                elif kind == "in":
                    lo, n_cols = IN_COLS[i]
                    halves(w[:, 0:KT * n_cols].rearrange("p (c n) -> p c n", c=KT),
                           a["w_in"][l].rearrange("(c p) n -> p c n", p=P)[:, :, lo:lo + n_cols])
                elif kind == "out":
                    lo = P * sum(OUT_TILES[:i])
                    n_cols = P * OUT_TILES[i]
                    dst = w[:, 0:KT * n_cols].rearrange("p (c n) -> p c n", c=KT)
                    src = a["w_out"][l][:, lo:lo + n_cols]
                    sp.dma_start(dst[:, 0:NJ], src[0:NJ * P].rearrange("(c p) n -> p c n", p=P)).then_inc(landed, 16)
                    for g in range(KVH):
                        lo_r = NJ * P + g * GRP * HD
                        sp.dma_start(dst[g * HD:(g + 1) * HD, NJ:2 * NJ],
                                     src[lo_r:lo_r + GRP * HD].rearrange("(c p) n -> p c n", p=HD)).then_inc(landed, 16)
                    sp.dma_start(dst[:, 2 * NJ:KT],
                                 src[2 * NJ * P:D].rearrange("(c p) n -> p c n", p=P)).then_inc(landed, 16)
                else:
                    job, m = divmod(i, JOB_ITEMS)
                    e0 = EPG * job if first_expert is None else first_expert
                    if m < EPG:
                        dst = w.rearrange("p (c n) -> p c n", c=KT)
                        for half, name in enumerate(("moe_w1", "moe_w3")):
                            sp.dma_start(dst[:, :, half * DE:(half + 1) * DE],
                                         expert(name, l, e0 + m).rearrange("(c p) n -> p c n", p=P)).then_inc(landed, 16)
                    else:
                        for k in range(2):
                            sp.dma_start(w[:, 2048 * k:2048 * (k + 1)].rearrange("p (f n) -> p f n", f=2),
                                         expert("moe_w2", l, e0 + 2 * (m - EPG) + k).rearrange("(f p) n -> p f n", p=P)
                                         ).then_inc(landed, 16)

            def expert(name, l, e):
                if isinstance(e, int):
                    return a[name][l, e]
                return a[name][l, bass.ds(e, 1)].rearrange("o r n -> (o r) n")

            n = 0
            while n < len(ORDER):
                kind, l, i = ORDER[n]
                if kind != "job" or i < OVER * JOB_ITEMS:
                    item(n)
                    n += 1
                    continue
                over = i // JOB_ITEMS - OVER
                if over == 0:
                    sp.wait_ge(plan_up, l + 1)
                count = sp.value_load(plan[0:1, 0:1], min_val=0, max_val=2)
                with sp.If(count > over):
                    e0 = sp.value_load(plan[0:1, 1 + over:2 + over], min_val=0, max_val=NE - EPG)
                    for m in range(JOB_ITEMS):
                        item(n + m, e0)
                with sp.Else():
                    for m in range(JOB_ITEMS):
                        slot = slot_in[(n + m) % RING]
                        sp.wait_ge(slot, landed_value(n + m - RING))
                        sp.sem_inc(slot, landed_value(n + m) - landed_value(n + m - RING))
                n += JOB_ITEMS

        @block.gpsimd
        def _(pool):
            pool.dma_start(level, a["level"]).then_inc(level_in, 16)
            for l in range(DEPTH):
                if l > 0:
                    pool.wait_ge(route_mm, l)
                    pool.wait_ge(st_mm, 2 * l)
                for dst, name in ((lora_w2, "rw_w2"), (lora_a2, "rw_a2")):
                    pool.dma_start(dst[:, :], a[name][l].rearrange("d r c -> (d r) c")).then_inc(small_in, 16)
                pool.dma_start(lora_g2[:, :], a["rw_g2"][l]).then_inc(small_in, 16)
                pool.dma_start(pool_w[:, :, :],
                               a["pool_w"][l].rearrange("(t g) c d -> t (g c) d", t=2).rearrange("t p d -> p t d")
                               ).then_inc(small_in, 16)
                pool.dma_start(route_w[:, :, 0:NG], a["rt_grp_w"][l].rearrange("(c p) n -> p c n", p=P)).then_inc(small_in, 16)
                pool.dma_start(route_w[:, :, NG:20], a["rt_exp_w"][l].rearrange("(c p) n -> p c n", p=P)).then_inc(small_in, 16)
                pool.dma_start(route_b[:, 0:NG], a["rt_grp_b"][l:l + 1, :]).then_inc(small_in, 16)
                pool.dma_start(route_b[:, NG:20], a["rt_exp_b"][l:l + 1, :]).then_inc(small_in, 16)
                pool.dma_start(ctx_k[:, :], a["cache_k"][0, l].rearrange("t h c -> t (h c)")).then_inc(small_in, 16)
                pool.dma_start(ctx_v[:, :], a["cache_v"][0, l].rearrange("t h c -> t (h c)")).then_inc(small_in, 16)
                if l == 0:
                    pool.wait_ge(set_up, 1)
                for d in range(2):
                    for e in range(2):
                        src = a["state_rwkv"][0, l, d].rearrange("(j e) v k -> e v j k", e=2)[e]
                        pool.dma_start(state_nat[e * HD:(e + 1) * HD, :, d, e * HD:(e + 1) * HD], src).then_inc(small_in, 16)
                pool.wait_ge(u_up, 2 * KT * l + KT)
                pool.dma_start(bands, a["bands"]).then_inc(bands_in, 16)
                pool.wait_ge(front_cp, FRONT * l + 5)
                pool.dma_start(new_v[0, l].rearrange("t h c -> t (h c)"), vp[:, 0, 0:P]).then_inc(v_out, 16)
                pool.wait_ge(kh_cp, l + 1)
                pool.dma_start(new_k[0, l].rearrange("t h c -> t (h c)"), kh_out).then_inc(k_out, 16)
                for s in range(3):
                    n = l * 3 + s
                    if s == 0:
                        pool.wait_ge(poolw_cp, 2 * (l + 1))
                        pool.wait_ge(bonus_up, NJ * (l + 1))
                        pool.wait_ge(v_out, 16 * (l + 1))
                        pool.wait_ge(k_out, 16 * (l + 1))
                    else:
                        pool.wait_ge(t_mm, NJ * (LEVELS - 1) * n)
                    for m in (x_m, xt_m):
                        for j in range(NJ):
                            if s > 0 and m is xt_m:
                                pool.wait_ge(sa_mm, NJ * (n - 1) + j + 1)
                            pool.tensor_copy(m[:, j], ident.unsqueeze(1).broadcast_to([P, 4, P])).then_inc(x_init, 1)
                pool.wait_ge(so_cp, 2 * (l + 1))
                for d in range(2):
                    for e in range(2):
                        dst = new_state[0, l, d].rearrange("(j e) v k -> e v j k", e=2)[e]
                        pool.dma_start(dst, state_out[e * HD:(e + 1) * HD, :, d, e * HD:(e + 1) * HD]).then_inc(s_out, 16)
            for t in range(NT):
                pool.wait_ge(tail_cp, 2 * (t + 1))
                dst = y_prompt[0] if t == 0 else y_sample[0, (t - 1) * P:t * P]
                pool.dma_start(dst, y_out[:, t, :]).then_inc(y_out_s, 16)
            pool.wait_ge(v_out, 16 * DEPTH)
            pool.wait_ge(k_out, 16 * DEPTH)
            pool.wait_ge(s_out, 64 * DEPTH)
            pool.wait_ge(y_out_s, 16 * NT)

        @block.tensor
        def _(pe):
            def item_in(kind, l, i):
                n = PLACE[kind, l, i]
                pe.wait_ge(slot_in[n % RING], landed_value(n))
                return ring[:, n % RING, :]

            def attention(l):
                def unit(i):
                    return i // AH, i % AH

                def scores(i):
                    t, hq = unit(i)
                    j, g = hq % GRP, hq // GRP
                    n = 18 * l + i
                    if i >= 2:
                        pe.wait_ge(prob_up, n - 1)
                        pe.wait_ge(max_up, n - 1)
                    q = qk[g * HD:(g + 1) * HD, j, tc(t)]
                    if t == 0:
                        last = pe.matmul(bank[i % 2][:, 0:P], q, qk[g * HD:(g + 1) * HD, 3, 0:P], start=True, stop=True)
                    else:
                        pe.matmul(bank[i % 2][:, 0:DEC], q, qk[g * HD:(g + 1) * HD, 3, P:T], start=True, stop=True)
                        last = pe.matmul(bank[i % 2][:, DEC:T], q, ckt[g * HD:(g + 1) * HD, :], start=True, stop=True)
                    last.then_inc(score_mm, 1)

                def turn(i):
                    t, _ = unit(i)
                    n = 18 * l + i
                    pe.wait_ge(pn_up, n + 1)
                    if i >= 2:
                        pe.wait_ge(pt_cp, n - 1)
                    for c in range(1 if t == 0 else 3):
                        last = pe.transpose(bank[2 + i % 2][:, tc(c)], prob[:, i % 2, tc(c)], ident)
                    last.then_inc(pt_mm, 1)

                def outs(i):
                    t, hq = unit(i)
                    j, g = hq % GRP, hq // GRP
                    n = 18 * l + i
                    pe.wait_ge(pt_cp, n + 1)
                    dst = bank[4 + t][g * HD:(g + 1) * HD, tc(j)]
                    if t == 0:
                        values = [vp[:, 0, g * HD:(g + 1) * HD]]
                    else:
                        values = [vp[:, 1, g * HD:(g + 1) * HD], vp[:, 2, g * HD:(g + 1) * HD],
                                  ctx_v[:, g * HD:(g + 1) * HD]]
                    for c, vals in enumerate(values):
                        last = pe.matmul(dst, vals, prob_t[:, i % 2, tc(c)], start=(c == 0), stop=(c == len(values) - 1))
                    last.then_inc(o_mm, 1)

                pe.wait_ge(qkr_up, l + 1)
                pe.wait_ge(ckt_cp, l + 1)
                for i in range(18 + 2):
                    if i < 18:
                        scores(i)
                    if 1 <= i <= 18:
                        turn(i - 1)
                    if i >= 2:
                        outs(i - 2)

            def pooling(l):
                pe.wait_ge(o_cp, 3 * l + 3)
                pe.wait_ge(bands_in, 16 * (l + 1))
                for c in range(2):
                    for g in range(2):
                        dst = bank[6 + c][g * HD:(g + 1) * HD, :]
                        src = slice(P + (2 * c + g) * HD, P + (2 * c + g + 1) * HD)
                        pe.matmul(dst[:, 0:P], vp[:, 0, src], band_p[:, 2 * c + g, :], start=True, stop=True)
                        for k in range(2):
                            last = pe.matmul(dst[:, P:T], vp[:, 1 + k, src], band_s[:, 2 * (2 * c + g) + k, :],
                                             start=(k == 0), stop=(k == 1))
                    last.then_inc(pool_mm, 1)
                for c in range(2):
                    pe.wait_ge(pool_cp, 2 * l + c + 1)
                    for g in range(2):
                        rows_g = slice(g * HD, (g + 1) * HD)
                        last = pe.matmul(bank[6 + c][rows_g, 0:T], pool_w[rows_g, c, :], pool_d[rows_g, c, :],
                                         start=True, stop=True)
                    last.then_inc(poolw_mm, 1)

            def rwkv_step(l, s):
                n = l * 3 + s
                if s == 0:
                    pe.wait_ge(poolw_cp, 2 * (l + 1))
                if s == 1:
                    pe.wait_ge(so_cp, 2 * (l + 1))
                    for d2 in range(2):
                        for q in range(3):
                            jd = 3 * d2 + q
                            last = pe.transpose(bank[6 + d2][:, tc(q)], state_nat[:, jd // 2, jd % 2, :], ident)
                        last.then_inc(st_mm, 1)
                def tok(g):
                    if g >= 2:
                        pe.wait_ge(tok_cp, 4 * n + g - 1)
                    for q in range(4 if g % 2 == 0 else 2):
                        jd = 4 * (g % 2) + q
                        last = pe.transpose(bank[6 + g % 2][:, tc(q)], scaled[:, 2 + g // 2, jd // 2, tc(jd % 2)], ident)
                    last.then_inc(tok_mm, 1)

                pe.wait_ge(scaled_up, 2 * n + 1)
                for j in range(NJ):
                    if j == 2 and n > 0:
                        pe.wait_ge(ys_up, NJ * n)
                    for q in range(4):
                        d = q % 2
                        for e in range(2):
                            rows_e = slice(e * HD, (e + 1) * HD)
                            al, be = scaled[rows_e, 1, j, tc(d)], scaled[rows_e, 2, j, tc(d)]
                            lhs, rhs = (al, be) if q < 2 else (be, al)
                            last = pe.matmul(bank[2 * j + e][:, tc(q)], lhs, rhs, start=True, stop=True)
                            if q == 3:
                                last.then_inc(inv_mm, 1)
                if s == 1:
                    pe.wait_ge(st_cp, 2 * (l + 1))
                tok(0)
                tok(1)
                for k in range(1, LEVELS):
                    if k == 2:
                        pe.wait_ge(tok_cp, 4 * (n + 1))
                    if l + 1 < DEPTH and k >= 2:
                        if k <= 5:
                            mod_rows(l + 1, 4 * s + k - 2)
                        if k >= 3:
                            mod_turn(l + 1, 4 * s + k - 3)
                    for j in range(NJ):
                        if k == 1:
                            pe.wait_ge(at_up, NJ * (n + 1))
                        else:
                            pe.wait_ge(x_up, xi(l, s, k - 1, j, 1))
                        for q in range(4):
                            last = pe.matmul(bank[j][:, tc(q)], at_m[:, j, q, :], x_m[:, j, q, :], start=True, stop=True)
                        last.then_inc(t_mm, 1)
                    if k == 1:
                        tok(2)
                        tok(3)
                    for j in range(NJ):
                        pe.wait_ge(t_cp, ((l * 3 + s) * (LEVELS - 1) + k - 1) * NJ + j + 1)
                        if k < LEVELS - 1:
                            for q in range(4):
                                last = pe.matmul(bank[j][:, tc(q)], xt_m[:, j, q, :], t_m[:, j, q, :], start=True, stop=True)
                            last.then_inc(x_mm, 1)
                        for q in range(4):
                            last = pe.matmul(bank[3 + j][:, tc(q)], t_m[:, j, q, :], xt_m[:, j, q, :], start=True, stop=True)
                        last.then_inc(x_mm, 1)

                if l + 1 < DEPTH:
                    pe.wait_ge(modt_cp, N_MOD * (l + 1) + 4 * (s + 1))

                def masked(j):
                    if j == 0:
                        pe.wait_ge(scaled_up, 2 * n + 2)
                        pe.wait_ge(x_up, xi(l, s, LEVELS - 1, NJ - 1, 1))
                    else:
                        pe.wait_ge(msc_up, 3 * (NJ * n + j))
                    for m, (kl, kr_) in enumerate(((3, 1), (2, 0), (3, 0))):
                        for d in range(2):
                            for e in range(2):
                                rows_e = slice(e * HD, (e + 1) * HD)
                                last = pe.matmul(bank[2 * (m // 2) + e][:, tc(2 * (m % 2) + d)],
                                                 scaled[rows_e, kl, j, tc(d)], scaled[rows_e, kr_, j, tc(d)],
                                                 start=True, stop=True)
                                if d == 1:
                                    last.then_inc(msc_mm, 1)

                def rhs_of(j):
                    pe.wait_ge(msc_up, 3 * (NJ * n + j) + 1)
                    pe.wait_ge(shat_up, n + 1)
                    if n * NJ + j > 0:
                        pe.wait_ge(rhs_cp, NJ * n + j)
                    for d in range(2):
                        t = tiles(s)[d]
                        pe.matmul(bank[6][:, tc(d)], scaled[:, 1, j, tc(d)], s_hat[:, j, d, :], start=True, stop=False,
                                  skip_group_check=True)
                        for e in range(2):
                            col = slice(d * P + e * HD, d * P + (e + 1) * HD)
                            last = pe.matmul(bank[6][:, col], masks_of[j][:, 0, 2 * d + e, :],
                                             v_tok[:, t, j * P + e * HD:j * P + (e + 1) * HD], start=False, stop=True,
                                             skip_group_check=True)
                    last.then_inc(rhs_mm, 1)

                def solve(j):
                    pe.wait_ge(rhs_cp, NJ * n + j + 1)
                    if n * NJ + j > 0:
                        pe.wait_ge(sa_cp, NJ * n + j)
                    for q in range(4):
                        col = slice(q * HD, (q + 1) * HD)
                        last = pe.matmul(bank[7][:, col], xt_m[:, j, q, :], r_s[:, col], start=True, stop=True)
                    last.then_inc(sa_mm, 1)

                def outputs(j):
                    b = 4 + j % 2
                    pe.wait_ge(sa_cp, NJ * n + j + 1)
                    pe.wait_ge(msc_up, 3 * (NJ * n + j) + 3)
                    if j == 2:
                        pe.wait_ge(ys_up, NJ * n + 1)
                    for d in range(2):
                        t = tiles(s)[d]
                        pe.matmul(bank[b][:, tc(d)], s_hat[:, j, d, :], scaled[:, 0, j, tc(d)], start=True, stop=False,
                                  skip_group_check=True)
                        for e in range(2):
                            rows_e = slice(e * HD, (e + 1) * HD)
                            pe.matmul(bank[b][rows_e, tc(d)], sa_s[:, d * P + e * HD:d * P + (e + 1) * HD],
                                      masks_of[j][:, 1, 2 * d + e, :], start=False, stop=False, skip_group_check=True)
                            pe.matmul(bank[b][rows_e, tc(d)], v_tok[:, t, j * P + e * HD:j * P + (e + 1) * HD],
                                      masks_of[j][:, 2, 2 * d + e, :], start=False, stop=True, skip_group_check=True)
                        dst = bank[b][:, tc(2 + d)]
                        pe.matmul(dst, tok_m[:, 1, j, tc(d)], v_tok[:, t, tc(j)], start=True, stop=False,
                                  skip_group_check=True)
                        last = pe.matmul(dst, tok_m[:, 0, j, tc(d)], sa_s[:, tc(d)], start=False, stop=True,
                                         skip_group_check=True)
                    last.then_inc(ys_mm, 1)

                masked(0)
                rhs_of(0)
                masked(1)
                for j in range(NJ):
                    solve(j)
                    if j == 0:
                        masked(2)
                    if j + 1 < NJ:
                        rhs_of(j + 1)
                    outputs(j)
                if s == 0:
                    pe.wait_ge(state_up, NJ * n + NJ)
                    for d2 in range(2):
                        for q in range(3):
                            jd = 3 * d2 + q
                            last = pe.transpose(bank[6 + d2][:, tc(q)], s_t[:, jd // 2, jd % 2, :], ident)
                        last.then_inc(so_mm, 1)

            def mod_rows(l, i):
                m = N_MOD * l + i
                w = item_in("mod", l, i).rearrange("p (c n) -> p c n", c=KT)
                if m > 0:
                    pe.wait_ge(modr_cp, m)
                for c in range(KT):
                    for q in range(4):
                        last = pe.matmul(bank[6][CTILE * q:CTILE * (q + 1), 0:P], cond[:, c, :], w[:, c, tc(q)],
                                         start=(c == 0), stop=(c == KT - 1))
                last.then_inc(mod_mm, 1)

            def mod_turn(l, i):
                m = N_MOD * l + i
                pe.wait_ge(modr_cp, m + 1)
                if m > 0:
                    pe.wait_ge(modt_cp, m)
                pe.transpose(bank[7][:, 0:P], mod_row, ident).then_inc(modt_mm, 1)

            def norm_sums(l, which, ready, per):
                src = h if which == 0 else sq
                for c in range(KT):
                    pe.wait_ge(ready, per(c))
                    last = pe.matmul(bank[4 + which][:, 0:T], ones_d, src[:, c, :], start=(c == 0), stop=(c == KT - 1))
                last.then_inc(ln_mm, 1)

            pe.wait_ge(cst_in, 16)
            pe.wait_ge(par_in, 16 * N_PAR_DMAS)
            for l in range(DEPTH):
                pe.transpose(bank[l][:, 0:n_par(l)], rows[0:n_par(l), l, :],
                             ident[0:n_par(l), 0:n_par(l)]).then_inc(head_mm, 1)
            pe.wait_ge(x_in_s, 16 * NT)
            for t in range(NT):
                for half in range(2):
                    for q in range(4):
                        last = pe.transpose(bank[2 + 2 * t + half][:, tc(q)], x_in[:, t, tc(4 * half + q)], ident)
                    last.then_inc(head_mm, 1)

            for l in range(DEPTH):
                if l == 0:
                    pe.wait_ge(cond_up, 1)
                    pe.wait_ge(head_cp, 8)
                    for i in range(N_MOD + 1):
                        if i < N_MOD:
                            mod_rows(0, i)
                        if i >= 1:
                            mod_turn(0, i - 1)
                n_front = [0]

                def front_bank():
                    n = FRONT * l + n_front[0]
                    b = n_front[0] % 7
                    if n_front[0] >= 7:
                        pe.wait_ge(front_cp, n - 6)
                    n_front[0] += 1
                    return bank[b]

                for c in range(KT):
                    pe.wait_ge(u_up, 2 * KT * l + c + 1)
                for i in range(len(IN_COLS)):
                    n_cols = IN_COLS[i][1]
                    w = item_in("in", l, i)[:, 0:KT * n_cols].rearrange("p (c n) -> p c n", c=KT)
                    for m in range(4 if i == 0 else 3):
                        dst = front_bank()
                        for c in range(KT):
                            if i in (1, 2):
                                last_c = pe.matmul(dst[:, 0:n_cols], u[:, c, tc(m)], w[:, c, :],
                                                   start=(c == 0), stop=(c == KT - 1))
                            else:
                                last_c = pe.matmul(dst[:, 0:T], w[:, c, tc(m)], u[:, c, :],
                                                   start=(c == 0), stop=(c == KT - 1))
                        last_c.then_inc(front_mm, 1)
                pe.wait_ge(small_in, 16 * SMALL * (l + 1))
                for d in range(2):
                    for j in range(NJ):
                        for w2, lo in ((lora_w2, lo_w), (lora_a2, lo_a)):
                            dst = front_bank()
                            pe.wait_ge(front_cp, FRONT * l + 12)
                            pe.matmul(dst[:, 0:T], w2[d * HD:(d + 1) * HD, tc(j)], lo[d * HD:(d + 1) * HD, :],
                                      start=True, stop=True).then_inc(front_mm, 1)
                pe.wait_ge(qk_sq, l + 1)
                for m in range(4):
                    dst = front_bank()
                    pe.matmul(dst[:, 0:T], head_ones, qk_s[:, m, :], start=True, stop=True).then_inc(front_mm, 1)
                pe.wait_ge(kk_sq, l + 1)
                for j in range(NJ):
                    dst = front_bank()
                    pe.matmul(dst[:, 0:T], head_ones, kr[:, j, :], start=True, stop=True).then_inc(front_mm, 1)
                for j in range(NJ):
                    dst = front_bank()
                    for t in range(NT):
                        last = pe.transpose(dst[:, tc(t)], v_tok[:, t, tc(j)], ident)
                    last.then_inc(front_mm, 1)
                pe.wait_ge(front_cp, FRONT * (l + 1))
                pe.transpose(bank[0][:, 0:P], ctx_k[:, :], ident).then_inc(ckt_mm, 1)
                pe.wait_ge(qk_up, l + 1)
                pe.transpose(bank[1][:, 0:P], qk[:, 3, 0:P], ident).then_inc(khead_mm, 1)
                for m in range(4):
                    last = pe.matmul(bank[2 + m // 2][:, (m % 2) * DEC:(m % 2 + 1) * DEC], rot, qk[:, m, P:T],
                                     start=True, stop=True)
                    if m % 2:
                        last.then_inc(rot_mm, 1)
                pe.wait_ge(kh_cp, l + 1)
                attention(l)
                pooling(l)
                pe.wait_ge(bonus_in, l + 1)
                for j in range(NJ):
                    pe.matmul(bank[j][:, 0:T], head_ones, kr[:, j, :], start=True, stop=True).then_inc(bonus_mm, 1)
                pe.wait_ge(bonus_up, NJ * (l + 1))
                for s in range(3):
                    rwkv_step(l, s)
                pe.wait_ge(state_up, NJ * 3 * (l + 1))
                for j in range(NJ):
                    pe.matmul(bank[j][:, 0:T], head_ones, y_t[:, j, :], start=True, stop=True).then_inc(gn_mm, 1)
                for j in range(NJ):
                    pe.matmul(bank[3 + j][:, 0:T], lora_g2[:, tc(j)], lo_g, start=True, stop=True).then_inc(g_mm, 1)
                for j in range(NJ):
                    pe.wait_ge(gn_sq, NJ * l + j + 1)
                    pe.matmul(bank[j][:, 0:T], head_ones, gn_s[:, j, :], start=True, stop=True).then_inc(gn_mm, 1)
                pe.wait_ge(mixa_up, NJ * (l + 1))
                pe.wait_ge(poolw_cp, 2 * (l + 1))
                dt = 0
                for i in range(len(OUT_TILES)):
                    w = item_in("out", l, i)[:, 0:KT * P * OUT_TILES[i]].rearrange("p (c n) -> p c n", c=KT)
                    for m in range(OUT_TILES[i]):
                        if dt >= 4:
                            pe.wait_ge(z_up, KT * l + dt - 3)
                        for c in range(KT):
                            last = pe.matmul(bank[dt % 4][:, 0:T], w[:, c, tc(m)], mixed[:, c, :],
                                             start=(c == 0), stop=(c == KT - 1))
                        last.then_inc(proj_mm, 1)
                        dt += 1
                norm_sums(l, 0, z_up, lambda c: KT * l + c + 1)
                norm_sums(l, 1, ln_sq, lambda c: KT * (2 * l) + c + 1)
                for c in range(KT):
                    pe.wait_ge(u_up, 2 * KT * l + KT + c + 1)
                for t in range(NT):
                    dst = bank[7][:, t * 20:(t + 1) * 20]
                    for c in range(KT):
                        pe.matmul(dst, u[:, c, tc(t)], route_w[:, c, :], start=(c == 0), stop=False)
                    last = pe.matmul(dst, ones_row[:, :], route_b[:, :], start=False, stop=True)
                last.then_inc(route_mm, 1)

                for g in range(2 * NT):
                    t, half = g // 2, g % 2
                    for q in range(4):
                        last = pe.transpose(bank[g][:, tc(q)], u[:, 4 * half + q, tc(t)], ident)
                    last.then_inc(utok_mm, 1)
                pe.wait_ge(onehot_up, l + 1)
                for t in range(NT + 1):
                    dst = bank[6][:, 4 * t:4 * t + 4]
                    parts = [(strict[:, 0, :], t)] if t < NT else []
                    for before in range(t):
                        parts += [(incl[:, 0, :], before), (strict[:, 1, :], before)]
                    for i, (ones, of) in enumerate(parts):
                        last = pe.matmul(dst, ones, group_1h[:, of, :], start=(i == 0), stop=(i == len(parts) - 1))
                last.then_inc(rank_mm, 1)

                def prepare(job):
                    jn, b = JOBS * l + job, job % 2
                    pe.wait_ge(sel_up, jn + 1)
                    pe.wait_ge(z2_up, KT * (jn - 1 if job in (1, 2, 3) else jn))
                    for c in range(KT):
                        for t in range(NT):
                            last = pe.matmul(bank[2 + c // 4][:, tc(c % 4)], u_tok[:, t, tc(c)], sel[:, b, t, :],
                                             start=(t == 0), stop=(t == NT - 1))
                        if c % 4 == 3:
                            last.then_inc(xg_mm, 1)
                    pe.wait_ge(misc_cp, jn)
                    for t in range(NT):
                        pe.transpose(bank[7][:, tc(t)], sel[:, b, t, :], ident)
                    for t in range(NT):
                        last = pe.matmul(bank[7][:, T:T + EPG], sel[:, b, t, :], inner[:, t, :],
                                         start=(t == 0), stop=(t == NT - 1))
                    last.then_inc(misc_mm, 1)

                def hidden(job, j):
                    jn = JOBS * l + job
                    w = item_in("job", l, JOB_ITEMS * job + j).rearrange("p (c n) -> p c n", c=KT)
                    if j == 0:
                        pe.wait_ge(xg_cp, 2 * jn + 2)
                    if EPG * jn + j >= 2:
                        pe.wait_ge(hid_up, EPG * jn + j - 1)
                    for c in range(KT):
                        last = pe.matmul(bank[j % 2][:, :], xs[:, job % 2, c, :], w[:, c, :],
                                         start=(c == 0), stop=(c == KT - 1))
                    last.then_inc(hid_mm, 1)

                def turn(job, j):
                    n = EPG * (JOBS * l + job) + j
                    pe.wait_ge(hid_up, n + 1)
                    if n > 0:
                        pe.wait_ge(ht_cp, n)
                    for f in range(2):
                        last = pe.transpose(bank[4][:, tc(f)], hs[:, j % 2, tc(f)], ident)
                    last.then_inc(ht_mm, 1)

                def down(job):
                    jn = JOBS * l + job
                    pe.wait_ge(ys_cp, 2 * jn)
                    for pair in range(2):
                        w = item_in("job", l, JOB_ITEMS * job + EPG + pair).rearrange("p (f n) -> p f n", f=4)
                        pe.wait_ge(ht_cp, EPG * jn + 2 * pair + 2)
                        for f in range(4):
                            for half in range(2):
                                last = pe.matmul(bank[5 + half][:, :], hid[:, job % 2, 4 * pair + f, :],
                                                 w[:, f, 512 * half:512 * half + 512],
                                                 start=(pair == 0 and f == 0), stop=(pair == 1 and f == 3))
                        last.then_inc(down_mm, 1)

                def scatter(job, prepared):
                    jn = JOBS * l + job
                    pe.wait_ge(ys_cp, 2 * jn + 2)
                    pe.wait_ge(misc_cp, jn + 1)
                    pe.wait_ge(xg_cp, 2 * (JOBS * l + prepared))
                    for c in range(KT):
                        if c >= 2:
                            pe.wait_ge(z2_up, KT * jn + c - 1)
                        pe.matmul(bank[2 + c % 2][:, 0:T], ys[:, tc(c)], sel_t[:, job % 2, :],
                                  start=True, stop=True).then_inc(un_mm, 1)

                pe.wait_ge(utok_cp, 2 * NT * (l + 1))
                prepare(0)
                for job in range(NG):
                    hidden(job, 0)
                    if job > 0:
                        scatter(job - 1, job + 1)
                    for j in range(1, EPG):
                        hidden(job, j)
                        turn(job, j - 1)
                    if job + 1 < NG:
                        prepare(job + 1)
                    turn(job, EPG - 1)
                    down(job)
                scatter(NG - 1, NG)
                pe.wait_ge(plan_up, l + 1)
                count = pe.value_load(plan[0:1, 0:1], min_val=0, max_val=2)
                for over in range(2):
                    job = OVER + over
                    with pe.If(count > over):
                        prepare(job)
                        for j in range(EPG):
                            hidden(job, j)
                            turn(job, j)
                        down(job)
                        scatter(job, job + 1)
                    with pe.Else():
                        skip(pe, JOBS * l + job, ((xg_mm, 2), (misc_mm, 1), (hid_mm, EPG), (ht_mm, EPG),
                                                  (down_mm, 2), (un_mm, KT)))
                norm_sums(l, 0, z2_up, lambda c: KT * JOBS * (l + 1))
                norm_sums(l, 1, ln_sq, lambda c: KT * (2 * l + 1) + c + 1)
            pe.wait_ge(h_up, KT * 2 * DEPTH)
            for t in range(NT):
                for half in range(2):
                    for q in range(4):
                        last = pe.transpose(bank[2 * t + half][:, tc(q)], h[:, 4 * half + q, tc(t)], ident)
                    last.then_inc(tail_mm, 1)

        @block.scalar
        def _(act):
            def copy(dst, src):
                return act.activation(dst, src, ACT.Copy)

            def row(at_row, n, src, cols=P, to=0, layers=DEPTH):
                act.dma_start(rows[at_row:at_row + n, 0:layers, to:to + cols],
                              src.rearrange("l (a b) -> a l b", b=cols)).then_inc(par_in, 16)

            act.dma_start(cst[:, :], a["mats"]).then_inc(cst_in, 16)
            for s, name in enumerate(("c_ctx", "c")):
                src = a[name].rearrange("(k p) -> k p", p=P) if s == 0 else a[name][0].rearrange("(k p) -> k p", p=P)
                act.dma_start(rows[COND + KT * s:COND + KT * (s + 1), 0, :], src).then_inc(par_in, 16)
            row(BMOD, 48, a["b_mod"])
            for at_row, name in ((LN1G, "ln1_g"), (LN1B, "ln1_b"), (LN2G, "ln2_g"), (LN2B, "ln2_b")):
                row(at_row, KT, a[name])
            row(W0, 6, a["rw_w0"].rearrange("l d c -> l (d c)"))
            row(A0, 6, a["rw_a0"].rearrange("l d c -> l (d c)"))
            row(KKP, NJ, a["rw_kk"])
            row(KAP, NJ, a["rw_ka"])
            row(RKP, NJ, a["rw_rk"].rearrange("l h c -> l (h c)"))
            row(GNG, NJ, a["rw_gn_g"])
            row(GNB, NJ, a["rw_gn_b"])
            row(PSC, 2, a["pool_scale"])
            for at_row, name in ((QN, "q_norm"), (KN, "k_norm")):
                for e in range(2):
                    row(at_row, 1, a[name], HD, e * HD)
            for t in range(NT):
                src = a["x_prompt"][0] if t == 0 else a["x_sample"][0, (t - 1) * P:t * P]
                act.dma_start(x_in[:, t, :], src).then_inc(x_in_s, 16)
            for l in range(DEPTH):
                act.wait_ge(head_mm, l + 1)
                copy(par[:, l, 0:n_par(l)], bank[l][:, 0:n_par(l)]).then_inc(head_cp, 1)
            act.wait_ge(head_cp, 1)
            for k in range(KT):
                both_conds = par[:, 0, COND:COND + 2 * KT].rearrange("p (s k) -> p k s", s=2)[:, k, :].unsqueeze(1).broadcast_to([P, CTILE // 2, 2])
                last = act.activation(cond[:, k, :].rearrange("p (r s) -> p r s", s=2), both_conds, ACT.Silu)
            last.then_inc(cond_up, 1)
            for g in range(2 * NT):
                t, half = g // 2, g % 2
                act.wait_ge(head_mm, DEPTH + g + 1)
                copy(h[:, 4 * half:4 * half + 4, tc(t)], bank4(2 + g)).then_inc(head_cp, 1)
            act.wait_ge(set_up, 1)

            def mod_rows(l, i):
                act.wait_ge(mod_mm, N_MOD * l + i + 1)
                if N_MOD * l + i > 0:
                    act.wait_ge(modt_mm, N_MOD * l + i)
                copy(mod_row, bank[6][:, 0:P]).then_inc(modr_cp, 1)

            def mod_turned(l, i):
                act.wait_ge(modt_mm, N_MOD * l + i + 1)
                copy(mod_raw[:, 4 * i:4 * i + 4, :],
                     bank[7][:, 0:P].rearrange("p (m s) -> p m s", m=4)[:, :, 0:2]).then_inc(modt_cp, 1)

            for i in range(N_MOD):
                mod_rows(0, i)
                mod_turned(0, i)

            def front(l):
                def arrived(n):
                    act.wait_ge(front_mm, FRONT * l + n + 1)
                    return bank[n % 7][:, 0:T]

                jobs = [(qk[:, m, :], ACT.Copy) for m in range(4)]
                jobs += [(vp[:, t, :], ACT.Copy) for t in range(NT)]
                jobs += [(v_tok[:, t, :], ACT.Copy) for t in range(NT)]
                jobs += [(lo_w, ACT.Tanh), (lo_a, ACT.Copy), (lo_g, ACT.Sigmoid)]
                jobs += [(r_t[:, j, :], ACT.Copy) for j in range(NJ)]
                jobs += [(k_t[:, j, :], ACT.Copy) for j in range(NJ)]
                n = 0
                for dst, func in jobs:
                    act.activation(dst, arrived(n), func).then_inc(front_cp, 1)
                    n += 1
                for d in range(2):
                    for j in range(NJ):
                        for dst, col in ((rate, W0), (b_t, A0)):
                            act.activation(dst[:, d, j, :], arrived(n), ACT.Sigmoid,
                                           bias=par[:, l, col + 3 * d + j:col + 3 * d + j + 1]).then_inc(front_cp, 1)
                            n += 1
                for m in range(4):
                    act.activation(rs[:, m, :], arrived(n), ACT.Sqrt, bias=eps[:, 0:1], scale=1.0 / HD).then_inc(front_cp, 1)
                    n += 1
                for j in range(NJ):
                    act.activation(y_t[:, j, :], arrived(n), ACT.Sqrt).then_inc(front_cp, 1)
                    n += 1
                for j in range(NJ):
                    copy(v_t[:, j, :], arrived(n)).then_inc(front_cp, 1)
                    n += 1

            def attention(l):
                def width(i):
                    return P if i < AH else T

                def exps(i):
                    n = 18 * l + i
                    act.wait_ge(max_up, n + 1)
                    if i >= 2:
                        act.wait_ge(pt_mm, n - 1)
                    act.activation(prob[:, i % 2, 0:width(i)], bank[i % 2][:, 0:width(i)], ACT.Exp,
                                   bias=stat[:, 0, i:i + 1], scale=HD ** -0.5,
                                   accum_out=stat[:, 1, i:i + 1]).then_inc(prob_up, 1)

                def turned(i):
                    n = 18 * l + i
                    act.wait_ge(pt_mm, n + 1)
                    if i >= 2:
                        act.wait_ge(o_mm, n - 1)
                    copy(prob_t[:, i % 2, 0:width(i)], bank[2 + i % 2][:, 0:width(i)]).then_inc(pt_cp, 1)

                def heads(t):
                    act.wait_ge(o_mm, 18 * l + AH * (t + 1))
                    copy(mixed[:, NJ:2 * NJ, tc(t)],
                         bank[4 + t][:, 0:T].rearrange("p (j n) -> p j n", j=NJ)).then_inc(o_cp, 1)

                for i in range(19):
                    if i < 18:
                        exps(i)
                    if i >= 1:
                        turned(i - 1)
                    if i >= 7 and (i - 7) % AH == 0:
                        heads((i - 7) // AH)
                heads(2)

            def exps(s, kinds):
                for d in range(2):
                    runs = run[:, 9 * d:9 * d + 9, :].rearrange("p (j t) n -> p j t n", j=NJ)[:, :, tiles(s)[d], :]
                    for kind in kinds:
                        with_t, sign = (((1, -1), (0, -1), (1, 1)), ((0, 1), (1, 1), (0, -1)))[d][kind]
                        act.activation(scaled[:, kind, :, tc(d)], runs[:, :, with_t:with_t + P], ACT.Exp,
                                       scale=sign * DECAY).then_inc(exp_up, 1)

            def rwkv_step(l, s):
                n = l * 3 + s
                if s == 0:
                    exps(s, (2, 1))
                else:
                    act.wait_ge(ys_mm, NJ * n)
                exps(s, (0,))
                if s == 1:
                    for d2 in range(2):
                        act.wait_ge(st_mm, 2 * l + d2 + 1)
                        copy(s_t.rearrange("p j d n -> p (j d) n")[:, 3 * d2:3 * d2 + 3, :],
                             bank4(6 + d2)[:, 0:3, :]).then_inc(st_cp, 1)

                def tok(g):
                    w = 4 if g % 2 == 0 else 2
                    act.wait_ge(tok_mm, 4 * n + g + 1)
                    copy(tok_m[:, g // 2].rearrange("p j n -> p (j n)")[:, 512 * (g % 2):512 * (g % 2) + w * P],
                         bank[6 + g % 2][:, 0:w * P]).then_inc(tok_cp, 1)

                tok(0)
                tok(1)
                for k in range(1, LEVELS):
                    if l + 1 < DEPTH and k >= 2:
                        if k <= 5:
                            mod_rows(l + 1, 4 * s + k - 2)
                        if k >= 3:
                            mod_turned(l + 1, 4 * s + k - 3)
                    for j in range(NJ):
                        act.wait_ge(t_mm, (n * (LEVELS - 1) + k - 1) * NJ + j + 1)
                        copy(t_m[:, j], bank4(j)).then_inc(t_cp, 1)
                    if k == 1:
                        tok(2)
                        tok(3)
                for j in range(NJ):
                    act.wait_ge(rhs_mm, NJ * n + j + 1)
                    copy(r_s, bank[6][:, 0:2 * P]).then_inc(rhs_cp, 1)
                    act.wait_ge(sa_mm, NJ * n + j + 1)
                    copy(sa_s, bank[7][:, 0:2 * P]).then_inc(sa_cp, 1)
                if s < 2:
                    exps(s + 1, (2, 1))
                if s == 0:
                    if l > 0:
                        act.wait_ge(s_out, 64 * l)
                    for d2 in range(2):
                        act.wait_ge(so_mm, 2 * l + d2 + 1)
                        copy(state_out[:, :, :, :].rearrange("p j d n -> p (j d) n")[:, 3 * d2:3 * d2 + 3, :],
                             bank4(6 + d2)[:, 0:3, :]).then_inc(so_cp, 1)

            def norm(l, which):
                n = 2 * l + which
                for c in range(KT):
                    act.wait_ge(xc_up, KT * n + c + 1)
                    act.activation(sq[:, c, :], h[:, c, :], ACT.Square).then_inc(ln_sq, 1)
                act.wait_ge(ln_mm, 2 * n + 2)
                act.activation(rstd, bank[5][:, 0:T], ACT.Sqrt, bias=eps[:, 2:3]).then_inc(ln_rt, 1)

            for l in range(DEPTH):
                front(l)
                act.wait_ge(ckt_mm, l + 1)
                copy(ckt, bank[0][:, 0:P]).then_inc(ckt_cp, 1)
                act.wait_ge(khead_mm, l + 1)
                copy(kh_out, bank[1][:, 0:P]).then_inc(kh_cp, 1)
                attention(l)
                for c in range(2):
                    act.wait_ge(pool_mm, 2 * l + c + 1)
                    copy(pool_d[:, c, :], bank[6 + c][:, 0:T]).then_inc(pool_cp, 1)
                for c in range(2):
                    act.wait_ge(poolw_mm, 2 * l + c + 1)
                    act.activation(mixed[:, 2 * NJ + c, :], bank[6 + c][:, 0:T], ACT.Copy,
                                   scale=par[:, l, PSC + c:PSC + c + 1]).then_inc(poolw_cp, 1)
                act.wait_ge(rates_up, l + 1)
                act.activation(edge, centre, ACT.Exp, scale=-DECAY).then_inc(edge_up, 1)
                act.wait_ge(bonus_up, NJ * (l + 1))
                act.wait_ge(v_out, 16 * (l + 1))
                act.wait_ge(k_out, 16 * (l + 1))
                for s in range(3):
                    rwkv_step(l, s)
                for j in range(NJ):
                    act.wait_ge(gn_c, NJ * l + j + 1)
                    act.activation(gn_s[:, j, :], y_t[:, j, :], ACT.Square).then_inc(gn_sq, 1)
                for j in range(NJ):
                    act.wait_ge(gn_mm, 2 * NJ * l + NJ + j + 1)
                    act.activation(gn_r[:, j, :], bank[j][:, 0:T], ACT.Sqrt, bias=eps[:, 1:2],
                                   scale=1.0 / HD).then_inc(gn_rt, 1)
                norm(l, 0)
                for g in range(2 * NT):
                    t, half = g // 2, g % 2
                    act.wait_ge(utok_mm, 2 * NT * l + g + 1)
                    copy(u_tok[:, t, 512 * half:512 * half + 512], bank[g][:, :]).then_inc(utok_cp, 1)
                act.wait_ge(d_up, 2 * l + 1)
                act.activation(g4[1], g4[0], ACT.Exp).then_inc(gexp_up, 1)
                act.wait_ge(d_up, 2 * l + 2)
                act.activation(g1[1], g1[0], ACT.Exp).then_inc(e2_up, 1)


                def prepared(job):
                    jn, b = JOBS * l + job, job % 2
                    for half in range(2):
                        act.wait_ge(xg_mm, 2 * jn + half + 1)
                        copy(xs[:, b, 4 * half:4 * half + 4, :], bank4(2 + half)).then_inc(xg_cp, 1)
                    act.wait_ge(misc_mm, jn + 1)
                    copy(sel_t[:, b, :], bank[7][:, 0:T])
                    copy(gates[:, b, :], bank[7][:, T:T + EPG]).then_inc(misc_cp, 1)

                def hidden(job, j):
                    n = EPG * (JOBS * l + job) + j
                    act.wait_ge(hid_mm, n + 1)
                    if n >= 2:
                        act.wait_ge(hid_up, n - 1)
                    act.activation(silu[:, j % 2, :], bank[j % 2][:, 0:DE], ACT.Silu).then_inc(silu_up, 1)

                def turned(job, j):
                    act.wait_ge(ht_mm, EPG * (JOBS * l + job) + j + 1)
                    copy(hid[:, job % 2, 2 * j:2 * j + 2, :], bank4(4)[:, 0:2, :]).then_inc(ht_cp, 1)

                def down(job):
                    jn = JOBS * l + job
                    act.wait_ge(down_mm, 2 * jn + 2)
                    for half in range(2):
                        copy(ys[:, 512 * half:512 * half + 512], bank[5 + half][:, :]).then_inc(ys_cp, 1)

                prepared(0)
                for job in range(NG):
                    hidden(job, 0)
                    for j in range(1, EPG):
                        hidden(job, j)
                        turned(job, j - 1)
                    if job + 1 < NG:
                        prepared(job + 1)
                    turned(job, EPG - 1)
                    down(job)
                act.wait_ge(plan_up, l + 1)
                count = act.value_load(plan[0:1, 0:1], min_val=0, max_val=2)
                for over in range(2):
                    job = OVER + over
                    with act.If(count > over):
                        prepared(job)
                        for j in range(EPG):
                            hidden(job, j)
                            turned(job, j)
                        down(job)
                    with act.Else():
                        skip(act, JOBS * l + job, ((xg_cp, 2), (misc_cp, 1), (silu_up, EPG), (ht_cp, EPG), (ys_cp, 2)))
                norm(l, 1)
            for g in range(2 * NT):
                t, half = g // 2, g % 2
                act.wait_ge(tail_mm, g + 1)
                copy(y_out[:, t, 512 * half:512 * half + 512], bank[g][:, :]).then_inc(tail_cp, 1)

        @block.vector
        def _(dve):
            steps = [0]

            def mark(ins):
                steps[0] += 1
                ins.then_inc(vec_step, 1)
                return steps[0]

            def after(n=None):
                dve.wait_ge(vec_step, steps[0] if n is None else n)

            def link(ins):
                mark(ins)
                after()

            tt, ts, stt = dve.tensor_tensor, dve.tensor_scalar, dve.scalar_tensor_tensor
            dve.memset(eps[:, 0:1], QK_EPS)
            dve.memset(eps[:, 1:2], GN_EPS)
            dve.memset(eps[:, 2:3], LN_EPS / ALPHA ** 2)
            dve.memset(ones_row[:, :], 1.0)
            dve.memset(state_nat[:, :, :, :], 0.0).then_inc(set_up, 1)
            dve.wait_ge(level_in, 16)
            link(dve.tensor_copy(lev[:, :, :, :].rearrange("p a b n -> p (a b n)"), level))

            def modulate(l, which):
                base = 24 * which
                for c in range(KT):
                    for g, (lo, hi) in enumerate(STREAMS):
                        last = ts(u[:, c, lo:hi], h[:, c, lo:hi], mod[:, base + 8 + c, g:g + 1],
                                  mod[:, base + c, g:g + 1], ALU.mult, ALU.add)
                    last.then_inc(u_up, 1)

            def residual(l, c, base, psum, done):
                for g, (lo, hi) in enumerate(STREAMS):
                    last = stt(h[:, c, lo:hi], psum[:, lo:hi], mod[:, base + c, g:g + 1], h[:, c, lo:hi],
                               ALU.mult, ALU.add)
                last.then_inc(done, 1)

            def norm(l, which):
                n = 2 * l + which
                g0, b0 = ((LN1G, LN1B), (LN2G, LN2B))[which]
                dve.wait_ge(ln_mm, 2 * n + 1)
                for c in range(KT):
                    tt(h[:, c, :], h[:, c, :], bank[4][:, 0:T], ALU.subtract).then_inc(xc_up, 1)
                dve.wait_ge(ln_rt, n + 1)
                link(dve.reciprocal(rstd, rstd))
                first_step = steps[0]
                dve.wait_ge(ln_sq, KT * (n + 1))
                for c in range(KT):
                    mark(stt(h[:, c, :], h[:, c, :], par[:, l, g0 + c:g0 + c + 1], rstd, ALU.mult, ALU.mult))
                for c in range(KT):
                    after(first_step + c + 1)
                    ts(h[:, c, :], h[:, c, :], par[:, l, b0 + c:b0 + c + 1], None, ALU.add).then_inc(h_up, 1)
                dve.wait_ge(h_up, KT * (n + 1))

            def front(l):
                base = FRONT * l
                dve.wait_ge(front_cp, base + 4)
                tt(qk_s, qk, qk, ALU.mult).then_inc(qk_sq, 1)
                dve.memset(run[:, :, 0:1], 0.0)
                dve.wait_ge(front_cp, base + 19)
                for j in range(NJ):
                    last = ts(kk_t[:, j, :], k_t[:, j, :], par[:, l, KKP + j:KKP + j + 1], None, ALU.mult)
                link(last)
                tt(kr, kk_t, kk_t, ALU.mult).then_inc(kk_sq, 1)
                dve.wait_ge(front_cp, base + 31)
                for d in range(2):
                    for j in range(NJ):
                        for t in range(NT):
                            src = rate[:, d, j, tc(t)]
                            last = dve.tensor_tensor_scan(run[:, 9 * d + 3 * j + t, 1:P + 1], src, src, 0.0,
                                                          ALU.add, ALU.max)
                link(last)
                link(ts(centre, run[:, :, P], 0.5, None, ALU.mult))
                tt(run, run, centre.unsqueeze(2).broadcast_to([P, 2 * NJ * NT, P + 1]), ALU.subtract).then_inc(rates_up, 1)
                for d in range(2):
                    for j in range(NJ):
                        last = ts(kd_t[:, d, j, :], b_t[:, d, j, :], par[:, l, KAP + j:KAP + j + 1],
                                  one_less_ka[:, j:j + 1], ALU.mult, ALU.add)
                link(last)
                for d in range(2):
                    last = tt(kd_t[:, d], kd_t[:, d], k_t, ALU.mult)
                link(last)
                dve.wait_ge(front_cp, base + 35)
                link(dve.reciprocal(rs, rs))
                for m in range(4):
                    col = QN if m < 3 else KN
                    last = stt(qk[:, m, :], qk[:, m, :], par[:, l, col:col + 1], rs[:, m, :], ALU.mult, ALU.mult)
                last.then_inc(qk_up, 1)
                dve.wait_ge(front_cp, base + 38)
                link(ts(y_t, y_t, 1e-12, None, ALU.max))
                link(dve.reciprocal(y_t, y_t))
                link(tt(kk_t, kk_t, y_t, ALU.mult))
                for d in range(2):
                    mark(tt(b_t[:, d], b_t[:, d], kk_t, ALU.mult))
                link(tt(kr, kd_t[:, 0], kd_t[:, 1], ALU.add))
                for j in range(NJ):
                    last = stt(kr[:, j, :], r_t[:, j, :], par[:, l, RKP + j:RKP + j + 1], kr[:, j, :], ALU.mult, ALU.mult)
                last.then_inc(bonus_in, 1)
                dve.wait_ge(qk_up, l + 1)
                mark(tt(rs[:, :, P:T], qk[:, :, P:T], rope_cos.unsqueeze(1).broadcast_to([P, 4, DEC]), ALU.mult))
                for m in range(2):
                    dve.wait_ge(rot_mm, 2 * l + m + 1)
                    last = tt(qk_s[:, 2 * m:2 * m + 2, P:T], bank[2 + m][:, :].rearrange("p (m n) -> p m n", m=2),
                              rope_sin.unsqueeze(1).broadcast_to([P, 2, DEC]), ALU.mult)
                link(last)
                tt(qk[:, :, P:T], rs[:, :, P:T], qk_s[:, :, P:T], ALU.add).then_inc(qkr_up, 1)

            def attention(l):
                def maxima(i):
                    w = P if i < AH else T
                    dve.wait_ge(score_mm, 18 * l + i + 1)
                    link(dve.tensor_reduce(stat[:, 2, i:i + 1], bank[i % 2][:, 0:w], AX.X, ALU.max, negate=True))
                    ts(stat[:, 0, i:i + 1], stat[:, 2, i:i + 1], HD ** -0.5, None, ALU.mult).then_inc(max_up, 1)

                def normal(i):
                    w = P if i < AH else T
                    dve.wait_ge(prob_up, 18 * l + i + 1)
                    link(dve.reciprocal(stat[:, 2, i:i + 1], stat[:, 1, i:i + 1]))
                    ts(prob[:, i % 2, 0:w], prob[:, i % 2, 0:w], stat[:, 2, i:i + 1], None, ALU.mult).then_inc(pn_up, 1)

                for i in range(19):
                    if i < 18:
                        maxima(i)
                    if i >= 1:
                        normal(i - 1)

            def scaled_first(l, s):
                n = l * 3 + s
                dve.wait_ge(exp_up, 6 * n + 4)
                for d in range(2):
                    t = tiles(s)[d]
                    mark(tt(scaled[:, 3, :, tc(d)], scaled[:, 2, :, tc(d)], kd_t[:, d, :, tc(t)], ALU.mult))
                    tt(scaled[:, 2, :, tc(d)], scaled[:, 2, :, tc(d)], b_t[:, d, :, tc(t)], ALU.mult)
                    last = stt(scaled[:, 1, :, tc(d)], kk_t[:, :, tc(t)], -1.0, scaled[:, 1, :, tc(d)], ALU.mult, ALU.mult)
                last.then_inc(scaled_up, 1)

            def rwkv_step(l, s):
                n = l * 3 + s
                if s == 0:
                    scaled_first(l, s)
                dve.wait_ge(x_init, 2 * NJ * (n + 1))
                for j in range(NJ):
                    for e in range(2):
                        b = bank4(2 * j + e)
                        dve.wait_ge(inv_mm, 2 * (NJ * n + j) + e + 1)
                        dve.copy_predicated(quad(x_m[:, j])[:, :, e, :], lev[:, 0, 0:2, :], b[:, 0:2, :])
                        tt(quad(at_m[:, j])[:, :, e, :], b[:, 2:4, :], strict, ALU.mult)
                        last = dve.copy_predicated(quad(xt_m[:, j])[:, :, e, :], lev[:, 0, 1:3, :], b[:, 2:4, :])
                    last.then_inc(at_up, 1)
                dve.wait_ge(exp_up, 6 * (n + 1))
                for d in range(2):
                    part = scaled[:, 0, :, tc(d)]
                    last = tt(part, part, r_t[:, :, tc(tiles(s)[d])], ALU.mult)
                last.then_inc(scaled_up, 1)
                if s == 0:
                    link(dve.memset(s_t, 0.0))
                if s == 1:
                    dve.wait_ge(st_cp, 2 * (l + 1))
                dve.wait_ge(edge_up, l + 1)
                for d in range(2):
                    t = tiles(s)[d]
                    for j in range(NJ):
                        i = 9 * d + 3 * j + t
                        last = ts(s_hat[:, j, d, :], s_t[:, j, d, :], edge[:, i:i + 1], None, ALU.mult)
                last.then_inc(shat_up, 1)
                for k in range(1, LEVELS):
                    for j in range(NJ):
                        if k < LEVELS - 1:
                            dve.wait_ge(x_mm, xi(l, s, k, j, 0))
                            dve.copy_predicated(quad(x_m[:, j]), both(lev[:, k, 0:2, :]), quad(bank4(j))).then_inc(x_up, 1)
                        dve.wait_ge(x_mm, xi(l, s, k, j, 1))
                        dve.copy_predicated(quad(xt_m[:, j]), both(lev[:, k, 1:3, :]), quad(bank4(3 + j))).then_inc(x_up, 1)

                def masks(j):
                    for m, mask in enumerate((strict, incl, incl)):
                        for e in range(2):
                            dve.wait_ge(msc_mm, 6 * (NJ * n + j) + 2 * max(m, 1) + e + 1)
                            last = tt(quad(masks_of[j][:, m])[:, :, e, :], bank4(2 * (m // 2) + e)[:, 2 * (m % 2):2 * (m % 2) + 2, :],
                                      mask, ALU.mult)
                        last.then_inc(msc_up, 1)

                def outputs(j):
                    b = 4 + j % 2
                    dve.wait_ge(ys_mm, NJ * n + j + 1)
                    for d in range(2):
                        t = tiles(s)[d]
                        dst = y_t[:, j, tc(t)]
                        if s == 1 or (s == 0 and d == 0):
                            link(dve.tensor_copy(dst, bank[b][:, tc(d)]))
                        else:
                            link(tt(dst, dst, bank[b][:, tc(d)], ALU.add))
                    for d in range(2):
                        i = 9 * d + 3 * j + tiles(s)[d]
                        last = stt(s_new[:, d, :], bank[b][:, tc(2 + d)], edge[:, i:i + 1], head_ones, ALU.mult, ALU.mult)
                    last.then_inc(ys_up, 1)
                    dve.wait_ge(ys_up, NJ * n + j + 1)
                    for d in range(2):
                        i = 9 * d + 3 * j + tiles(s)[d]
                        last = stt(s_t[:, j, d, :], s_hat[:, j, d, :], edge[:, i:i + 1], s_new[:, d, :], ALU.mult, ALU.add)
                    last.then_inc(state_up, 1)

                for j in range(NJ):
                    masks(j)
                for j in range(NJ):
                    if j == NJ - 1 and s < 2:
                        scaled_first(l, s + 1)
                    outputs(j)
                dve.wait_ge(state_up, NJ * (n + 1))

            def heads_norm(l):
                for j in range(NJ):
                    dve.wait_ge(gn_mm, 2 * NJ * l + j + 1)
                    stt(y_t[:, j, :], bank[j][:, 0:T], -1.0 / HD, y_t[:, j, :], ALU.mult, ALU.add).then_inc(gn_c, 1)
                dve.wait_ge(gn_rt, NJ * (l + 1))
                link(dve.reciprocal(gn_r, gn_r))
                link(tt(y_t, y_t, gn_r, ALU.mult))
                for j in range(NJ):
                    last = ts(y_t[:, j, :], y_t[:, j, :], par[:, l, GNG + j:GNG + j + 1], par[:, l, GNB + j:GNB + j + 1],
                              ALU.mult, ALU.add)
                link(last)
                link(tt(y_t, y_t, v_t, ALU.add))
                for j in range(NJ):
                    dve.wait_ge(g_mm, NJ * l + j + 1)
                    tt(mixed[:, j, :], y_t[:, j, :], bank[3 + j][:, 0:T], ALU.mult).then_inc(mixa_up, 1)

            def route(l):
                gd, ge, gm, ls, oh1, oh2, gtmp = g4[:7]
                (p1e, e2, mx, s_g, m1, m2, mw, den, p1, p2, rank, rank1, more, at_over, code, is_over, base_t) = g1
                nb, upto, base, here, ids, plan_f = row4

                def wide(v):
                    return v.unsqueeze(2).broadcast_to([P, NT, 4])

                def every(v):
                    return v.unsqueeze(1).broadcast_to([P, NT, 4])

                def first_of(src, top):
                    link(tt(gtmp, src, wide(top), ALU.is_equal))
                    link(tt(gtmp, gtmp, first, ALU.mult))
                    link(dve.tensor_reduce(mw, gtmp, AX.X, ALU.max))
                    return gtmp, wide(mw)

                def pick(dst, per_group):
                    link(tt(gtmp, group_1h, per_group, ALU.mult))
                    link(dve.tensor_reduce(dst, gtmp, AX.X, ALU.add))

                dve.wait_ge(route_mm, l + 1)
                link(dve.tensor_copy(rl, bank[7][:, 0:20 * NT].rearrange("p (t n) -> p t n", t=NT)))
                lg = rl[:, :, 0:NG]
                link(dve.tensor_reduce(mx, lg, AX.X, ALU.max))
                tt(gd, lg, wide(mx), ALU.subtract).then_inc(d_up, 1)
                v, top = first_of(lg, mx)
                tt(group_1h, v, top, ALU.is_equal).then_inc(onehot_up, 1)
                dve.wait_ge(onehot_up, l + 1)
                experts = rl[:, :, NG:20].rearrange("p t (g j) -> p t g j", g=NG)
                link(tt(les_in, experts, group_1h.unsqueeze(3).broadcast_to([P, NT, NG, EPG]), ALU.mult))
                link(dve.tensor_reduce(ls, les_in.rearrange("p t g j -> p t j g"), AX.X, ALU.add))
                link(dve.tensor_reduce(m1, ls, AX.X, ALU.max))
                v, top = first_of(ls, m1)
                link(tt(oh1, v, top, ALU.is_equal))
                link(stt(gm, oh1, -1e30, ls, ALU.mult, ALU.add))
                link(dve.tensor_reduce(m2, gm, AX.X, ALU.max))
                tt(p1e, m2, m1, ALU.subtract).then_inc(d_up, 1)
                v, top = first_of(gm, m2)
                link(tt(oh2, v, top, ALU.is_equal))
                dve.wait_ge(rank_mm, l + 1)
                link(dve.tensor_copy(rank_s, bank[6][:, 0:16]))
                pick(rank, rank_s[:, 0:12].rearrange("p (t g) -> p t g", t=NT))
                link(ts(rank1, rank, 1.0, None, ALU.add))
                link(tt(codes, group_1h, wide(rank1), ALU.mult))
                link(ts(codes, codes, 1.0, None, ALU.subtract))
                dve.wait_ge(gexp_up, l + 1)
                link(dve.tensor_reduce(s_g, ge, AX.X, ALU.add))
                dve.wait_ge(e2_up, l + 1)
                link(ts(den, e2, 1.0, None, ALU.add))
                link(tt(den, den, s_g, ALU.mult))
                link(dve.reciprocal(p1, den))
                link(tt(p2, p1, e2, ALU.mult))
                mark(tt(oh1, oh1, wide(p1), ALU.mult))
                link(tt(oh2, oh2, wide(p2), ALU.mult))
                link(tt(inner, oh1, oh2, ALU.add))
                choose(l, 0)
                choose(l, 1)
                size = rank_s[:, 12:16]
                link(ts(nb, size, P + 0.5, None, ALU.is_gt))
                link(stt(nb, size, 2 * P + 0.5, nb, ALU.is_gt, ALU.add))
                link(dve.tensor_tensor_scan(upto, nb, nb, 0.0, ALU.add, ALU.max))
                link(tt(base, upto, nb, ALU.subtract))
                pick(base_t, every(base))
                link(ts(more, rank, P - 0.5, None, ALU.is_gt))
                link(stt(more, rank, 2 * P - 0.5, more, ALU.is_gt, ALU.add))
                link(ts(is_over, more, 0.5, None, ALU.is_gt))
                link(tt(at_over, base_t, more, ALU.add))
                link(tt(at_over, at_over, is_over, ALU.mult))
                link(stt(code, more, -float(P), rank1, ALU.mult, ALU.add))
                link(ts(ids, first[:, 0, :], -float(EPG), float(EPG * NG), ALU.mult, ALU.add))
                link(dve.tensor_copy(plan_f[:, 0:1], upto[:, 3:4]))
                for over in range(2):
                    link(stt(over_codes[:, :, over], at_over, over + 1.0, code, ALU.is_equal, ALU.mult))
                    link(ts(here, base, over + 0.5, None, ALU.is_lt))
                    link(stt(here, upto, over + 0.5, here, ALU.is_gt, ALU.mult))
                    link(tt(here, here, ids, ALU.mult))
                    link(dve.tensor_reduce(plan_f[:, 1 + over:2 + over], here, AX.X, ALU.add))
                link(ts(over_codes, over_codes, 1.0, None, ALU.subtract))
                dve.tensor_copy(plan[0:1, 0:3], plan_f[0:1, 0:3]).then_inc(plan_up, 1)

            def choose(l, job):
                jn = JOBS * l + job
                if jn >= 2:
                    dve.wait_ge(misc_mm, jn - 1)
                for t in range(NT):
                    code = codes[:, t, job:job + 1] if job < NG else over_codes[:, t, job - NG:job - NG + 1]
                    last = ts(sel[:, job % 2, t, :], slots, code, None, ALU.is_equal)
                last.then_inc(sel_up, 1)

            def experts(l):
                def hidden(job, j):
                    jn = JOBS * l + job
                    n = EPG * jn + j
                    dve.wait_ge(silu_up, n + 1)
                    dve.wait_ge(misc_cp, jn + 1)
                    if n >= 2:
                        dve.wait_ge(ht_mm, n - 1)
                    stt(hs[:, j % 2, :], silu[:, j % 2, :], gates[:, job % 2, j:j + 1], bank[j % 2][:, DE:2 * DE],
                        ALU.mult, ALU.mult).then_inc(hid_up, 1)

                def add(job):
                    jn = JOBS * l + job
                    if jn > 0:
                        dve.wait_ge(z2_up, KT * jn)
                    for c in range(KT):
                        dve.wait_ge(un_mm, KT * jn + c + 1)
                        residual(l, c, 40, bank[2 + c % 2], z2_up)

                for job in range(NG):
                    for j in range(EPG):
                        hidden(job, j)
                        if j == 0 and job > 0:
                            add(job - 1)
                    if job + 2 < NG:
                        choose(l, job + 2)
                add(NG - 1)
                dve.wait_ge(plan_up, l + 1)
                count = dve.value_load(plan[0:1, 0:1], min_val=0, max_val=2)
                for over in range(2):
                    job = OVER + over
                    with dve.If(count > over):
                        choose(l, job)
                        for j in range(EPG):
                            hidden(job, j)
                        add(job)
                    with dve.Else():
                        skip(dve, JOBS * l + job, ((sel_up, 1), (hid_up, EPG), (z2_up, KT)))

            for l in range(DEPTH):
                dve.wait_ge(modt_cp, N_MOD * (l + 1))
                dve.wait_ge(head_cp, 8)
                link(tt(mod[:, :, :], mod_raw[:, :, :],
                        par[:, l, 0:48].unsqueeze(2).broadcast_to([P, 48, 2]), ALU.add))
                for which in range(2):
                    lo = 24 * which
                    mark(ts(mod[:, lo + 8:lo + 16, :], mod[:, lo + 8:lo + 16, :], 1.0, None, ALU.add))
                    mark(ts(mod[:, lo + 16:lo + 24, :], mod[:, lo + 16:lo + 24, :], 1.0 / ALPHA, None, ALU.mult))
                link(ts(one_less_ka[:, :], par[:, l, KAP:KAP + NJ], -1.0, 1.0, ALU.mult, ALU.add))
                if l == 0:
                    dve.wait_ge(cst_in, 16)
                modulate(l, 0)
                front(l)
                attention(l)
                for j in range(NJ):
                    dve.wait_ge(bonus_mm, NJ * l + j + 1)
                    dve.wait_ge(front_cp, FRONT * (l + 1))
                    tt(v_t[:, j, :], v_t[:, j, :], bank[j][:, 0:T], ALU.mult).then_inc(bonus_up, 1)
                dve.wait_ge(poolw_cp, 2 * (l + 1))
                dve.wait_ge(v_out, 16 * (l + 1))
                dve.wait_ge(k_out, 16 * (l + 1))
                for s in range(3):
                    rwkv_step(l, s)
                heads_norm(l)
                for c in range(KT):
                    dve.wait_ge(proj_mm, KT * l + c + 1)
                    residual(l, c, 16, bank[c % 4], z_up)
                norm(l, 0)
                modulate(l, 1)
                route(l)
                experts(l)
                norm(l, 1)


INPUTS = ("x_prompt", "x_sample", "state_rwkv", "cache_k", "cache_v", "c", "c_ctx", "w_in", "w_out", "w_mod", "b_mod",
          "ln1_g", "ln1_b", "ln2_g", "ln2_b", "rw_w0", "rw_w2", "rw_a0", "rw_a2", "rw_g2", "rw_kk", "rw_ka", "rw_rk",
          "rw_gn_g", "rw_gn_b", "q_norm", "k_norm", "pool_w", "pool_scale", "rt_grp_w", "rt_grp_b", "rt_exp_w",
          "rt_exp_b", "moe_w1", "moe_w3", "moe_w2")
OUTPUTS = ((1, SEQ, D), (1, DEC, D), (1, DEPTH, 2, AH, HD, HD), (1, DEPTH, SEQ, KVH, HD), (1, DEPTH, SEQ, KVH, HD))


def kernel(**inputs):
    import concourse.bacc as bacc
    from concourse.bass_utils import run_bass_kernel_spmd

    nc = bacc.Bacc("TRN2", target_bir_lowering=False, num_devices=1)
    arrays = {name: np.ascontiguousarray(inputs[name]) for name in INPUTS}
    arrays.update(constants())
    aps = {name: nc.dram_tensor(f"in_{name}", v.shape, mybir.dt.from_np(v.dtype), kind="ExternalInput").ap()
           for name, v in arrays.items()}
    outs = [nc.dram_tensor(f"out_{i}", shape, F32, kind="ExternalOutput").ap() for i, shape in enumerate(OUTPUTS)]
    build(nc, aps, outs)
    r = run_bass_kernel_spmd(nc, [{f"in_{name}": v for name, v in arrays.items()}], core_ids=[0])
    return tuple(r.results[0][f"out_{i}"] for i in range(len(OUTPUTS)))
```

```python
from contextlib import ExitStack

import numpy as np

import concourse.bass as bass
from concourse import mybir

ALU = mybir.AluOpType
ACT = mybir.ActivationFunctionType
AX = mybir.AxisListType
F32 = mybir.dt.float32
U8 = mybir.dt.uint8

P = 128
DEPTH = 2
D = 1024
KT = D // P
SEQ, DEC = 128, 256
T = SEQ + DEC
NT = T // P
GRID_W = 64
HD = 64
AH = 6
NJ = AH // 2
KVH = 2
GRP = 3
POOL_WINDOWS = (2, 4, 8, 16)
NG, EPG = 4, 4
NE = NG * EPG
DE = 256
ALPHA = (2 * DEPTH) ** 0.25
DECAY = 0.606531
LN_EPS, GN_EPS, QK_EPS = 1e-5, 64e-5, 1e-6
LEVELS = 7
STREAMS = ((0, SEQ), (SEQ, T))

BMOD, LN1G, LN1B, LN2G, LN2B = 0, 48, 56, 64, 72
W0, A0, KKP, KAP, RKP, GNG, GNB, PSC, QN, KN, COND, NPAR = 80, 86, 92, 95, 98, 101, 104, 107, 109, 110, 111, 127

RING = 3
SLOT = 4096
IN_COLS = ((1536, 512), (2048, 384), (768, 384), (1152, 384), (0, 384), (384, 384))
OUT_TILES = (3, 3, 2)
N_MOD = 12
JOBS = NG + 2
OVER = NG
JOB_ITEMS = EPG + 2
MOD_FIRST = 4
ORDER = [("mod", 0, i) for i in range(MOD_FIRST)]
for _l in range(DEPTH):
    for _i in range(len(IN_COLS)):
        ORDER += [("in", _l, _i)] + ([("mod", 0, MOD_FIRST + _i)] if _l == 0 else [])
    ORDER += [("mod", 0, i) for i in range(MOD_FIRST + len(IN_COLS), N_MOD)] if _l == 0 else []
    ORDER += [("mod", _l + 1, i) for i in range(N_MOD)] if _l + 1 < DEPTH else []
    ORDER += [("out", _l, i) for i in range(len(OUT_TILES))]
    ORDER += [("job", _l, i) for i in range(JOBS * JOB_ITEMS)]
PLACE = {item: n for n, item in enumerate(ORDER)}

N_PAR_DMAS = 19
N_PAR2 = 8
CTILE = 32
FRONT = 19 + 12 + 4 + NJ + NJ
SMALL = 14


def item_dmas(item):
    kind, _, i = item
    return 4 if kind == "out" else 7 if kind == "in" and i == 0 else 2


def landed_value(n):
    return sum(16 * item_dmas(ORDER[m]) for m in range(n % RING, n + 1, RING))


def constants():
    f = np.float32
    ident = np.eye(P, dtype=f)
    ones_d = np.full((P, P), 1.0 / D, f)
    head_ones = np.kron(np.eye(2), np.ones((HD, HD))).astype(f)
    rot = np.zeros((P, P), f)
    for c in range(P):
        i = c % 32
        if i < 16:
            rot[c + 16, c] = -1.0
        else:
            rot[c - 16, c] = 1.0
    n = HD // 4
    inv = (1.0 / (10000.0 ** (np.arange(n, dtype=f) / n))).astype(f)
    t = np.arange(DEC)
    pos = np.stack([(t // GRID_W).astype(f), (t % GRID_W).astype(f)])
    rope = np.zeros((P, 2, DEC), f)
    for c in range(P):
        ang = pos[(c % HD) // 32] * inv[c % 16]
        rope[c, 0], rope[c, 1] = np.cos(ang), np.sin(ang)

    def band(length):
        out = np.zeros((4, length, length), f)
        tt = np.arange(length)
        for g, w in enumerate(POOL_WINDOWS):
            lo, hi = np.clip(tt - w // 2, 0, length), np.clip(tt + w // 2, 0, length)
            s = np.arange(length)[:, None]
            out[g] = ((s >= lo) & (s < hi)) / (hi - lo).astype(f)
            out[g] -= np.eye(length, dtype=f)
        return out

    band_p = band(SEQ).transpose(1, 0, 2)
    band_s = band(DEC).reshape(4, 2, P, DEC).transpose(2, 0, 1, 3).reshape(P, 8, DEC)
    s, tt = np.arange(P)[:, None], np.arange(P)[None, :]
    strict = np.stack([s < tt, s > tt], 1).astype(f)
    incl = np.stack([s <= tt, s >= tt], 1).astype(f)
    level = np.zeros((P, LEVELS, 3, P), f)
    for k in range(LEVELS):
        b = 1 << k
        low = (s // (2 * b) == tt // (2 * b)) & ((s // b) % 2 == 1) & ((tt // b) % 2 == 0)
        level[:, k, 0], level[:, k, 1], level[:, k, 2] = low, low.T, low
    slots = np.tile(np.arange(P, dtype=f), (P, 1))
    first = np.tile(np.arange(4, 0, -1, dtype=f), (P, NT, 1))
    mats = np.concatenate([ident, ones_d, head_ones, rot, rope.reshape(P, -1), strict.reshape(P, -1),
                           incl.reshape(P, -1), first.reshape(P, -1), slots], 1)
    bands = np.concatenate([band_p.reshape(P, -1), band_s.reshape(P, -1)], 1)
    return {"mats": np.ascontiguousarray(mats), "bands": np.ascontiguousarray(bands),
            "level": np.ascontiguousarray(level.reshape(P, -1))}


def build(nc, a, out):
    y_prompt, y_sample, new_state, new_k, new_v = out
    with ExitStack() as ctx:
        def sb(name, shape, dt=F32):
            return ctx.enter_context(nc.sbuf_tensor(name, shape, dt))

        def sem(name):
            return ctx.enter_context(nc.semaphore(name))

        bank = [ctx.enter_context(nc.psum_tensor(f"bank{i}", [P, 512], F32)) for i in range(8)]

        n_mats = a["mats"].shape[1]
        cst = sb("cst", [P, n_mats])
        at = [0]

        def const(n):
            at[0] += n
            return cst[:, at[0] - n:at[0]]

        ident, ones_d, head_ones, rot = const(P), const(P), const(P), const(P)
        rope_cos, rope_sin = const(DEC), const(DEC)
        strict = const(2 * P).rearrange("p (d n) -> p d n", d=2)
        incl = const(2 * P).rearrange("p (d n) -> p d n", d=2)
        first = const(NT * 4).rearrange("p (t n) -> p t n", t=NT)
        slots = const(P)
        lev = sb("lev", [P, LEVELS, 3, P], U8)
        ones_row = incl[0:1, 0, :]
        eps = sb("eps", [P, 3])

        h = sb("h", [P, KT, T])
        u = sb("u", [P, KT, T])
        mixed = u
        ring = sb("ring", [P, RING, SLOT])
        par = sb("par", [P, DEPTH, NPAR])
        cond = sb("cond", [P, KT, CTILE])
        mod = sb("mod", [P, 48, 2])
        mod_raw = sb("mod_raw", [P, 48, 2])
        shift = sb("shift", [P, KT, 2])
        mod_row = sb("mod_row", [P, P])
        plan = sb("plan", [1, 4], mybir.dt.int32)
        one_less_ka = sb("one_less_ka", [P, NJ])
        lora_w2 = sb("lora_w2", [P, NJ * P])
        lora_a2 = sb("lora_a2", [P, NJ * P])
        lora_g2 = sb("lora_g2", [P, NJ * P])
        pool_w = sb("pool_w", [P, 2, HD])
        route_w = sb("route_w", [P, KT, 20])
        route_b = sb("route_b", [1, 20])
        ctx_k = sb("ctx_k", [P, P])
        ctx_v = sb("ctx_v", [P, P])
        state_nat = sb("state_nat", [P, NJ, 2, P])

        REGION = 28184
        region = sb("region", [P, REGION])
        off = [0]

        def view(*shape):
            n = int(np.prod(shape))
            v = region[:, off[0]:off[0] + n]
            off[0] += n
            assert off[0] <= REGION, off[0]
            if len(shape) == 2:
                v = v.rearrange("p (a b) -> p a b", a=shape[0])
            if len(shape) == 3:
                v = v.rearrange("p (a b c) -> p a b c", a=shape[0], b=shape[1])
            return v

        r_t = view(NJ, T)
        kk_t = view(NJ, T)
        v_t = view(NJ, T)
        kd_t = view(2, NJ, T)
        b_t = view(2, NJ, T)
        run = view(2 * NJ * NT, P + 1)
        lo_g = view(T)
        v_tok = view(NT, NJ * P)
        y_t = view(NJ, T)
        centre = view(2 * NJ * NT)
        edge = view(2 * NJ * NT)
        shared = off[0]
        x_m = view(NJ, 4, P)
        xt_m = view(NJ, 4, P)
        at_m = view(NJ, 4, P)
        t_m = view(NJ, 4, P)
        scaled = view(4, NJ, 2 * P)
        tok_m = view(2, NJ, 2 * P)
        lmasks = view(3, 4, P)
        masks_of = (lmasks, at_m, t_m)
        r_s = view(2 * P)
        sa_s = view(2 * P)
        s_t = view(NJ, 2, P)
        s_hat = view(NJ, 2, P)
        s_new = view(2, P)
        off[0] = shared
        k_t = view(NJ, T)
        lo_w = view(T)
        lo_a = view(T)
        qk = view(4, T)
        qk_s = view(4, T)
        rs = view(4, T)
        kr = view(NJ, T)
        vp = view(NT, T)
        ckt = view(P)
        kh_out = view(P)
        stat = view(3, 18)
        pool_d = view(2, T)
        bands = view(4 * SEQ + 8 * DEC)
        band_p = bands[:, 0:4 * SEQ].rearrange("p (g n) -> p g n", g=4)
        band_s = bands[:, 4 * SEQ:].rearrange("p (g n) -> p g n", g=8)
        rate = view(2, NJ, T)
        prob = qk_s[:, 0:2, :]
        prob_t = qk_s[:, 2:4, :]
        off[0] = shared
        gn_s = view(NJ, T)
        gn_r = view(NJ, T)
        off[0] = 0
        sq = view(KT, T)
        rstd = view(T)
        u_tok = view(NT, D)
        sel = view(2, NT, P)
        sel_t = view(2, T)
        xs = view(2, KT, P)
        logits = view(T)[0:20, :]
        silu = view(2, DE)
        hs = view(2, DE)
        hid = view(2, 2 * EPG, P)
        ys = view(D)
        gates = view(2, EPG)
        rl = view(NT, 20)
        g4 = [view(NT, 4) for _ in range(9)]
        g1 = [view(NT) for _ in range(17)]
        les_in = view(NT, 4, 4)
        group_1h, codes, inner, over_codes = view(NT, 4), view(NT, 4), view(NT, 4), view(NT, 2)
        rank_s = view(16)
        row4 = [view(4) for _ in range(6)]
        off[0] = 0
        x_in = view(NT, D)
        rows = view(DEPTH, P)
        level = view(LEVELS * 3 * P)
        off[0] = 0
        y_out = view(NT, D)
        state_out = sb("state_out", [P, NJ, 2, P])

        cst_in, x_in_s, par_in, small_in = sem("cst_in"), sem("x_in"), sem("par_in"), sem("small_in")
        level_in, par2_in = sem("level_in"), sem("par2_in")
        slot_in = [sem(f"slot_in{i}") for i in range(RING)]
        k_out, v_out, s_out, y_out_s = sem("k_out"), sem("v_out"), sem("s_out"), sem("y_out_s")
        bands_in = sem("bands_in")
        head_mm = sem("head_mm")
        mod_mm = sem("mod_mm")
        front_mm = sem("front_mm")
        khead_mm, rot_mm, ckt_mm = sem("khead_mm"), sem("rot_mm"), sem("ckt_mm")
        score_mm, pt_mm, o_mm = sem("score_mm"), sem("pt_mm"), sem("o_mm")
        pool_mm, poolw_mm, bonus_mm = sem("pool_mm"), sem("poolw_mm"), sem("bonus_mm")
        st_mm, tok_mm, inv_mm, t_mm, x_mm = sem("st_mm"), sem("tok_mm"), sem("inv_mm"), sem("t_mm"), sem("x_mm")
        msc_mm, rhs_mm, sa_mm, ys_mm = sem("msc_mm"), sem("rhs_mm"), sem("sa_mm"), sem("ys_mm")
        so_mm, gn_mm, g_mm = sem("so_mm"), sem("gn_mm"), sem("g_mm")
        proj_mm, ln_mm = sem("proj_mm"), sem("ln_mm")
        modt_mm = sem("modt_mm")
        logit_mm, logit_cp = sem("logit_mm"), sem("logit_cp")
        route_mm, utok_mm, rank_mm, hid_mm, down_mm = (sem("route_mm"), sem("utok_mm"), sem("rank_mm"),
                                                       sem("hid_mm"), sem("down_mm"))
        xg_mm, misc_mm, ht_mm, un_mm = sem("xg_mm"), sem("misc_mm"), sem("ht_mm"), sem("un_mm")
        tail_mm = sem("tail_mm")
        head_cp, cond_up, front_cp = sem("head_cp"), sem("cond_up"), sem("front_cp")
        kh_cp, ckt_cp, prob_up, pt_cp, o_cp = sem("kh_cp"), sem("ckt_cp"), sem("prob_up"), sem("pt_cp"), sem("o_cp")
        pool_cp, poolw_cp = sem("pool_cp"), sem("poolw_cp")
        edge_up, exp_up, st_cp, tok_cp, t_cp = sem("edge_up"), sem("exp_up"), sem("st_cp"), sem("tok_cp"), sem("t_cp")
        rhs_cp, sa_cp, so_cp = sem("rhs_cp"), sem("sa_cp"), sem("so_cp")
        gn_rt, gn_sq, ln_sq, ln_rt = sem("gn_rt"), sem("gn_sq"), sem("ln_sq"), sem("ln_rt")
        modr_cp, modt_cp = sem("modr_cp"), sem("modt_cp")
        gexp_up, e2_up, utok_cp, silu_up = sem("gexp_up"), sem("e2_up"), sem("utok_cp"), sem("silu_up")
        xg_cp, misc_cp, ht_cp, ys_cp = sem("xg_cp"), sem("misc_cp"), sem("ht_cp"), sem("ys_cp")
        tail_cp = sem("tail_cp")
        vec_step = sem("vec_step")
        set_up, mod_up, u_up = sem("set_up"), sem("mod_up"), sem("u_up")
        qk_sq, kk_sq, qk_up, qkr_up, max_up, pn_up = (sem("qk_sq"), sem("kk_sq"), sem("qk_up"), sem("qkr_up"),
                                                      sem("max_up"), sem("pn_up"))
        rot_up, inner_up = sem("rot_up"), sem("inner_up")
        rates_up, bonus_in, bonus_up = sem("rates_up"), sem("bonus_in"), sem("bonus_up")
        scaled_up, at_up, x_up, shat_up = sem("scaled_up"), sem("at_up"), sem("x_up"), sem("shat_up")
        msc_up, ys_up, state_up = sem("msc_up"), sem("ys_up"), sem("state_up")
        gn_c, mixa_up, z_up, xc_up = sem("gn_c"), sem("mixa_up"), sem("z_up"), sem("xc_up")
        d_up, onehot_up, sel_up, plan_up, hid_up, z2_up, h_up = (
            sem("d_up"), sem("onehot_up"), sem("sel_up"), sem("plan_up"), sem("hid_up"), sem("z2_up"), sem("h_up"))
        x_init = sem("x_init")

        def tiles(s):
            return ((0, 0), (1, 2), (2, 1))[s]

        def tc(t):
            return slice(t * P, (t + 1) * P)

        def both(m):
            return m.unsqueeze(2).broadcast_to([P, 2, 2, P])

        def n_par(l):
            return NPAR if l == 0 else COND

        X_ORDER = [(which, j) for which in range(2) for j in range(NJ)]

        def proj_bank(c):
            return bank[(6, 7, 0, 1)[c % 4]]

        def score_bank(i):
            return bank[(0, 1, 7)[i % 3]]

        def quad(ap):
            return ap.rearrange("p (d e) n -> p d e n", d=2)

        def bank4(b):
            return bank[b][:, :].rearrange("p (q n) -> p q n", q=4)

        XL = 2 * NJ * (LEVELS - 2) + NJ

        def xi(l, s, k, j, which):
            base = (l * 3 + s) * XL
            if k < LEVELS - 1:
                return base + (k - 1) * 2 * NJ + 2 * j + which + 1
            return base + (LEVELS - 2) * 2 * NJ + j + 1

        def used(n):
            kind, l, i = ORDER[n]
            if kind == "mod":
                return mod_mm, N_MOD * l + i + 1
            if kind == "in":
                return front_mm, FRONT * l + 3 * (i + 1) + 1 + (4 if i >= 3 else 0)
            if kind == "out":
                return proj_mm, KT * l + sum(OUT_TILES[:i + 1])
            job, i = divmod(i, JOB_ITEMS)
            jn = JOBS * l + job
            return (hid_mm, EPG * jn + i + 1) if i < EPG else (down_mm, 2 * jn + i - EPG + 1)

        def skip(eng, jn, per_job):
            for s, per in per_job:
                eng.wait_ge(s, per * jn)
                eng.sem_inc(s, per)

        def row(eng, at_row, n, src, cols=P, to=0, done=None):
            eng.dma_start(rows[at_row:at_row + n, :, to:to + cols],
                          src.rearrange("l (a b) -> a l b", b=cols)).then_inc(done or par_in, 16)

        block = ctx.enter_context(nc.Block())

        @block.sync
        def _(sp):
            def item(n, first_expert=None):
                kind, l, i = ORDER[n]
                slot = n % RING
                if n == 1:
                    sp.wait_ge(par_in, 16 * (N_PAR_DMAS - N_PAR2))
                if n >= RING:
                    sp.wait_ge(*used(n - RING))
                w = ring[:, slot, :]
                landed = slot_in[slot]

                def halves(dst, src):
                    k = dst.shape[1] // 2
                    sp.dma_start(dst[:, 0:k], src[:, 0:k]).then_inc(landed, 16)
                    sp.dma_start(dst[:, k:2 * k], src[:, k:2 * k]).then_inc(landed, 16)

                if kind == "mod":
                    halves(w.rearrange("p (c n) -> p c n", c=KT),
                           a["w_mod"][l].rearrange("(c p) n -> p c n", p=P)[:, :, i * 512:(i + 1) * 512])
                elif kind == "in" and i == 0:
                    lo, n_cols = IN_COLS[0]
                    dst = w.rearrange("p (c n) -> p c n", c=KT)
                    src = a["w_in"][l].rearrange("(c p) n -> p c n", p=P)[:, :, lo:lo + n_cols]
                    for hq in range(GRP * KVH):
                        to = P * (hq % GRP) + HD * (hq // GRP)
                        sp.dma_start(dst[:, :, to:to + HD], src[:, :, hq * HD:(hq + 1) * HD]).then_inc(landed, 16)
                    sp.dma_start(dst[:, :, T:n_cols], src[:, :, T:n_cols]).then_inc(landed, 16)
                elif kind == "in":
                    lo, n_cols = IN_COLS[i]
                    halves(w[:, 0:KT * n_cols].rearrange("p (c n) -> p c n", c=KT),
                           a["w_in"][l].rearrange("(c p) n -> p c n", p=P)[:, :, lo:lo + n_cols])
                elif kind == "out":
                    lo = P * sum(OUT_TILES[:i])
                    n_cols = P * OUT_TILES[i]
                    dst = w[:, 0:KT * n_cols].rearrange("p (c n) -> p c n", c=KT)
                    src = a["w_out"][l][:, lo:lo + n_cols]
                    sp.dma_start(dst[:, 0:NJ], src[0:NJ * P].rearrange("(c p) n -> p c n", p=P)).then_inc(landed, 16)
                    for g in range(KVH):
                        lo_r = NJ * P + g * GRP * HD
                        sp.dma_start(dst[g * HD:(g + 1) * HD, NJ:2 * NJ],
                                     src[lo_r:lo_r + GRP * HD].rearrange("(c p) n -> p c n", p=HD)).then_inc(landed, 16)
                    sp.dma_start(dst[:, 2 * NJ:KT],
                                 src[2 * NJ * P:D].rearrange("(c p) n -> p c n", p=P)).then_inc(landed, 16)
                else:
                    job, m = divmod(i, JOB_ITEMS)
                    e0 = EPG * job if first_expert is None else first_expert
                    if m < EPG:
                        dst = w.rearrange("p (c n) -> p c n", c=KT)
                        for half, name in enumerate(("moe_w1", "moe_w3")):
                            sp.dma_start(dst[:, :, half * DE:(half + 1) * DE],
                                         expert(name, l, e0 + m).rearrange("(c p) n -> p c n", p=P)).then_inc(landed, 16)
                    else:
                        for k in range(2):
                            sp.dma_start(w[:, 2048 * k:2048 * (k + 1)].rearrange("p (f n) -> p f n", f=2),
                                         expert("moe_w2", l, e0 + 2 * (m - EPG) + k).rearrange("(f p) n -> p f n", p=P)
                                         ).then_inc(landed, 16)

            def expert(name, l, e):
                if isinstance(e, int):
                    return a[name][l, e]
                return a[name][l, bass.ds(e, 1)].rearrange("o r n -> (o r) n")

            n = 0
            while n < len(ORDER):
                kind, l, i = ORDER[n]
                if kind != "job" or i < OVER * JOB_ITEMS:
                    item(n)
                    n += 1
                    continue
                over = i // JOB_ITEMS - OVER
                if over == 0:
                    sp.wait_ge(plan_up, l + 1)
                count = sp.value_load(plan[0:1, 0:1], min_val=0, max_val=2)
                with sp.If(count > over):
                    e0 = sp.value_load(plan[0:1, 1 + over:2 + over], min_val=0, max_val=NE - EPG)
                    for m in range(JOB_ITEMS):
                        item(n + m, e0)
                with sp.Else():
                    for m in range(JOB_ITEMS):
                        slot = slot_in[(n + m) % RING]
                        sp.wait_ge(slot, landed_value(n + m - RING))
                        sp.sem_inc(slot, landed_value(n + m) - landed_value(n + m - RING))
                n += JOB_ITEMS

        @block.gpsimd
        def _(pool):
            row(pool, W0, 6, a["rw_w0"].rearrange("l d c -> l (d c)"), done=par2_in)
            row(pool, A0, 6, a["rw_a0"].rearrange("l d c -> l (d c)"), done=par2_in)
            row(pool, KKP, NJ, a["rw_kk"], done=par2_in)
            row(pool, KAP, NJ, a["rw_ka"], done=par2_in)
            row(pool, RKP, NJ, a["rw_rk"].rearrange("l h c -> l (h c)"), done=par2_in)
            row(pool, GNG, NJ, a["rw_gn_g"], done=par2_in)
            row(pool, GNB, NJ, a["rw_gn_b"], done=par2_in)
            row(pool, PSC, 2, a["pool_scale"], done=par2_in)
            pool.wait_ge(par_in, 16 * (N_PAR_DMAS - N_PAR2))
            pool.dma_start(level, a["level"]).then_inc(level_in, 16)
            pool.wait_ge(mod_mm, 3)
            for l in range(DEPTH):
                if l > 0:
                    pool.wait_ge(route_mm, l)
                    pool.wait_ge(st_mm, 2 * l)
                for dst, name in ((lora_w2, "rw_w2"), (lora_a2, "rw_a2")):
                    pool.dma_start(dst[:, :], a[name][l].rearrange("d r c -> (d r) c")).then_inc(small_in, 16)
                pool.dma_start(lora_g2[:, :], a["rw_g2"][l]).then_inc(small_in, 16)
                pool.dma_start(pool_w[:, :, :],
                               a["pool_w"][l].rearrange("(t g) c d -> t (g c) d", t=2).rearrange("t p d -> p t d")
                               ).then_inc(small_in, 16)
                pool.dma_start(route_w[:, :, 0:NG], a["rt_grp_w"][l].rearrange("(c p) n -> p c n", p=P)).then_inc(small_in, 16)
                pool.dma_start(route_w[:, :, NG:20], a["rt_exp_w"][l].rearrange("(c p) n -> p c n", p=P)).then_inc(small_in, 16)
                pool.dma_start(route_b[:, 0:NG], a["rt_grp_b"][l:l + 1, :]).then_inc(small_in, 16)
                pool.dma_start(route_b[:, NG:20], a["rt_exp_b"][l:l + 1, :]).then_inc(small_in, 16)
                pool.dma_start(ctx_k[:, :], a["cache_k"][0, l].rearrange("t h c -> t (h c)")).then_inc(small_in, 16)
                pool.dma_start(ctx_v[:, :], a["cache_v"][0, l].rearrange("t h c -> t (h c)")).then_inc(small_in, 16)
                if l == 0:
                    pool.wait_ge(set_up, 1)
                for d in range(2):
                    for e in range(2):
                        src = a["state_rwkv"][0, l, d].rearrange("(j e) v k -> e v j k", e=2)[e]
                        pool.dma_start(state_nat[e * HD:(e + 1) * HD, :, d, e * HD:(e + 1) * HD], src).then_inc(small_in, 16)
                pool.wait_ge(u_up, 2 * KT * l + KT)
                pool.dma_start(bands, a["bands"]).then_inc(bands_in, 16)
                pool.wait_ge(front_cp, FRONT * l + 5)
                pool.dma_start(new_v[0, l].rearrange("t h c -> t (h c)"), vp[:, 0, 0:P]).then_inc(v_out, 16)
                pool.wait_ge(kh_cp, l + 1)
                pool.dma_start(new_k[0, l].rearrange("t h c -> t (h c)"), kh_out).then_inc(k_out, 16)
                for s in range(3):
                    n = l * 3 + s
                    if s == 0:
                        pool.wait_ge(bonus_in, NJ * (l + 1))
                    else:
                        pool.wait_ge(t_mm, NJ * (LEVELS - 1) * n)
                    for which, j in X_ORDER:
                        if s == 0 and (which, j) == (1, 0):
                            pool.wait_ge(poolw_cp, 2 * (l + 1))
                            pool.wait_ge(bonus_up, NJ * (l + 1))
                            pool.wait_ge(v_out, 16 * (l + 1))
                            pool.wait_ge(k_out, 16 * (l + 1))
                        if s > 0 and which == 1:
                            pool.wait_ge(sa_mm, NJ * (n - 1) + j + 1)
                        pool.tensor_copy((x_m, xt_m)[which][:, j],
                                         ident.unsqueeze(1).broadcast_to([P, 4, P])).then_inc(x_init, 1)
                pool.wait_ge(so_cp, 2 * (l + 1))
                for d in range(2):
                    for e in range(2):
                        dst = new_state[0, l, d].rearrange("(j e) v k -> e v j k", e=2)[e]
                        pool.dma_start(dst, state_out[e * HD:(e + 1) * HD, :, d, e * HD:(e + 1) * HD]).then_inc(s_out, 16)
            pool.wait_ge(v_out, 16 * DEPTH)
            pool.wait_ge(k_out, 16 * DEPTH)
            pool.wait_ge(s_out, 64 * DEPTH)
            pool.wait_ge(y_out_s, 16 * NT)

        @block.tensor
        def _(pe):
            def item_in(kind, l, i):
                n = PLACE[kind, l, i]
                pe.wait_ge(slot_in[n % RING], landed_value(n))
                return ring[:, n % RING, :]

            def attention(l):
                def unit(i):
                    return i // AH, i % AH

                def scores(i):
                    t, hq = unit(i)
                    j, g = hq % GRP, hq // GRP
                    n = 18 * l + i
                    if i >= 3:
                        pe.wait_ge(prob_up, n - 2)
                        pe.wait_ge(max_up, n - 2)
                    dst = score_bank(i)
                    q = qk[g * HD:(g + 1) * HD, j, tc(t)]
                    if t == 0:
                        last = pe.matmul(dst[:, 0:P], q, qk[g * HD:(g + 1) * HD, 3, 0:P], start=True, stop=True)
                    else:
                        pe.matmul(dst[:, 0:DEC], q, qk[g * HD:(g + 1) * HD, 3, P:T], start=True, stop=True)
                        last = pe.matmul(dst[:, DEC:T], q, ckt[g * HD:(g + 1) * HD, :], start=True, stop=True)
                    last.then_inc(score_mm, 1)

                def turn(i):
                    t, _ = unit(i)
                    n = 18 * l + i
                    pe.wait_ge(pn_up, n + 1)
                    if i >= 2:
                        pe.wait_ge(pt_cp, n - 1)
                    for c in range(1 if t == 0 else 3):
                        last = pe.transpose(bank[2 + i % 2][:, tc(c)], prob[:, i % 2, tc(c)], ident)
                    last.then_inc(pt_mm, 1)

                def outs(i):
                    t, hq = unit(i)
                    j, g = hq % GRP, hq // GRP
                    n = 18 * l + i
                    pe.wait_ge(pt_cp, n + 1)
                    dst = bank[4 + t][g * HD:(g + 1) * HD, tc(j)]
                    if t == 0:
                        values = [vp[:, 0, g * HD:(g + 1) * HD]]
                    else:
                        values = [vp[:, 1, g * HD:(g + 1) * HD], vp[:, 2, g * HD:(g + 1) * HD],
                                  ctx_v[:, g * HD:(g + 1) * HD]]
                    for c, vals in enumerate(values):
                        last = pe.matmul(dst, vals, prob_t[:, i % 2, tc(c)], start=(c == 0), stop=(c == len(values) - 1))
                    last.then_inc(o_mm, 1)

                pe.wait_ge(qkr_up, l + 1)
                pe.wait_ge(modt_cp, N_MOD * (l + 1))
                pe.wait_ge(ckt_cp, l + 1)
                scores(0)
                for i in range(18 + 2):
                    if i + 1 < 18:
                        scores(i + 1)
                    if 1 <= i <= 18:
                        turn(i - 1)
                    if i == 17:
                        pooling(l)
                    if i >= 2:
                        outs(i - 2)

            def pooling(l):
                pe.wait_ge(o_cp, 3 * l + 2)
                pe.wait_ge(bands_in, 16 * (l + 1))
                for c in range(2):
                    for g in range(2):
                        dst = bank[4 + c][g * HD:(g + 1) * HD, :]
                        src = slice(P + (2 * c + g) * HD, P + (2 * c + g + 1) * HD)
                        pe.matmul(dst[:, 0:P], vp[:, 0, src], band_p[:, 2 * c + g, :], start=True, stop=True)
                        for k in range(2):
                            last = pe.matmul(dst[:, P:T], vp[:, 1 + k, src], band_s[:, 2 * (2 * c + g) + k, :],
                                             start=(k == 0), stop=(k == 1))
                    last.then_inc(pool_mm, 1)

            def pooling_out(l):
                for c in range(2):
                    pe.wait_ge(pool_cp, 2 * l + c + 1)
                    for g in range(2):
                        rows_g = slice(g * HD, (g + 1) * HD)
                        last = pe.matmul(bank[4 + c][rows_g, 0:T], pool_w[rows_g, c, :], pool_d[rows_g, c, :],
                                         start=True, stop=True)
                    last.then_inc(poolw_mm, 1)

            def rwkv_step(l, s):
                n = l * 3 + s
                if s == 0:
                    pe.wait_ge(poolw_cp, 2 * (l + 1))
                if s == 1:
                    pe.wait_ge(so_cp, 2 * (l + 1))
                    for d2 in range(2):
                        for q in range(3):
                            jd = 3 * d2 + q
                            last = pe.transpose(bank[6 + d2][:, tc(q)], state_nat[:, jd // 2, jd % 2, :], ident)
                        last.then_inc(st_mm, 1)
                def tok(g):
                    if g >= 2:
                        pe.wait_ge(tok_cp, 4 * n + g - 1)
                    for q in range(4 if g % 2 == 0 else 2):
                        jd = 4 * (g % 2) + q
                        last = pe.transpose(bank[6 + g % 2][:, tc(q)], scaled[:, 2 + g // 2, jd // 2, tc(jd % 2)], ident)
                    last.then_inc(tok_mm, 1)

                pe.wait_ge(scaled_up, 2 * n + 1)
                for j in range(NJ):
                    if j == 2 and n > 0:
                        pe.wait_ge(ys_up, NJ * n)
                    for q in range(4):
                        d = q % 2
                        for e in range(2):
                            rows_e = slice(e * HD, (e + 1) * HD)
                            al, be = scaled[rows_e, 1, j, tc(d)], scaled[rows_e, 2, j, tc(d)]
                            lhs, rhs = (al, be) if q < 2 else (be, al)
                            last = pe.matmul(bank[2 * j + e][:, tc(q)], lhs, rhs, start=True, stop=True)
                            if q == 3:
                                last.then_inc(inv_mm, 1)
                if s == 1:
                    pe.wait_ge(st_cp, 2 * (l + 1))
                tok(0)
                tok(1)
                for k in range(1, LEVELS):
                    if k == 2:
                        pe.wait_ge(tok_cp, 4 * (n + 1))
                    if l + 1 < DEPTH and k >= 2:
                        if k <= 5:
                            mod_rows(l + 1, 4 * s + k - 2)
                        if k >= 3:
                            mod_turn(l + 1, 4 * s + k - 3)
                    for j in range(NJ):
                        if k == 1:
                            pe.wait_ge(at_up, NJ * (n + 1))
                        else:
                            pe.wait_ge(x_up, xi(l, s, k - 1, j, 1))
                        for q in range(4):
                            last = pe.matmul(bank[j][:, tc(q)], at_m[:, j, q, :], x_m[:, j, q, :], start=True, stop=True)
                        last.then_inc(t_mm, 1)
                    if k == 1:
                        tok(2)
                        tok(3)
                    for j in range(NJ):
                        pe.wait_ge(t_cp, ((l * 3 + s) * (LEVELS - 1) + k - 1) * NJ + j + 1)
                        if k < LEVELS - 1:
                            for q in range(4):
                                last = pe.matmul(bank[j][:, tc(q)], xt_m[:, j, q, :], t_m[:, j, q, :], start=True, stop=True)
                            last.then_inc(x_mm, 1)
                        for q in range(4):
                            last = pe.matmul(bank[3 + j][:, tc(q)], t_m[:, j, q, :], xt_m[:, j, q, :], start=True, stop=True)
                        last.then_inc(x_mm, 1)

                if l + 1 < DEPTH:
                    pe.wait_ge(modt_cp, N_MOD * (l + 1) + 4 * (s + 1))

                def masked(j):
                    if j == 0:
                        pe.wait_ge(scaled_up, 2 * n + 2)
                        pe.wait_ge(x_up, xi(l, s, LEVELS - 1, NJ - 1, 1))
                    else:
                        pe.wait_ge(msc_up, 3 * (NJ * n + j))
                    for m, (kl, kr_) in enumerate(((3, 1), (2, 0), (3, 0))):
                        for d in range(2):
                            for e in range(2):
                                rows_e = slice(e * HD, (e + 1) * HD)
                                last = pe.matmul(bank[2 * (m // 2) + e][:, tc(2 * (m % 2) + d)],
                                                 scaled[rows_e, kl, j, tc(d)], scaled[rows_e, kr_, j, tc(d)],
                                                 start=True, stop=True)
                                if d == 1:
                                    last.then_inc(msc_mm, 1)

                def rhs_of(j):
                    pe.wait_ge(msc_up, 3 * (NJ * n + j) + 1)
                    pe.wait_ge(shat_up, n + 1)
                    if n * NJ + j > 0:
                        pe.wait_ge(rhs_cp, NJ * n + j)
                    for d in range(2):
                        t = tiles(s)[d]
                        pe.matmul(bank[6][:, tc(d)], scaled[:, 1, j, tc(d)], s_hat[:, j, d, :], start=True, stop=False,
                                  skip_group_check=True)
                        for e in range(2):
                            col = slice(d * P + e * HD, d * P + (e + 1) * HD)
                            last = pe.matmul(bank[6][:, col], masks_of[j][:, 0, 2 * d + e, :],
                                             v_tok[:, t, j * P + e * HD:j * P + (e + 1) * HD], start=False, stop=True,
                                             skip_group_check=True)
                    last.then_inc(rhs_mm, 1)

                def solve(j):
                    pe.wait_ge(rhs_cp, NJ * n + j + 1)
                    if n * NJ + j > 0:
                        pe.wait_ge(sa_cp, NJ * n + j)
                    for q in range(4):
                        col = slice(q * HD, (q + 1) * HD)
                        last = pe.matmul(bank[7][:, col], xt_m[:, j, q, :], r_s[:, col], start=True, stop=True)
                    last.then_inc(sa_mm, 1)

                def outputs(j):
                    b = 4 + j % 2
                    pe.wait_ge(sa_cp, NJ * n + j + 1)
                    pe.wait_ge(msc_up, 3 * (NJ * n + j) + 3)
                    if j == 2:
                        pe.wait_ge(ys_up, NJ * n + 1)
                    for d in range(2):
                        t = tiles(s)[d]
                        pe.matmul(bank[b][:, tc(d)], s_hat[:, j, d, :], scaled[:, 0, j, tc(d)], start=True, stop=False,
                                  skip_group_check=True)
                        for e in range(2):
                            rows_e = slice(e * HD, (e + 1) * HD)
                            pe.matmul(bank[b][rows_e, tc(d)], sa_s[:, d * P + e * HD:d * P + (e + 1) * HD],
                                      masks_of[j][:, 1, 2 * d + e, :], start=False, stop=False, skip_group_check=True)
                            pe.matmul(bank[b][rows_e, tc(d)], v_tok[:, t, j * P + e * HD:j * P + (e + 1) * HD],
                                      masks_of[j][:, 2, 2 * d + e, :], start=False, stop=True, skip_group_check=True)
                        dst = bank[b][:, tc(2 + d)]
                        pe.matmul(dst, tok_m[:, 1, j, tc(d)], v_tok[:, t, tc(j)], start=True, stop=False,
                                  skip_group_check=True)
                        last = pe.matmul(dst, tok_m[:, 0, j, tc(d)], sa_s[:, tc(d)], start=False, stop=True,
                                         skip_group_check=True)
                    last.then_inc(ys_mm, 1)

                masked(0)
                rhs_of(0)
                masked(1)
                for j in range(NJ):
                    solve(j)
                    if j == 0:
                        masked(2)
                    if j + 1 < NJ:
                        rhs_of(j + 1)
                    outputs(j)
                if s == 0:
                    pe.wait_ge(state_up, NJ * n + NJ)
                    for d2 in range(2):
                        for q in range(3):
                            jd = 3 * d2 + q
                            last = pe.transpose(bank[6 + d2][:, tc(q)], s_t[:, jd // 2, jd % 2, :], ident)
                        last.then_inc(so_mm, 1)

            def mod_rows(l, i, dst=bank[6]):
                m = N_MOD * l + i
                w = item_in("mod", l, i).rearrange("p (c n) -> p c n", c=KT)
                if m > 0:
                    pe.wait_ge(modr_cp, m)
                for c in range(KT):
                    for q in range(4):
                        last = pe.matmul(dst[CTILE * q:CTILE * (q + 1), 0:P], cond[:, c, :], w[:, c, tc(q)],
                                         start=(c == 0), stop=(c == KT - 1))
                last.then_inc(mod_mm, 1)

            def mod_turn(l, i, lo=0):
                m = N_MOD * l + i
                pe.wait_ge(modr_cp, m + 1)
                if m > 0:
                    pe.wait_ge(modt_cp, m)
                pe.transpose(bank[7][:, lo:lo + P], mod_row[:, :], ident).then_inc(modt_mm, 1)

            def norm_sums(l, which, ready, per):
                src = h if which == 0 else sq
                for c in range(KT):
                    pe.wait_ge(ready, per(c))
                    last = pe.matmul(bank[4 + which][:, 0:T], ones_d, src[:, c, :], start=(c == 0), stop=(c == KT - 1))
                last.then_inc(ln_mm, 1)

            pe.wait_ge(cst_in, 16)
            pe.wait_ge(par_in, 16 * (N_PAR_DMAS - N_PAR2))
            pe.wait_ge(par2_in, 16 * N_PAR2)
            for l in range(DEPTH):
                pe.transpose(bank[l][:, 0:n_par(l)], rows[0:n_par(l), l, :],
                             ident[0:n_par(l), 0:n_par(l)]).then_inc(head_mm, 1)
            pe.wait_ge(x_in_s, 16 * NT)
            for t in range(NT):
                for half in range(2):
                    for q in range(4):
                        last = pe.transpose(bank[2 + 2 * t + half][:, tc(q)], x_in[:, t, tc(4 * half + q)], ident)
                    last.then_inc(head_mm, 1)

            for l in range(DEPTH):
                if l == 0:
                    pe.wait_ge(cond_up, 1)
                    pe.wait_ge(head_cp, 8)
                    for i in range(MOD_FIRST + 1):
                        if i < MOD_FIRST:
                            mod_rows(0, i)
                        if i >= 1:
                            mod_turn(0, i - 1)
                n_front = [0]

                def front_bank():
                    n = FRONT * l + n_front[0]
                    b = n_front[0] % 7
                    if n_front[0] == 6 and l == 0:
                        pe.wait_ge(modr_cp, MOD_FIRST)
                    if n_front[0] >= 7:
                        pe.wait_ge(front_cp, n - 6)
                    n_front[0] += 1
                    return bank[b]

                for i in range(len(IN_COLS)):
                    n_cols = IN_COLS[i][1]
                    w = item_in("in", l, i)[:, 0:KT * n_cols].rearrange("p (c n) -> p c n", c=KT)
                    if i == 0:
                        tiles_0 = [front_bank() for m in range(4)]
                        for c in range(KT):
                            pe.wait_ge(u_up, 2 * KT * l + c + 1)
                            for m in range(4):
                                last_c = pe.matmul(tiles_0[m][:, 0:T], w[:, c, tc(m)], u[:, c, :],
                                                   start=(c == 0), stop=(c == KT - 1))
                                if c == KT - 1:
                                    last_c.then_inc(front_mm, 1)
                        if l == 0:
                            pe.wait_ge(modt_cp, MOD_FIRST)
                            mod_rows(0, MOD_FIRST, bank[7])
                            mod_turn(0, MOD_FIRST, P)
                    for m in range(0 if i == 0 else 3):
                        if l == 0 and m == 1:
                            if i == 3:
                                pe.wait_ge(ckt_cp, 1)
                            if i == 4:
                                pe.wait_ge(kh_cp, 1)
                            if i == 5:
                                pe.wait_ge(rot_up, 1)
                            pe.wait_ge(modt_cp, MOD_FIRST + i)
                            mod_rows(0, MOD_FIRST + i, bank[7])
                        if l == 0 and m == 2:
                            mod_turn(0, MOD_FIRST + i, P)
                        dst = front_bank()
                        for c in range(KT):
                            if i in (1, 2):
                                last_c = pe.matmul(dst[:, 0:n_cols], u[:, c, tc(m)], w[:, c, :],
                                                   start=(c == 0), stop=(c == KT - 1))
                            else:
                                last_c = pe.matmul(dst[:, 0:T], w[:, c, tc(m)], u[:, c, :],
                                                   start=(c == 0), stop=(c == KT - 1))
                        last_c.then_inc(front_mm, 1)
                    if l == 0:
                        pe.wait_ge(modt_cp, MOD_FIRST + i + 1)
                    if i == 2:
                        pe.wait_ge(qk_sq, l + 1)
                        for m in range(4):
                            dst = front_bank()
                            pe.matmul(dst[:, 0:T], head_ones, qk_s[:, m, :], start=True, stop=True).then_inc(front_mm, 1)
                        pe.wait_ge(small_in, 16 * SMALL * (l + 1))
                        pe.transpose(bank[7][:, 0:P], ctx_k[:, :], ident).then_inc(ckt_mm, 1)
                    if i == 3:
                        pe.wait_ge(qk_up, l + 1)
                        pe.wait_ge(ckt_cp, l + 1)
                        pe.transpose(bank[7][:, 0:P], qk[:, 3, 0:P], ident).then_inc(khead_mm, 1)
                    if i >= 4:
                        if i == 4:
                            pe.wait_ge(kh_cp, l + 1)
                        else:
                            pe.wait_ge(rot_up, 2 * l + 1)
                        for m in range(2):
                            last_c = pe.matmul(bank[7][:, m * DEC:(m + 1) * DEC], rot, qk[:, 2 * (i - 4) + m, P:T],
                                               start=True, stop=True)
                        last_c.then_inc(rot_mm, 1)
                for d in range(2):
                    if l == 0:
                        pe.wait_ge(rot_up, 2)
                        pe.wait_ge(modt_cp, MOD_FIRST + len(IN_COLS) + d)
                        mod_rows(0, MOD_FIRST + len(IN_COLS) + d, bank[7])
                    for j in range(NJ):
                        if l == 0 and j == 1:
                            mod_turn(0, MOD_FIRST + len(IN_COLS) + d, P)
                        for w2, lo in ((lora_w2, lo_w), (lora_a2, lo_a)):
                            dst = front_bank()
                            pe.wait_ge(front_cp, FRONT * l + 16)
                            pe.matmul(dst[:, 0:T], w2[d * HD:(d + 1) * HD, tc(j)], lo[d * HD:(d + 1) * HD, :],
                                      start=True, stop=True).then_inc(front_mm, 1)
                pe.wait_ge(kk_sq, l + 1)
                for j in range(NJ):
                    dst = front_bank()
                    pe.matmul(dst[:, 0:T], head_ones, kr[:, j, :], start=True, stop=True).then_inc(front_mm, 1)
                for j in range(NJ):
                    dst = front_bank()
                    for t in range(NT):
                        last = pe.transpose(dst[:, tc(t)], v_tok[:, t, tc(j)], ident)
                    last.then_inc(front_mm, 1)
                pe.wait_ge(front_cp, FRONT * (l + 1))
                attention(l)
                pooling_out(l)
                pe.wait_ge(bonus_in, NJ * (l + 1))
                for j in range(NJ):
                    pe.matmul(bank[j][:, 0:T], head_ones, kr[:, j, :], start=True, stop=True).then_inc(bonus_mm, 1)
                pe.wait_ge(bonus_up, NJ * (l + 1))
                for s in range(3):
                    rwkv_step(l, s)
                pe.wait_ge(state_up, NJ * 3 * (l + 1))
                for j in range(NJ):
                    pe.matmul(bank[j][:, 0:T], head_ones, y_t[:, j, :], start=True, stop=True).then_inc(gn_mm, 1)
                for j in range(NJ):
                    pe.matmul(bank[3 + j][:, 0:T], lora_g2[:, tc(j)], lo_g, start=True, stop=True).then_inc(g_mm, 1)
                for j in range(NJ):
                    pe.wait_ge(gn_sq, NJ * l + j + 1)
                    pe.matmul(bank[j][:, 0:T], head_ones, gn_s[:, j, :], start=True, stop=True).then_inc(gn_mm, 1)
                pe.wait_ge(poolw_cp, 2 * (l + 1))

                def project(i, m, cs):
                    dst = proj_bank(sum(OUT_TILES[:i]) + m)
                    w = ring[:, PLACE["out", l, i] % RING, 0:KT * P * OUT_TILES[i]].rearrange("p (c n) -> p c n", c=KT)
                    for c in cs:
                        last = pe.matmul(dst[:, 0:T], w[:, c, tc(m)], mixed[:, c, :], start=(c == NJ),
                                         stop=(c == NJ - 1), skip_group_check=True)
                    return last

                others = list(range(NJ, KT))
                item_in("out", l, 0)
                for m in range(2):
                    project(0, m, others)
                pe.wait_ge(mixa_up, NJ * (l + 1))
                dt = 0
                for i in range(len(OUT_TILES)):
                    item_in("out", l, i)
                    for m in range(OUT_TILES[i]):
                        if dt >= 4:
                            pe.wait_ge(z_up, KT * l + dt - 3)
                        project(i, m, ([] if dt < 2 else others) + list(range(NJ))).then_inc(proj_mm, 1)
                        dt += 1
                norm_sums(l, 0, z_up, lambda c: KT * l + c + 1)
                norm_sums(l, 1, ln_sq, lambda c: KT * (2 * l) + c + 1)
                for c in range(KT):
                    pe.wait_ge(u_up, 2 * KT * l + KT + c + 1)
                    last = pe.matmul(bank[7][0:20, 0:T], route_w[:, c, :], u[:, c, :], start=(c == 0), stop=(c == KT - 1))
                last.then_inc(logit_mm, 1)
                pe.wait_ge(logit_cp, l + 1)
                for t in range(NT):
                    dst = bank[7][:, t * 20:(t + 1) * 20]
                    pe.matmul(dst, logits[:, tc(t)], ident[0:20, 0:20], start=True, stop=False)
                    last = pe.matmul(dst, ones_row, route_b[:, :], start=False, stop=True)
                last.then_inc(route_mm, 1)

                for g in range(2 * NT):
                    t, half = g // 2, g % 2
                    for q in range(4):
                        last = pe.transpose(bank[g][:, tc(q)], u[:, 4 * half + q, tc(t)], ident)
                    last.then_inc(utok_mm, 1)
                pe.wait_ge(onehot_up, l + 1)
                for t in range(NT + 1):
                    dst = bank[6][:, 4 * t:4 * t + 4]
                    parts = [(strict[:, 0, :], t)] if t < NT else []
                    for before in range(t):
                        parts += [(incl[:, 0, :], before), (strict[:, 1, :], before)]
                    for i, (ones, of) in enumerate(parts):
                        last = pe.matmul(dst, ones, group_1h[:, of, :], start=(i == 0), stop=(i == len(parts) - 1))
                last.then_inc(rank_mm, 1)

                def prepare(job):
                    jn, b = JOBS * l + job, job % 2
                    pe.wait_ge(sel_up, jn + 1)
                    pe.wait_ge(z2_up, KT * (jn - 1 if job in (1, 2, 3) else jn))
                    for c in range(KT):
                        for t in range(NT):
                            last = pe.matmul(bank[2 + c // 4][:, tc(c % 4)], u_tok[:, t, tc(c)], sel[:, b, t, :],
                                             start=(t == 0), stop=(t == NT - 1))
                        if c % 4 == 3:
                            last.then_inc(xg_mm, 1)
                    pe.wait_ge(misc_cp, jn)
                    for t in range(NT):
                        pe.transpose(bank[7][:, tc(t)], sel[:, b, t, :], ident)
                    pe.wait_ge(inner_up, l + 1)
                    for t in range(NT):
                        last = pe.matmul(bank[7][:, T:T + EPG], sel[:, b, t, :], inner[:, t, :],
                                         start=(t == 0), stop=(t == NT - 1))
                    last.then_inc(misc_mm, 1)

                def hidden(job, j):
                    jn = JOBS * l + job
                    w = item_in("job", l, JOB_ITEMS * job + j).rearrange("p (c n) -> p c n", c=KT)
                    if j == 0:
                        pe.wait_ge(xg_cp, 2 * jn + 2)
                    if EPG * jn + j >= 2:
                        pe.wait_ge(hid_up, EPG * jn + j - 1)
                    for c in range(KT):
                        last = pe.matmul(bank[j % 2][:, :], xs[:, job % 2, c, :], w[:, c, :],
                                         start=(c == 0), stop=(c == KT - 1))
                    last.then_inc(hid_mm, 1)

                def turn(job, j):
                    n = EPG * (JOBS * l + job) + j
                    pe.wait_ge(hid_up, n + 1)
                    if n > 0:
                        pe.wait_ge(ht_cp, n)
                    for f in range(2):
                        last = pe.transpose(bank[4][:, tc(f)], hs[:, j % 2, tc(f)], ident)
                    last.then_inc(ht_mm, 1)

                def down(job):
                    jn = JOBS * l + job
                    pe.wait_ge(ys_cp, 2 * jn)
                    for pair in range(2):
                        w = item_in("job", l, JOB_ITEMS * job + EPG + pair).rearrange("p (f n) -> p f n", f=4)
                        pe.wait_ge(ht_cp, EPG * jn + 2 * pair + 2)
                        for f in range(4):
                            for half in range(2):
                                last = pe.matmul(bank[5 + half][:, :], hid[:, job % 2, 4 * pair + f, :],
                                                 w[:, f, 512 * half:512 * half + 512],
                                                 start=(pair == 0 and f == 0), stop=(pair == 1 and f == 3))
                        last.then_inc(down_mm, 1)

                def scatter(job, prepared):
                    jn = JOBS * l + job
                    pe.wait_ge(ys_cp, 2 * jn + 2)
                    pe.wait_ge(misc_cp, jn + 1)
                    pe.wait_ge(xg_cp, 2 * (JOBS * l + prepared))
                    for c in range(KT):
                        if c >= 2:
                            pe.wait_ge(z2_up, KT * jn + c - 1)
                        pe.matmul(bank[2 + c % 2][:, 0:T], ys[:, tc(c)], sel_t[:, job % 2, :],
                                  start=True, stop=True).then_inc(un_mm, 1)

                pe.wait_ge(utok_cp, 2 * NT * (l + 1))
                prepare(0)
                for job in range(NG):
                    hidden(job, 0)
                    if job > 0:
                        scatter(job - 1, job + 1)
                    for j in range(1, EPG):
                        hidden(job, j)
                        turn(job, j - 1)
                    if job + 1 < NG:
                        prepare(job + 1)
                    turn(job, EPG - 1)
                    down(job)
                scatter(NG - 1, NG)
                pe.wait_ge(plan_up, l + 1)
                count = pe.value_load(plan[0:1, 0:1], min_val=0, max_val=2)
                for over in range(2):
                    job = OVER + over
                    with pe.If(count > over):
                        prepare(job)
                        for j in range(EPG):
                            hidden(job, j)
                            turn(job, j)
                        down(job)
                        scatter(job, job + 1)
                    with pe.Else():
                        skip(pe, JOBS * l + job, ((xg_mm, 2), (misc_mm, 1), (hid_mm, EPG), (ht_mm, EPG),
                                                  (down_mm, 2), (un_mm, KT)))
                norm_sums(l, 0, z2_up, lambda c: KT * JOBS * (l + 1))
                norm_sums(l, 1, ln_sq, lambda c: KT * (2 * l + 1) + c + 1)
            pe.wait_ge(h_up, KT * 2 * DEPTH)
            for t in range(NT):
                for half in range(2):
                    for q in range(4):
                        last = pe.transpose(bank[2 * t + half][:, tc(q)], h[:, 4 * half + q, tc(t)], ident)
                    last.then_inc(tail_mm, 1)

        @block.scalar
        def _(act):
            def copy(dst, src):
                return act.activation(dst, src, ACT.Copy)

            act.dma_start(cst[:, :], a["mats"]).then_inc(cst_in, 16)
            for s, name in enumerate(("c_ctx", "c")):
                src = a[name].rearrange("(k p) -> k p", p=P) if s == 0 else a[name][0].rearrange("(k p) -> k p", p=P)
                act.dma_start(rows[COND + KT * s:COND + KT * (s + 1), 0, :], src).then_inc(par_in, 16)
            row(act, BMOD, 48, a["b_mod"])
            for at_row, name in ((LN1G, "ln1_g"), (LN1B, "ln1_b"), (LN2G, "ln2_g"), (LN2B, "ln2_b")):
                row(act, at_row, KT, a[name])
            for at_row, name in ((QN, "q_norm"), (KN, "k_norm")):
                for e in range(2):
                    row(act, at_row, 1, a[name], HD, e * HD)
            for t in range(NT):
                src = a["x_prompt"][0] if t == 0 else a["x_sample"][0, (t - 1) * P:t * P]
                act.dma_start(x_in[:, t, :], src).then_inc(x_in_s, 16)
            def parameters(l):
                act.wait_ge(head_mm, l + 1)
                copy(par[:, l, 0:n_par(l)], bank[l][:, 0:n_par(l)]).then_inc(head_cp, 1)

            parameters(0)
            act.wait_ge(head_cp, 1)
            for k in range(KT):
                both_conds = par[:, 0, COND:COND + 2 * KT].rearrange("p (s k) -> p k s", s=2)[:, k, :].unsqueeze(1).broadcast_to([P, CTILE // 2, 2])
                last = act.activation(cond[:, k, :].rearrange("p (r s) -> p r s", s=2), both_conds, ACT.Silu)
            last.then_inc(cond_up, 1)
            for l in range(1, DEPTH):
                parameters(l)
            for g in range(2 * NT):
                t, half = g // 2, g % 2
                act.wait_ge(head_mm, DEPTH + g + 1)
                copy(h[:, 4 * half:4 * half + 4, tc(t)], bank4(2 + g)).then_inc(head_cp, 1)
            act.wait_ge(set_up, 1)

            def mod_rows(l, i, src=bank[6]):
                act.wait_ge(mod_mm, N_MOD * l + i + 1)
                if N_MOD * l + i > 0:
                    act.wait_ge(modt_mm, N_MOD * l + i)
                copy(mod_row[:, :], src[:, 0:P]).then_inc(modr_cp, 1)

            def mod_turned(l, i, lo=0):
                act.wait_ge(modt_mm, N_MOD * l + i + 1)
                if l > 0:
                    act.wait_ge(mod_up, l)
                copy(mod_raw[:, 4 * i:4 * i + 4, :],
                     bank[7][:, lo:lo + P].rearrange("p (m s) -> p m s", m=4)[:, :, 0:2]).then_inc(modt_cp, 1)

            for i in range(MOD_FIRST):
                mod_rows(0, i)
                mod_turned(0, i)

            def front(l):
                def arrived(n):
                    act.wait_ge(front_mm, FRONT * l + n + 1)
                    return bank[n % 7][:, 0:T]

                n = 0

                def rest_of_mod(k, m):
                    if l == 0 and m == 1:
                        mod_rows(0, MOD_FIRST + k, bank[7])
                    if l == 0 and m == 2:
                        mod_turned(0, MOD_FIRST + k, P)

                def evacuate(k, jobs):
                    nonlocal n
                    for m, (dst, func) in enumerate(jobs):
                        rest_of_mod(k, m)
                        act.activation(dst, arrived(n), func).then_inc(front_cp, 1)
                        n += 1

                evacuate(0, [(qk[:, m, :], ACT.Copy) for m in range(4)])
                evacuate(1, [(vp[:, t, :], ACT.Copy) for t in range(NT)])
                evacuate(2, [(v_tok[:, t, :], ACT.Copy) for t in range(NT)])
                for m in range(4):
                    act.activation(rs[:, m, :], arrived(n), ACT.Sqrt, bias=eps[:, 0:1], scale=1.0 / HD).then_inc(front_cp, 1)
                    n += 1
                act.wait_ge(ckt_mm, l + 1)
                copy(ckt, bank[7][:, 0:P]).then_inc(ckt_cp, 1)
                evacuate(3, [(lo_w, ACT.Tanh), (lo_a, ACT.Copy), (lo_g, ACT.Sigmoid)])
                act.wait_ge(khead_mm, l + 1)
                copy(kh_out, bank[7][:, 0:P]).then_inc(kh_cp, 1)
                evacuate(4, [(r_t[:, j, :], ACT.Copy) for j in range(NJ)])
                evacuate(5, [(k_t[:, j, :], ACT.Copy) for j in range(NJ)])
                for d in range(2):
                    rest_of_mod(len(IN_COLS) + d, 1)
                    for j in range(NJ):
                        rest_of_mod(len(IN_COLS) + d, j + 1 if j else 0)
                        for dst, col in ((rate, W0), (b_t, A0)):
                            act.activation(dst[:, d, j, :], arrived(n), ACT.Sigmoid,
                                           bias=par[:, l, col + 3 * d + j:col + 3 * d + j + 1]).then_inc(front_cp, 1)
                            n += 1
                for j in range(NJ):
                    act.activation(y_t[:, j, :], arrived(n), ACT.Sqrt).then_inc(front_cp, 1)
                    n += 1
                for j in range(NJ):
                    copy(v_t[:, j, :], arrived(n)).then_inc(front_cp, 1)
                    n += 1

            def attention(l):
                def width(i):
                    return P if i < AH else T

                def exps(i):
                    n = 18 * l + i
                    act.wait_ge(max_up, n + 1)
                    if i >= 2:
                        act.wait_ge(pt_mm, n - 1)
                    act.activation(prob[:, i % 2, 0:width(i)], score_bank(i)[:, 0:width(i)], ACT.Exp,
                                   bias=stat[:, 0, i:i + 1], scale=HD ** -0.5,
                                   accum_out=stat[:, 1, i:i + 1]).then_inc(prob_up, 1)

                def turned(i):
                    n = 18 * l + i
                    act.wait_ge(pt_mm, n + 1)
                    if i >= 2:
                        act.wait_ge(o_mm, n - 1)
                    copy(prob_t[:, i % 2, 0:width(i)], bank[2 + i % 2][:, 0:width(i)]).then_inc(pt_cp, 1)

                def heads(t):
                    act.wait_ge(o_mm, 18 * l + AH * (t + 1))
                    copy(mixed[:, NJ:2 * NJ, tc(t)],
                         bank[4 + t][:, 0:T].rearrange("p (j n) -> p j n", j=NJ)).then_inc(o_cp, 1)

                for i in range(19):
                    if i < 18:
                        exps(i)
                    if i >= 1:
                        turned(i - 1)
                    if i >= 7 and (i - 7) % AH == 0:
                        heads((i - 7) // AH)
                for c in range(2):
                    act.wait_ge(pool_mm, 2 * l + c + 1)
                    copy(pool_d[:, c, :], bank[4 + c][:, 0:T]).then_inc(pool_cp, 1)
                heads(2)

            def exps(s, kinds):
                for d in range(2):
                    runs = run[:, 9 * d:9 * d + 9, :].rearrange("p (j t) n -> p j t n", j=NJ)[:, :, tiles(s)[d], :]
                    for kind in kinds:
                        with_t, sign = (((1, -1), (0, -1), (1, 1)), ((0, 1), (1, 1), (0, -1)))[d][kind]
                        act.activation(scaled[:, kind, :, tc(d)], runs[:, :, with_t:with_t + P], ACT.Exp,
                                       scale=sign * DECAY).then_inc(exp_up, 1)

            def rwkv_step(l, s):
                n = l * 3 + s
                if s == 0:
                    exps(s, (2, 1))
                else:
                    act.wait_ge(ys_mm, NJ * n)
                exps(s, (0,))
                if s == 1:
                    for d2 in range(2):
                        act.wait_ge(st_mm, 2 * l + d2 + 1)
                        copy(s_t.rearrange("p j d n -> p (j d) n")[:, 3 * d2:3 * d2 + 3, :],
                             bank4(6 + d2)[:, 0:3, :]).then_inc(st_cp, 1)

                def tok(g):
                    w = 4 if g % 2 == 0 else 2
                    act.wait_ge(tok_mm, 4 * n + g + 1)
                    copy(tok_m[:, g // 2].rearrange("p j n -> p (j n)")[:, 512 * (g % 2):512 * (g % 2) + w * P],
                         bank[6 + g % 2][:, 0:w * P]).then_inc(tok_cp, 1)

                tok(0)
                tok(1)
                for k in range(1, LEVELS):
                    if l + 1 < DEPTH and k >= 2:
                        if k <= 5:
                            mod_rows(l + 1, 4 * s + k - 2)
                        if k >= 3:
                            mod_turned(l + 1, 4 * s + k - 3)
                    for j in range(NJ):
                        act.wait_ge(t_mm, (n * (LEVELS - 1) + k - 1) * NJ + j + 1)
                        copy(t_m[:, j], bank4(j)).then_inc(t_cp, 1)
                    if k == 1:
                        tok(2)
                        tok(3)
                for j in range(NJ):
                    act.wait_ge(rhs_mm, NJ * n + j + 1)
                    copy(r_s, bank[6][:, 0:2 * P]).then_inc(rhs_cp, 1)
                    act.wait_ge(sa_mm, NJ * n + j + 1)
                    copy(sa_s, bank[7][:, 0:2 * P]).then_inc(sa_cp, 1)
                if s < 2:
                    exps(s + 1, (2, 1))
                if s == 0:
                    if l > 0:
                        act.wait_ge(s_out, 64 * l)
                    for d2 in range(2):
                        act.wait_ge(so_mm, 2 * l + d2 + 1)
                        copy(state_out[:, :, :, :].rearrange("p j d n -> p (j d) n")[:, 3 * d2:3 * d2 + 3, :],
                             bank4(6 + d2)[:, 0:3, :]).then_inc(so_cp, 1)

            def norm(l, which):
                n = 2 * l + which
                for c in range(KT):
                    act.wait_ge(xc_up, KT * n + c + 1)
                    act.activation(sq[:, c, :], h[:, c, :], ACT.Square).then_inc(ln_sq, 1)
                act.wait_ge(ln_mm, 2 * n + 2)
                act.activation(rstd, bank[5][:, 0:T], ACT.Sqrt, bias=eps[:, 2:3]).then_inc(ln_rt, 1)

            for l in range(DEPTH):
                front(l)
                attention(l)
                for c in range(2):
                    act.wait_ge(poolw_mm, 2 * l + c + 1)
                    act.activation(mixed[:, 2 * NJ + c, :], bank[4 + c][:, 0:T], ACT.Copy,
                                   scale=par[:, l, PSC + c:PSC + c + 1]).then_inc(poolw_cp, 1)
                act.wait_ge(rates_up, 2 * NJ * (l + 1))
                act.activation(edge, centre, ACT.Exp, scale=-DECAY).then_inc(edge_up, 1)
                act.wait_ge(bonus_up, NJ * (l + 1))
                act.wait_ge(v_out, 16 * (l + 1))
                act.wait_ge(k_out, 16 * (l + 1))
                for s in range(3):
                    rwkv_step(l, s)
                for j in range(NJ):
                    act.wait_ge(gn_c, NJ * l + j + 1)
                    act.activation(gn_s[:, j, :], y_t[:, j, :], ACT.Square).then_inc(gn_sq, 1)
                for j in range(NJ):
                    act.wait_ge(gn_mm, 2 * NJ * l + NJ + j + 1)
                    act.activation(gn_r[:, j, :], bank[j][:, 0:T], ACT.Sqrt, bias=eps[:, 1:2],
                                   scale=1.0 / HD).then_inc(gn_rt, 1)
                norm(l, 0)
                act.wait_ge(logit_mm, l + 1)
                copy(logits, bank[7][0:20, 0:T]).then_inc(logit_cp, 1)
                for g in range(2 * NT):
                    t, half = g // 2, g % 2
                    act.wait_ge(utok_mm, 2 * NT * l + g + 1)
                    copy(u_tok[:, t, 512 * half:512 * half + 512], bank[g][:, :]).then_inc(utok_cp, 1)
                act.wait_ge(d_up, 2 * l + 1)
                act.activation(g4[1], g4[0], ACT.Exp).then_inc(gexp_up, 1)
                act.wait_ge(d_up, 2 * l + 2)
                act.activation(g1[1], g1[0], ACT.Exp).then_inc(e2_up, 1)


                def prepared(job):
                    jn, b = JOBS * l + job, job % 2
                    for half in range(2):
                        act.wait_ge(xg_mm, 2 * jn + half + 1)
                        copy(xs[:, b, 4 * half:4 * half + 4, :], bank4(2 + half)).then_inc(xg_cp, 1)
                    act.wait_ge(misc_mm, jn + 1)
                    copy(sel_t[:, b, :], bank[7][:, 0:T])
                    copy(gates[:, b, :], bank[7][:, T:T + EPG]).then_inc(misc_cp, 1)

                def hidden(job, j):
                    n = EPG * (JOBS * l + job) + j
                    act.wait_ge(hid_mm, n + 1)
                    if n >= 2:
                        act.wait_ge(hid_up, n - 1)
                    act.activation(silu[:, j % 2, :], bank[j % 2][:, 0:DE], ACT.Silu).then_inc(silu_up, 1)

                def turned(job, j):
                    act.wait_ge(ht_mm, EPG * (JOBS * l + job) + j + 1)
                    copy(hid[:, job % 2, 2 * j:2 * j + 2, :], bank4(4)[:, 0:2, :]).then_inc(ht_cp, 1)

                def down(job):
                    jn = JOBS * l + job
                    act.wait_ge(down_mm, 2 * jn + 2)
                    for half in range(2):
                        copy(ys[:, 512 * half:512 * half + 512], bank[5 + half][:, :]).then_inc(ys_cp, 1)

                prepared(0)
                for job in range(NG):
                    hidden(job, 0)
                    for j in range(1, EPG):
                        hidden(job, j)
                        turned(job, j - 1)
                    if job + 1 < NG:
                        prepared(job + 1)
                    turned(job, EPG - 1)
                    down(job)
                act.wait_ge(plan_up, l + 1)
                count = act.value_load(plan[0:1, 0:1], min_val=0, max_val=2)
                for over in range(2):
                    job = OVER + over
                    with act.If(count > over):
                        prepared(job)
                        for j in range(EPG):
                            hidden(job, j)
                            turned(job, j)
                        down(job)
                    with act.Else():
                        skip(act, JOBS * l + job, ((xg_cp, 2), (misc_cp, 1), (silu_up, EPG), (ht_cp, EPG), (ys_cp, 2)))
                norm(l, 1)
            for g in range(2 * NT):
                t, half = g // 2, g % 2
                act.wait_ge(tail_mm, g + 1)
                copy(y_out[:, t, 512 * half:512 * half + 512], bank[g][:, :]).then_inc(tail_cp, 1)
                if half == 1:
                    act.wait_ge(tail_cp, g + 1)
                    dst = y_prompt[0] if t == 0 else y_sample[0, (t - 1) * P:t * P]
                    act.dma_start(dst, y_out[:, t, :]).then_inc(y_out_s, 16)

        @block.vector
        def _(dve):
            steps = [0]

            def mark(ins):
                steps[0] += 1
                ins.then_inc(vec_step, 1)
                return steps[0]

            def after(n=None):
                dve.wait_ge(vec_step, steps[0] if n is None else n)

            def link(ins):
                mark(ins)
                after()

            tt, ts, stt = dve.tensor_tensor, dve.tensor_scalar, dve.scalar_tensor_tensor
            dve.memset(eps[:, 0:1], QK_EPS)
            dve.memset(eps[:, 1:2], GN_EPS)
            dve.memset(eps[:, 2:3], LN_EPS / ALPHA ** 2)
            dve.memset(state_nat[:, :, :, :], 0.0).then_inc(set_up, 1)
            dve.wait_ge(level_in, 16)
            link(dve.tensor_copy(lev[:, :, :, :].rearrange("p a b n -> p (a b n)"), level))

            def finish_mod(l, lo, hi):
                link(tt(mod[:, lo:hi, :], mod_raw[:, lo:hi, :],
                        par[:, l, lo:hi].unsqueeze(2).broadcast_to([P, hi - lo, 2]), ALU.add))
                for base in (0, 24):
                    if lo <= base + 8 < hi:
                        mark(ts(mod[:, base + 8:base + 16, :], mod[:, base + 8:base + 16, :], 1.0, None, ALU.add))
                    if lo <= base + 16 < hi:
                        mark(ts(mod[:, base + 16:base + 24, :], mod[:, base + 16:base + 24, :], 1.0 / ALPHA, None, ALU.mult))
                after()
                if hi == 48:
                    dve.sem_inc(mod_up, 1)

            def modulate(l):
                base = 0
                for c in range(KT):
                    for g, (lo, hi) in enumerate(STREAMS):
                        last = ts(u[:, c, lo:hi], h[:, c, lo:hi], mod[:, base + 8 + c, g:g + 1],
                                  mod[:, base + c, g:g + 1], ALU.mult, ALU.add)
                    last.then_inc(u_up, 1)

            def residual(l, c, base, psum, done):
                for g, (lo, hi) in enumerate(STREAMS):
                    last = stt(h[:, c, lo:hi], psum[:, lo:hi], mod[:, base + c, g:g + 1], h[:, c, lo:hi],
                               ALU.mult, ALU.add)
                last.then_inc(done, 1)

            def norm(l, which):
                n = 2 * l + which
                g0, b0 = ((LN1G, LN1B), (LN2G, LN2B))[which]
                dve.wait_ge(ln_mm, 2 * n + 1)
                for c in range(KT):
                    tt(h[:, c, :], h[:, c, :], bank[4][:, 0:T], ALU.subtract).then_inc(xc_up, 1)
                dve.wait_ge(ln_rt, n + 1)
                link(dve.reciprocal(rstd, rstd))
                dve.wait_ge(ln_sq, KT * (n + 1))
                scaled_steps = []
                for c in range(KT):
                    scaled_steps.append(mark(stt(h[:, c, :], h[:, c, :], par[:, l, g0 + c:g0 + c + 1], rstd,
                                                 ALU.mult, ALU.mult)))
                    if c > 0 and n + 1 < 2 * DEPTH:
                        after(scaled_steps[c - 1])
                        normed(c - 1, which)
                after()
                if n + 1 < 2 * DEPTH:
                    normed(KT - 1, which)
                if n + 1 < 2 * DEPTH:
                    dve.wait_ge(u_up, KT * (n + 2))
                for c in range(KT):
                    ts(h[:, c, :], h[:, c, :], par[:, l, b0 + c:b0 + c + 1], None, ALU.add).then_inc(h_up, 1)
                dve.wait_ge(h_up, KT * (n + 1))

            def normed(c, which):
                base = 24 * (1 - which)
                for g, (lo, hi) in enumerate(STREAMS):
                    last = ts(u[:, c, lo:hi], h[:, c, lo:hi], mod[:, base + 8 + c, g:g + 1], shift[:, c, g:g + 1],
                              ALU.mult, ALU.add)
                last.then_inc(u_up, 1)

            def shifts(l, which):
                base, b0 = 24 * (1 - which), (LN1B, LN2B)[which]
                link(tt(shift[:, :, :], mod[:, base + 8:base + 16, :],
                        par[:, l, b0:b0 + KT].unsqueeze(2).broadcast_to([P, KT, 2]), ALU.mult))
                link(tt(shift[:, :, :], shift[:, :, :], mod[:, base:base + 8, :], ALU.add))

            def front(l):
                base = FRONT * l
                dve.wait_ge(front_cp, base + 4)
                tt(qk_s, qk, qk, ALU.mult).then_inc(qk_sq, 1)
                dve.memset(run[:, :, 0:1], 0.0)
                dve.wait_ge(front_cp, base + 14)
                link(dve.reciprocal(rs, rs))
                for m in range(4):
                    col = QN if m < 3 else KN
                    last = stt(qk[:, m, :], qk[:, m, :], par[:, l, col:col + 1], rs[:, m, :], ALU.mult, ALU.mult)
                last.then_inc(qk_up, 1)
                dve.wait_ge(qk_up, l + 1)
                mark(tt(rs[:, :, P:T], qk[:, :, P:T], rope_cos.unsqueeze(1).broadcast_to([P, 4, DEC]), ALU.mult))
                for m in range(2):
                    dve.wait_ge(rot_mm, 2 * l + m + 1)
                    tt(qk_s[:, 2 * m:2 * m + 2, P:T], bank[7][:, :].rearrange("p (m n) -> p m n", m=2),
                       rope_sin.unsqueeze(1).broadcast_to([P, 2, DEC]), ALU.mult).then_inc(rot_up, 1)
                dve.wait_ge(rot_up, 2 * (l + 1))
                tt(qk[:, :, P:T], rs[:, :, P:T], qk_s[:, :, P:T], ALU.add).then_inc(qkr_up, 1)
                dve.wait_ge(front_cp, base + 23)
                for j in range(NJ):
                    last = ts(kk_t[:, j, :], k_t[:, j, :], par[:, l, KKP + j:KKP + j + 1], None, ALU.mult)
                link(last)
                tt(kr, kk_t, kk_t, ALU.mult).then_inc(kk_sq, 1)

            def decays(l, d, j):
                dve.wait_ge(front_cp, FRONT * l + 35)
                lo = 9 * d + 3 * j
                for t in range(NT):
                    src = rate[:, d, j, tc(t)]
                    last = dve.tensor_tensor_scan(run[:, lo + t, 1:P + 1], src, src, 0.0, ALU.add, ALU.max)
                mark(last)
                mark(ts(kd_t[:, d, j, :], b_t[:, d, j, :], par[:, l, KAP + j:KAP + j + 1],
                        one_less_ka[:, j:j + 1], ALU.mult, ALU.add))
                after(steps[0] - 1)
                link(ts(centre[:, lo:lo + NT], run[:, lo:lo + NT, P], 0.5, None, ALU.mult))
                tt(run[:, lo:lo + NT, :], run[:, lo:lo + NT, :],
                   centre[:, lo:lo + NT].unsqueeze(2).broadcast_to([P, NT, P + 1]), ALU.subtract).then_inc(rates_up, 1)
                mark(tt(kd_t[:, d, j, :], kd_t[:, d, j, :], k_t[:, j, :], ALU.mult))

            def removal(l, j):
                dve.wait_ge(front_cp, FRONT * l + 38)
                mark(tt(kr[:, j, :], kd_t[:, 0, j, :], kd_t[:, 1, j, :], ALU.add))
                link(ts(y_t[:, j, :], y_t[:, j, :], 1e-12, None, ALU.max))
                link(dve.reciprocal(y_t[:, j, :], y_t[:, j, :]))
                link(tt(kk_t[:, j, :], kk_t[:, j, :], y_t[:, j, :], ALU.mult))
                for d in range(2):
                    mark(tt(b_t[:, d, j, :], b_t[:, d, j, :], kk_t[:, j, :], ALU.mult))
                stt(kr[:, j, :], r_t[:, j, :], par[:, l, RKP + j:RKP + j + 1], kr[:, j, :],
                    ALU.mult, ALU.mult).then_inc(bonus_in, 1)

            def attention(l):
                def maxima(i):
                    w = P if i < AH else T
                    dve.wait_ge(score_mm, 18 * l + i + 1)
                    link(dve.tensor_reduce(stat[:, 2, i:i + 1], score_bank(i)[:, 0:w], AX.X, ALU.max, negate=True))
                    ts(stat[:, 0, i:i + 1], stat[:, 2, i:i + 1], HD ** -0.5, None, ALU.mult).then_inc(max_up, 1)

                def normal(i):
                    w = P if i < AH else T
                    dve.wait_ge(prob_up, 18 * l + i + 1)
                    link(dve.reciprocal(stat[:, 2, i:i + 1], stat[:, 1, i:i + 1]))
                    ts(prob[:, i % 2, 0:w], prob[:, i % 2, 0:w], stat[:, 2, i:i + 1], None, ALU.mult).then_inc(pn_up, 1)

                for i in range(19):
                    if i < 18:
                        maxima(i)
                    if i >= 1:
                        normal(i - 1)
                    if AH <= i < 2 * AH:
                        decays(l, (i - AH) // NJ, (i - AH) % NJ)
                    if 2 * AH <= i < 2 * AH + NJ:
                        removal(l, i - 2 * AH)

            def scaled_first(l, s):
                n = l * 3 + s
                dve.wait_ge(exp_up, 6 * n + 4)
                for d in range(2):
                    t = tiles(s)[d]
                    mark(tt(scaled[:, 3, :, tc(d)], scaled[:, 2, :, tc(d)], kd_t[:, d, :, tc(t)], ALU.mult))
                    tt(scaled[:, 2, :, tc(d)], scaled[:, 2, :, tc(d)], b_t[:, d, :, tc(t)], ALU.mult)
                    last = stt(scaled[:, 1, :, tc(d)], kk_t[:, :, tc(t)], -1.0, scaled[:, 1, :, tc(d)], ALU.mult, ALU.mult)
                last.then_inc(scaled_up, 1)

            def rwkv_step(l, s):
                n = l * 3 + s
                if s == 0:
                    scaled_first(l, s)
                for j in range(NJ):
                    dve.wait_ge(x_init, 2 * NJ * n + X_ORDER.index((1, j)) + 1)
                    for e in range(2):
                        b = bank4(2 * j + e)
                        dve.wait_ge(inv_mm, 2 * (NJ * n + j) + e + 1)
                        dve.copy_predicated(quad(x_m[:, j])[:, :, e, :], lev[:, 0, 0:2, :], b[:, 0:2, :])
                        tt(quad(at_m[:, j])[:, :, e, :], b[:, 2:4, :], strict, ALU.mult)
                        last = dve.copy_predicated(quad(xt_m[:, j])[:, :, e, :], lev[:, 0, 1:3, :], b[:, 2:4, :])
                    last.then_inc(at_up, 1)
                dve.wait_ge(exp_up, 6 * (n + 1))
                for d in range(2):
                    part = scaled[:, 0, :, tc(d)]
                    last = tt(part, part, r_t[:, :, tc(tiles(s)[d])], ALU.mult)
                last.then_inc(scaled_up, 1)
                if s == 0:
                    link(dve.memset(s_t, 0.0))
                if s == 1:
                    dve.wait_ge(st_cp, 2 * (l + 1))
                dve.wait_ge(edge_up, l + 1)
                for d in range(2):
                    t = tiles(s)[d]
                    for j in range(NJ):
                        i = 9 * d + 3 * j + t
                        last = ts(s_hat[:, j, d, :], s_t[:, j, d, :], edge[:, i:i + 1], None, ALU.mult)
                last.then_inc(shat_up, 1)
                for k in range(1, LEVELS):
                    for j in range(NJ):
                        if k < LEVELS - 1:
                            dve.wait_ge(x_mm, xi(l, s, k, j, 0))
                            dve.copy_predicated(quad(x_m[:, j]), both(lev[:, k, 0:2, :]), quad(bank4(j))).then_inc(x_up, 1)
                        dve.wait_ge(x_mm, xi(l, s, k, j, 1))
                        dve.copy_predicated(quad(xt_m[:, j]), both(lev[:, k, 1:3, :]), quad(bank4(3 + j))).then_inc(x_up, 1)

                def masks(j):
                    for m, mask in enumerate((strict, incl, incl)):
                        for e in range(2):
                            dve.wait_ge(msc_mm, 6 * (NJ * n + j) + 2 * max(m, 1) + e + 1)
                            last = tt(quad(masks_of[j][:, m])[:, :, e, :], bank4(2 * (m // 2) + e)[:, 2 * (m % 2):2 * (m % 2) + 2, :],
                                      mask, ALU.mult)
                        last.then_inc(msc_up, 1)

                def outputs(j):
                    b = 4 + j % 2
                    dve.wait_ge(ys_mm, NJ * n + j + 1)
                    for d in range(2):
                        t = tiles(s)[d]
                        dst = y_t[:, j, tc(t)]
                        if s == 1 or (s == 0 and d == 0):
                            link(dve.tensor_copy(dst, bank[b][:, tc(d)]))
                        else:
                            link(tt(dst, dst, bank[b][:, tc(d)], ALU.add))
                    for d in range(2):
                        i = 9 * d + 3 * j + tiles(s)[d]
                        last = stt(s_new[:, d, :], bank[b][:, tc(2 + d)], edge[:, i:i + 1], head_ones, ALU.mult, ALU.mult)
                    last.then_inc(ys_up, 1)
                    dve.wait_ge(ys_up, NJ * n + j + 1)
                    for d in range(2):
                        i = 9 * d + 3 * j + tiles(s)[d]
                        last = stt(s_t[:, j, d, :], s_hat[:, j, d, :], edge[:, i:i + 1], s_new[:, d, :], ALU.mult, ALU.add)
                    last.then_inc(state_up, 1)

                for j in range(NJ):
                    masks(j)
                for j in range(NJ):
                    if j == NJ - 1 and s < 2:
                        scaled_first(l, s + 1)
                    outputs(j)
                dve.wait_ge(state_up, NJ * (n + 1))

            def heads_norm(l):
                for j in range(NJ):
                    dve.wait_ge(gn_mm, 2 * NJ * l + j + 1)
                    stt(y_t[:, j, :], bank[j][:, 0:T], -1.0 / HD, y_t[:, j, :], ALU.mult, ALU.add).then_inc(gn_c, 1)
                for j in range(NJ):
                    mark(ts(v_t[:, j, :], v_t[:, j, :], par[:, l, GNB + j:GNB + j + 1], None, ALU.add))
                for j in range(NJ):
                    dve.wait_ge(gn_rt, NJ * l + j + 1)
                    mark(dve.reciprocal(gn_r[:, j, :], gn_r[:, j, :]))
                dve.wait_ge(gn_c, NJ * (l + 1))
                for j in range(NJ):
                    after(steps[0] - (NJ - 1))
                    mark(tt(y_t[:, j, :], gn_r[:, j, :], y_t[:, j, :], ALU.mult))
                for j in range(NJ):
                    after(steps[0] - (NJ - 1))
                    mark(stt(y_t[:, j, :], y_t[:, j, :], par[:, l, GNG + j:GNG + j + 1], v_t[:, j, :],
                             ALU.mult, ALU.add))
                first_step = steps[0] - NJ
                for j in range(NJ):
                    after(first_step + j + 1)
                    dve.wait_ge(g_mm, NJ * l + j + 1)
                    tt(mixed[:, j, :], y_t[:, j, :], bank[3 + j][:, 0:T], ALU.mult).then_inc(mixa_up, 1)

            def route(l):
                gd, ge, gm, ls, oh1, oh2, gtmp = g4[:7]
                (p1e, e2, mx, s_g, m1, m2, mw, den, p1, p2, rank, rank1, more, at_over, code, is_over, base_t) = g1
                nb, upto, base, here, ids, plan_f = row4

                def wide(v):
                    return v.unsqueeze(2).broadcast_to([P, NT, 4])

                def every(v):
                    return v.unsqueeze(1).broadcast_to([P, NT, 4])

                def first_of(src, top):
                    link(tt(gtmp, src, wide(top), ALU.is_equal))
                    link(tt(gtmp, gtmp, first, ALU.mult))
                    link(dve.tensor_reduce(mw, gtmp, AX.X, ALU.max))
                    return gtmp, wide(mw)

                def pick(dst, per_group):
                    link(tt(gtmp, group_1h, per_group, ALU.mult))
                    link(dve.tensor_reduce(dst, gtmp, AX.X, ALU.add))

                dve.wait_ge(route_mm, l + 1)
                link(dve.tensor_copy(rl, bank[7][:, 0:20 * NT].rearrange("p (t n) -> p t n", t=NT)))
                lg = rl[:, :, 0:NG]
                link(dve.tensor_reduce(mx, lg, AX.X, ALU.max))
                tt(gd, lg, wide(mx), ALU.subtract).then_inc(d_up, 1)
                v, top = first_of(lg, mx)
                tt(group_1h, v, top, ALU.is_equal).then_inc(onehot_up, 1)
                dve.wait_ge(onehot_up, l + 1)
                experts = rl[:, :, NG:20].rearrange("p t (g j) -> p t g j", g=NG)
                link(tt(les_in, experts, group_1h.unsqueeze(3).broadcast_to([P, NT, NG, EPG]), ALU.mult))
                link(dve.tensor_reduce(ls, les_in.rearrange("p t g j -> p t j g"), AX.X, ALU.add))
                link(dve.tensor_reduce(m1, ls, AX.X, ALU.max))
                v, top = first_of(ls, m1)
                link(tt(oh1, v, top, ALU.is_equal))
                link(stt(gm, oh1, -1e30, ls, ALU.mult, ALU.add))
                link(dve.tensor_reduce(m2, gm, AX.X, ALU.max))
                tt(p1e, m2, m1, ALU.subtract).then_inc(d_up, 1)
                v, top = first_of(gm, m2)
                link(tt(oh2, v, top, ALU.is_equal))
                dve.wait_ge(rank_mm, l + 1)
                link(dve.tensor_copy(rank_s, bank[6][:, 0:16]))
                pick(rank, rank_s[:, 0:12].rearrange("p (t g) -> p t g", t=NT))
                link(ts(rank1, rank, 1.0, None, ALU.add))
                link(tt(codes, group_1h, wide(rank1), ALU.mult))
                link(ts(codes, codes, 1.0, None, ALU.subtract))
                choose(l, 0)
                choose(l, 1)
                dve.wait_ge(gexp_up, l + 1)
                link(dve.tensor_reduce(s_g, ge, AX.X, ALU.add))
                dve.wait_ge(e2_up, l + 1)
                link(ts(den, e2, 1.0, None, ALU.add))
                link(tt(den, den, s_g, ALU.mult))
                link(dve.reciprocal(p1, den))
                link(tt(p2, p1, e2, ALU.mult))
                mark(tt(oh1, oh1, wide(p1), ALU.mult))
                link(tt(oh2, oh2, wide(p2), ALU.mult))
                tt(inner, oh1, oh2, ALU.add).then_inc(inner_up, 1)
                size = rank_s[:, 12:16]
                link(ts(nb, size, P + 0.5, None, ALU.is_gt))
                link(stt(nb, size, 2 * P + 0.5, nb, ALU.is_gt, ALU.add))
                link(dve.tensor_tensor_scan(upto, nb, nb, 0.0, ALU.add, ALU.max))
                link(tt(base, upto, nb, ALU.subtract))
                pick(base_t, every(base))
                link(ts(more, rank, P - 0.5, None, ALU.is_gt))
                link(stt(more, rank, 2 * P - 0.5, more, ALU.is_gt, ALU.add))
                link(ts(is_over, more, 0.5, None, ALU.is_gt))
                link(tt(at_over, base_t, more, ALU.add))
                link(tt(at_over, at_over, is_over, ALU.mult))
                link(stt(code, more, -float(P), rank1, ALU.mult, ALU.add))
                link(ts(ids, first[:, 0, :], -float(EPG), float(EPG * NG), ALU.mult, ALU.add))
                link(dve.tensor_copy(plan_f[:, 0:1], upto[:, 3:4]))
                for over in range(2):
                    link(stt(over_codes[:, :, over], at_over, over + 1.0, code, ALU.is_equal, ALU.mult))
                    link(ts(here, base, over + 0.5, None, ALU.is_lt))
                    link(stt(here, upto, over + 0.5, here, ALU.is_gt, ALU.mult))
                    link(tt(here, here, ids, ALU.mult))
                    link(dve.tensor_reduce(plan_f[:, 1 + over:2 + over], here, AX.X, ALU.add))
                link(ts(over_codes, over_codes, 1.0, None, ALU.subtract))
                dve.tensor_copy(plan[0:1, 0:3], plan_f[0:1, 0:3]).then_inc(plan_up, 1)

            def choose(l, job):
                jn = JOBS * l + job
                if jn >= 2:
                    dve.wait_ge(misc_mm, jn - 1)
                for t in range(NT):
                    code = codes[:, t, job:job + 1] if job < NG else over_codes[:, t, job - NG:job - NG + 1]
                    last = ts(sel[:, job % 2, t, :], slots, code, None, ALU.is_equal)
                last.then_inc(sel_up, 1)

            def experts(l):
                def hidden(job, j):
                    jn = JOBS * l + job
                    n = EPG * jn + j
                    dve.wait_ge(silu_up, n + 1)
                    dve.wait_ge(misc_cp, jn + 1)
                    if n >= 2:
                        dve.wait_ge(ht_mm, n - 1)
                    stt(hs[:, j % 2, :], silu[:, j % 2, :], gates[:, job % 2, j:j + 1], bank[j % 2][:, DE:2 * DE],
                        ALU.mult, ALU.mult).then_inc(hid_up, 1)

                def add(job):
                    jn = JOBS * l + job
                    if jn > 0:
                        dve.wait_ge(z2_up, KT * jn)
                    for c in range(KT):
                        dve.wait_ge(un_mm, KT * jn + c + 1)
                        residual(l, c, 40, bank[2 + c % 2], z2_up)

                for job in range(NG):
                    for j in range(EPG):
                        hidden(job, j)
                        if j == 0 and job > 0:
                            add(job - 1)
                    if job + 2 < NG:
                        choose(l, job + 2)
                add(NG - 1)
                dve.wait_ge(plan_up, l + 1)
                count = dve.value_load(plan[0:1, 0:1], min_val=0, max_val=2)
                for over in range(2):
                    job = OVER + over
                    with dve.If(count > over):
                        choose(l, job)
                        for j in range(EPG):
                            hidden(job, j)
                        add(job)
                    with dve.Else():
                        skip(dve, JOBS * l + job, ((sel_up, 1), (hid_up, EPG), (z2_up, KT)))

            for l in range(DEPTH):
                if l == 0:
                    dve.wait_ge(modt_cp, MOD_FIRST)
                    dve.wait_ge(head_cp, 8)
                    finish_mod(0, 0, 16)
                    dve.wait_ge(cst_in, 16)
                    modulate(0)
                link(ts(one_less_ka[:, :], par[:, l, KAP:KAP + NJ], -1.0, 1.0, ALU.mult, ALU.add))
                front(l)
                attention(l)
                if l == 0:
                    dve.wait_ge(modt_cp, N_MOD)
                    finish_mod(0, 16, 48)
                for j in range(NJ):
                    dve.wait_ge(bonus_mm, NJ * l + j + 1)
                    dve.wait_ge(front_cp, FRONT * (l + 1))
                    tt(v_t[:, j, :], v_t[:, j, :], bank[j][:, 0:T], ALU.mult).then_inc(bonus_up, 1)
                dve.wait_ge(poolw_cp, 2 * (l + 1))
                dve.wait_ge(v_out, 16 * (l + 1))
                dve.wait_ge(k_out, 16 * (l + 1))
                for s in range(3):
                    rwkv_step(l, s)
                heads_norm(l)
                shifts(l, 0)
                for c in range(KT):
                    dve.wait_ge(proj_mm, KT * l + c + 1)
                    residual(l, c, 16, proj_bank(c), z_up)
                norm(l, 0)
                route(l)
                experts(l)
                if l + 1 < DEPTH:
                    dve.wait_ge(modt_cp, N_MOD * (l + 2))
                    dve.wait_ge(z2_up, KT * JOBS * (l + 1))
                    finish_mod(l + 1, 0, 48)
                    shifts(l, 1)
                norm(l, 1)


INPUTS = ("x_prompt", "x_sample", "state_rwkv", "cache_k", "cache_v", "c", "c_ctx", "w_in", "w_out", "w_mod", "b_mod",
          "ln1_g", "ln1_b", "ln2_g", "ln2_b", "rw_w0", "rw_w2", "rw_a0", "rw_a2", "rw_g2", "rw_kk", "rw_ka", "rw_rk",
          "rw_gn_g", "rw_gn_b", "q_norm", "k_norm", "pool_w", "pool_scale", "rt_grp_w", "rt_grp_b", "rt_exp_w",
          "rt_exp_b", "moe_w1", "moe_w3", "moe_w2")
OUTPUTS = ((1, SEQ, D), (1, DEC, D), (1, DEPTH, 2, AH, HD, HD), (1, DEPTH, SEQ, KVH, HD), (1, DEPTH, SEQ, KVH, HD))


def kernel(**inputs):
    import concourse.bacc as bacc
    from concourse.bass_utils import run_bass_kernel_spmd

    nc = bacc.Bacc("TRN2", target_bir_lowering=False, num_devices=1)
    arrays = {name: np.ascontiguousarray(inputs[name]) for name in INPUTS}
    arrays.update(constants())
    aps = {name: nc.dram_tensor(f"in_{name}", v.shape, mybir.dt.from_np(v.dtype), kind="ExternalInput").ap()
           for name, v in arrays.items()}
    outs = [nc.dram_tensor(f"out_{i}", shape, F32, kind="ExternalOutput").ap() for i, shape in enumerate(OUTPUTS)]
    build(nc, aps, outs)
    r = run_bass_kernel_spmd(nc, [{f"in_{name}": v for name, v in arrays.items()}], core_ids=[0])
    return tuple(r.results[0][f"out_{i}"] for i in range(len(OUTPUTS)))
```
